# Optimizing a Trainium2 kernel written in Bass

```python
import jax, jax.numpy as jnp
from jax import lax
import numpy as np

D_MODEL = 1024
BATCH = 1
SEQ = 512
DEPTH = 2

N_MIXERS = 2
NORM_EPS = 1e-6
MLA_HEADS = 8
MLA_Q_LORA = 384
MLA_KV_LORA = 256
MLA_NOPE = 128
MLA_ROPE = 64
MLA_V = 128
ROPE_THETA = 10000.0
ATTN_QBLOCK = 128
HG_HEADS = 8
HG_DK = D_MODEL // HG_HEADS
HG_DV = D_MODEL // HG_HEADS
HG_CHUNK = 64
PEER_HEADS = 8
PEER_NKEYS = 128
PEER_EXPERTS = PEER_NKEYS * PEER_NKEYS
PEER_QDIM = 256
PEER_HALF = PEER_QDIM // 2
PEER_TOPK = 16
PEER_TBLOCK = 128

kernel_name = 'hybrid_mla_hgrn2_peer'

def _rmsnorm(x, g):
    xf = x.astype(jnp.float32)
    y = xf * lax.rsqrt(jnp.mean(xf * xf, axis=-1, keepdims=True) + NORM_EPS)
    return (y * g.astype(jnp.float32)).astype(x.dtype)

def _rope_tables(positions):
    inv = ROPE_THETA ** (-jnp.arange(0, MLA_ROPE, 2, dtype=jnp.float32) / MLA_ROPE)
    ang = positions.astype(jnp.float32)[..., None] * inv
    return jnp.cos(ang), jnp.sin(ang)

def _rope(x, cos, sin):
    x1, x2 = jnp.split(x.astype(jnp.float32), 2, axis=-1)
    return jnp.concatenate([x1 * cos - x2 * sin, x2 * cos + x1 * sin], axis=-1).astype(x.dtype)

def _mla(h, cos, sin, w_in, q_norm, w_q_up, kv_norm, w_kv_up, w_out):
    B, S, _ = h.shape
    z = h @ w_in
    c_q = z[..., :MLA_Q_LORA]
    c_kv = z[..., MLA_Q_LORA:MLA_Q_LORA + MLA_KV_LORA]
    k_rope = _rope(z[..., MLA_Q_LORA + MLA_KV_LORA:], cos, sin)
    q = (_rmsnorm(c_q, q_norm) @ w_q_up).reshape(B, S, MLA_HEADS, MLA_NOPE + MLA_ROPE)
    q_nope = q[..., :MLA_NOPE]
    q_rope = _rope(q[..., MLA_NOPE:], cos[:, :, None], sin[:, :, None])
    kv = (_rmsnorm(c_kv, kv_norm) @ w_kv_up).reshape(B, S, MLA_HEADS, MLA_NOPE + MLA_V)
    k_nope = kv[..., :MLA_NOPE]
    v = kv[..., MLA_NOPE:]
    scale = (MLA_NOPE + MLA_ROPE) ** -0.5
    nb = S // ATTN_QBLOCK
    qn_b = (q_nope * scale).reshape(B, nb, ATTN_QBLOCK, MLA_HEADS, MLA_NOPE).swapaxes(0, 1)
    qr_b = (q_rope * scale).reshape(B, nb, ATTN_QBLOCK, MLA_HEADS, MLA_ROPE).swapaxes(0, 1)
    starts = jnp.arange(nb, dtype=jnp.int32) * ATTN_QBLOCK
    kpos = jnp.arange(S, dtype=jnp.int32)

    def block(args):
        qn, qr, start = args
        s = (jnp.einsum('bqhd,bkhd->bhqk', qn, k_nope)
             + jnp.einsum('bqhr,bkr->bhqk', qr, k_rope)).astype(jnp.float32)
        qpos = start + jnp.arange(ATTN_QBLOCK, dtype=jnp.int32)
        mask = kpos[None, :] <= qpos[:, None]
        s = jnp.where(mask, s, -jnp.inf)
        p = jax.nn.softmax(s, axis=-1).astype(v.dtype)
        return jnp.einsum('bhqk,bkhd->bqhd', p, v)

    o = lax.map(block, (qn_b, qr_b, starts))
    o = o.swapaxes(0, 1).reshape(B, S, MLA_HEADS * MLA_V)
    return o @ w_out

def _hgrn2(h, lb, w_in, out_norm, w_out):
    B, S, _ = h.shape
    F = HG_HEADS * HG_DK
    E = HG_HEADS * HG_DV
    z = h @ w_in
    q_pre = z[..., :F]
    f_pre = z[..., F:2 * F]
    i_in = z[..., 2 * F:2 * F + E]
    g_pre = z[..., 2 * F + E:]
    f = lb + (1.0 - lb) * jax.nn.sigmoid(f_pre.astype(jnp.float32))
    log_f = jnp.log(f)
    k = 1.0 - f
    q = jax.nn.silu(q_pre.astype(jnp.float32))
    v = i_in.astype(jnp.float32)
    nc = S // HG_CHUNK

    def chunks(t, d):
        return t.reshape(B, nc, HG_CHUNK, HG_HEADS, d).transpose(1, 0, 3, 2, 4)

    causal = jnp.tril(jnp.ones((HG_CHUNK, HG_CHUNK), dtype=bool))[:, :, None]

    def step(state, inp):
        qc, kc, vc, lfc = inp
        b = jnp.cumsum(lfc, axis=2)
        o_inter = jnp.einsum('bhtd,bhde->bhte', qc * jnp.exp(b), state)
        diff = b[:, :, :, None, :] - b[:, :, None, :, :]
        decay = jnp.where(causal, jnp.exp(jnp.where(causal, diff, 0.0)), 0.0)
        a = jnp.einsum('bhtd,bhsd,bhtsd->bhts', qc, kc, decay)
        o_intra = jnp.einsum('bhts,bhse->bhte', a, vc)
        b_last = b[:, :, -1:, :]
        state = (jnp.exp(b_last[:, :, 0, :])[..., None] * state
                 + jnp.einsum('bhsd,bhse->bhde', kc * jnp.exp(b_last - b), vc))
        return state, o_inter + o_intra

    state0 = jnp.zeros((B, HG_HEADS, HG_DK, HG_DV), jnp.float32)
    _, o = lax.scan(step, state0, (chunks(q, HG_DK), chunks(k, HG_DK), chunks(v, HG_DV), chunks(log_f, HG_DK)))
    o = o.transpose(1, 0, 3, 2, 4).reshape(B, S, HG_HEADS, HG_DV)
    o = o * lax.rsqrt(jnp.mean(o * o, axis=-1, keepdims=True) + NORM_EPS)
    o = o.reshape(B, S, E) * out_norm.astype(jnp.float32) * jax.nn.silu(g_pre.astype(jnp.float32))
    return o.astype(h.dtype) @ w_out

def _peer(h, w_q, sub_keys, u, v):
    B, S, D = h.shape
    xb = h.reshape(B * S // PEER_TBLOCK, PEER_TBLOCK, D)

    def block(xt):
        q = (xt @ w_q).reshape(PEER_TBLOCK, PEER_HEADS, 2, PEER_HALF)
        s = jnp.einsum('thpd,hpnd->thpn', q, sub_keys).astype(jnp.float32)
        s1, i1 = lax.top_k(s[:, :, 0], PEER_TOPK)
        s2, i2 = lax.top_k(s[:, :, 1], PEER_TOPK)
        cand = (s1[..., :, None] + s2[..., None, :]).reshape(PEER_TBLOCK, PEER_HEADS, PEER_TOPK * PEER_TOPK)
        cidx = (i1[..., :, None] * PEER_NKEYS + i2[..., None, :]).reshape(PEER_TBLOCK, PEER_HEADS, PEER_TOPK * PEER_TOPK)
        top, pos = lax.top_k(cand, PEER_TOPK)
        eidx = jnp.take_along_axis(cidx, pos, axis=-1)
        gates = jax.nn.softmax(top, axis=-1)
        act = jax.nn.gelu(jnp.einsum('td,thkd->thk', xt, u[eidx]).astype(jnp.float32), approximate=False)
        return jnp.einsum('thk,thkd->td', (gates * act).astype(xt.dtype), v[eidx])

    return lax.map(block, xb).reshape(B, S, D)

def setup_inputs(seed: int = 0) -> dict:
    key = jax.random.key(seed)
    ks = jax.random.split(key, 20)
    n_a = (DEPTH + N_MIXERS - 1) // N_MIXERS
    n_b = DEPTH // N_MIXERS
    F = HG_HEADS * HG_DK
    E = HG_HEADS * HG_DV

    def nrm(k, shape, scale):
        return jax.random.normal(k, shape, jnp.float32) * scale

    def gain(k, shape):
        return 1.0 + 0.02 * jax.random.normal(k, shape, jnp.float32)

    return {
        'x': nrm(ks[0], (BATCH, SEQ, D_MODEL), 1.0),
        'positions': jnp.broadcast_to(jnp.arange(SEQ, dtype=jnp.int32), (BATCH, SEQ)),
        'ln_mix': gain(ks[1], (DEPTH, D_MODEL)),
        'ln_ffn': gain(ks[2], (DEPTH, D_MODEL)),
        'ln_final': gain(ks[3], (D_MODEL,)),
        'mla_w_in': nrm(ks[4], (n_a, D_MODEL, MLA_Q_LORA + MLA_KV_LORA + MLA_ROPE), D_MODEL ** -0.5),
        'mla_q_norm': gain(ks[5], (n_a, MLA_Q_LORA)),
        'mla_w_q_up': nrm(ks[6], (n_a, MLA_Q_LORA, MLA_HEADS * (MLA_NOPE + MLA_ROPE)), MLA_Q_LORA ** -0.5),
        'mla_kv_norm': gain(ks[7], (n_a, MLA_KV_LORA)),
        'mla_w_kv_up': nrm(ks[8], (n_a, MLA_KV_LORA, MLA_HEADS * (MLA_NOPE + MLA_V)), MLA_KV_LORA ** -0.5),
        'mla_w_out': nrm(ks[9], (n_a, MLA_HEADS * MLA_V, D_MODEL), (MLA_HEADS * MLA_V) ** -0.5),
        'hg_w_in': nrm(ks[10], (n_b, D_MODEL, 2 * F + 2 * E), D_MODEL ** -0.5),
        'hg_lb': nrm(ks[11], (DEPTH, F), 0.5),
        'hg_out_norm': gain(ks[12], (n_b, E)),
        'hg_w_out': nrm(ks[13], (n_b, E, D_MODEL), E ** -0.5),
        'peer_w_q': nrm(ks[14], (DEPTH, D_MODEL, PEER_HEADS * PEER_QDIM), D_MODEL ** -0.5),
        'peer_sub_keys': nrm(ks[15], (DEPTH, PEER_HEADS, 2, PEER_NKEYS, PEER_HALF), PEER_HALF ** -0.5),
        'peer_u': nrm(ks[16], (DEPTH, PEER_EXPERTS, D_MODEL), D_MODEL ** -0.5),
        'peer_v': nrm(ks[17], (DEPTH, PEER_EXPERTS, D_MODEL), (PEER_HEADS * PEER_TOPK) ** -0.5),
    }

def reference(x, positions, ln_mix, ln_ffn, ln_final, mla_w_in, mla_q_norm, mla_w_q_up, mla_kv_norm,
              mla_w_kv_up, mla_w_out, hg_w_in, hg_lb, hg_out_norm, hg_w_out, peer_w_q, peer_sub_keys,
              peer_u, peer_v):
    cos, sin = _rope_tables(positions)
    p = jax.nn.softmax(hg_lb.astype(jnp.float32), axis=0)
    lb_all = jnp.cumsum(p, axis=0) - p[0:1]
    h = x
    for i in range(DEPTH):
        j = i // N_MIXERS
        hn = _rmsnorm(h, ln_mix[i])
        if i % N_MIXERS == 0:
            h = h + _mla(hn, cos, sin, mla_w_in[j], mla_q_norm[j], mla_w_q_up[j], mla_kv_norm[j],
                         mla_w_kv_up[j], mla_w_out[j])
        else:
            h = h + _hgrn2(hn, lb_all[i], hg_w_in[j], hg_out_norm[j], hg_w_out[j])
        h = h + _peer(_rmsnorm(h, ln_ffn[i]), peer_w_q[i], peer_sub_keys[i], peer_u[i], peer_v[i])
    return _rmsnorm(h, ln_final)


_drawn_inputs = setup_inputs


def setup_inputs(seed=0):
    import zlib

    import numpy as np

    out = dict(_drawn_inputs(seed))
    spreads = {}
    factors = {'ln_mix': 3.158,
     'ln_ffn': 41.147,
     'ln_final': 9.027,
     'mla_q_norm': 8.0,
     'mla_kv_norm': 8.0,
     'hg_out_norm': 18.052}
    for name, (base, spread) in spreads.items():
        noise = np.random.default_rng([zlib.crc32(name.encode()), seed]).standard_normal(out[name].shape)
        drawn = base * np.exp(spread * noise) if base else spread * noise
        out[name] = __import__('jax').numpy.asarray(drawn.astype(out[name].dtype))
    for name, factor in factors.items():
        out[name] = (out[name] * factor).astype(out[name].dtype)
    return out
```

```python
from contextlib import ExitStack

import numpy as np

import concourse.bass as bass
from concourse import mybir

ALU = mybir.AluOpType
ACT = mybir.ActivationFunctionType
AX = mybir.AxisListType
F32 = mybir.dt.float32
F32R = mybir.dt.float32r
BF16 = mybir.dt.bfloat16
I32 = mybir.dt.int32
U32 = mybir.dt.uint32

P = 128
SEQ, DM = 512, 1024
TT = SEQ // P
KC = DM // P
HEADS = 8
EPS = 1e-6
Q_LORA, KV_LORA, NOPE, ROPE = 384, 256, 128, 64
QC, VC = Q_LORA // P, KV_LORA // P
ATT_SCALE = float(NOPE + ROPE) ** -0.5
THETA = 10000.0
NKEYS, TOPK = 128, 16
HK = HEADS * TOPK
LEVELS = 7
LOWEST = -3.0e38
SMALLEST_F = 2.0 ** -63
INV_2PI = 1.0 / (2.0 * np.pi)
ROUNDER = 12582912.0
TWO_PI = [6.28125, 0.0019350051879882812]
TWO_PI.append(2.0 * np.pi - TWO_PI[0] - TWO_PI[1])
PI_BELOW = 3.1415925

RING = 4
UNROLL = 8
TURNS = NKEYS // UNROLL
ROUTED_TURN = TURNS // 2
TOK = SEQ // (TURNS - ROUTED_TURN)
HALF_TOK = TOK // 2
GF = 4
GG = NKEYS // GF
H_SLOTS = UNROLL

STREAM = [("z", 7), ("q_up", 6), ("k_up", 2), ("v_up", 2), ("mla_out", 8),
          ("pq0", 16), ("u0", NKEYS), ("v0", NKEYS),
          ("hg_q", 8), ("hg_f", 8), ("hg_g", 8), ("hg_i", 8), ("hg_out", 8),
          ("pq1", 16), ("u1", NKEYS), ("v1", NKEYS)]
BASE, N_TILES = {}, 0
for _name, _n in STREAM:
    BASE[_name] = N_TILES
    N_TILES += _n

C_ID, C_ONE, C_IOTA, C_CAUSAL, C_INV, C_SGN, C_COLS = 0, 128, 256, 384, 512, 513, 514
G_NAMES = [("mix0", KC), ("ffn0", KC), ("mix1", KC), ("ffn1", KC), ("q", QC), ("kv", VC), ("out", KC),
           ("lb0", KC), ("lb1", KC)]
G_AT, G_COLS = {}, 0
for _name, _n in G_NAMES:
    G_AT[_name] = G_COLS
    G_COLS += _n

ARENA = 26112


class Banks:

    def __init__(self):
        self.bank, self.before, self.ready, self.frees = {}, {}, {}, {}
        self.signals = 0
        self.count = {"act": 0, "dve": 0, "exp": 0, "state": 0}
        self.turn, self.last = {}, {}

    def add(self, key, frees, tile=None, banks=tuple(range(8))):
        n = self.turn.get(banks, 0)
        self.turn[banks] = n + 1
        bank = self.bank[key] = banks[n % len(banks)]
        self.before[key] = self.last.get(bank)
        self.last[bank] = key
        if tile is None:
            self.signals += 1
            self.ready[key] = ("ps_ready", self.signals)
        else:
            self.ready[key] = ("tile_used", tile + 1)
        self.count[frees] += 1
        self.frees[key] = (frees, self.count[frees])


def plan():
    b = Banks()

    def norm(k):
        for c in range(KC):
            b.add(("xT", k, c), "dve")

    def eight(name, last_tile, frees):
        for n in range(8):
            b.add((name, n), frees, last_tile if n == 7 else None)

    norm(0)
    for m in range(7):
        b.add(("z", m), "dve" if m >= 5 else "act", BASE["z"] + m)
    b.add(("zss", 0), "dve")
    b.add(("zss", 1), "dve")
    for m in range(16):
        end = 3 * m + 2
        b.add(("q_up", m), "act" if m < 8 else "dve", BASE["q_up"] + end // 8 if end % 8 == 7 else None)
    for m in range(8):
        end = 2 * m + 1
        b.add(("k_up", m), "act", BASE["k_up"] + end // 8 if end % 8 == 7 else None)
    eight("v_up", BASE["v_up"] + VC - 1, "act")
    for n in range(4 * HEADS + 2):
        if n < 4 * HEADS:
            b.add(("s", n), "exp", None, (0, 1, 2))
        if n >= 2:
            b.add(("pT", n - 2), "act", None, (3, 4, 5))
            if n % 4 == 1:
                b.add(("o", (n - 2) // 4), "dve", None, (6, 7))
    eight("mla_out", BASE["mla_out"] + 7, "dve")

    def peer(layer):
        norm(2 * layer + 1)
        for n in range(17):
            if n < 16:
                b.add((f"pq{layer}", n), "act", BASE[f"pq{layer}"] + n)
            if n >= 1:
                b.add((f"sc{layer}", n - 1), "dve")
        eight(f"v{layer}", BASE[f"v{layer}"] + NKEYS - 1, "dve")

    peer(0)
    norm(2)
    for n in range(8):
        b.add(("hg_q", n), "act", BASE["hg_q"] + n)
    for n in range(8):
        b.add(("hg_f", n), "act", BASE["hg_f"] + n)
    for n in range(8):
        b.add(("hg_g", n), "act", BASE["hg_g"] + n)
    eight("hg_i", BASE["hg_i"] + 7, "act")
    for h in range(HEADS):
        b.add(("kd", h), "act", None, (4,))
        for lv in range(LEVELS + 1):
            if lv == 1:
                b.add(("st", h), "state", None, (5,))
            b.add(("a", h, lv), "dve", None, (0, 1, 2, 3))
        b.add(("ho", h), "act", None, (6, 7))
    for h in range(HEADS):
        b.add(("hss", h), "dve")
    eight("hg_out", BASE["hg_out"] + 7, "dve")
    peer(1)
    return b


def model(nc, x, pos, consts, masks, gains, fgain, mla_t, hg_t, pq_t, keys_t, u_t, v_t, out):
    jobs = plan()
    ctx = ExitStack()
    with ctx:
        def sb(name, shape, dt=F32):
            return ctx.enter_context(nc.sbuf_tensor(name, shape, dt))

        sems = {}

        def sem(name):
            if name not in sems:
                sems[name] = ctx.enter_context(nc.semaphore(name))
            return sems[name]

        acts_dram = nc.dram_tensor("acts_dram", [NKEYS, P, SEQ], F32, kind="Internal").ap()
        gates_dram = nc.dram_tensor("gates_dram", [GG, P, SEQ, GF], F32, kind="Internal").ap()

        PS = ctx.enter_context(nc.psum_tensor("PS", [P, 8, 512], F32))
        w_raw = sb("w_raw", [P, RING, 1024])
        w_hi = sb("w_hi", [P, RING, 1024], F32R)
        w_lo = sb("w_lo", [P, RING, 1024], F32R)
        x_hi = sb("x_hi", [P, KC, SEQ], F32R)
        x_lo = sb("x_lo", [P, KC, SEQ], F32R)
        resid = sb("resid", [P, TT, DM])
        const = sb("const", [P, C_COLS])
        mask_bits = sb("mask_bits", [P, SEQ + 8 * P], mybir.dt.uint16)
        mask = mask_bits[:, :].bitcast(BF16)
        gain = sb("gain", [P, G_COLS])
        stat = sb("stat", [P, 16])
        arena = sb("arena", [P, ARENA])

        ident = const[:, C_ID:C_ID + P]
        ones = const[:, C_ONE:C_ONE + P]
        iota = const[:, C_IOTA:C_IOTA + P]
        causal = const[:, C_CAUSAL:C_CAUSAL + P]
        keep = mask[:, 0:SEQ]
        level_mask = [mask[:, SEQ + P * n:SEQ + P * (n + 1)] for n in range(8)]

        def f32(ap):
            return ap.bitcast(F32)

        def cut(offset, *shape):
            n = int(np.prod(shape))
            ap = arena[:, offset:offset + n]
            if len(shape) == 1:
                return ap
            names = "abcd"[:len(shape)]
            return ap.rearrange(f"p ({' '.join(names)}) -> p {' '.join(names)}", **dict(zip(names, shape)))

        zT = cut(0, 7, SEQ)
        cosT, sinT = cut(3584, SEQ), cut(4096, SEQ)
        tmp = cut(4608, 4, SEQ)
        qn, kn = cut(6656, HEADS, SEQ), cut(10752, HEADS, SEQ)
        qr, kr = cut(14848, 4, SEQ), cut(16896, SEQ)
        vtok = cut(17408, TT, DM)
        pT = cut(21504, 2, TT, SEQ)
        prob = cut(0, 2, SEQ)
        posi = cut(21504, SEQ).bitcast(I32)
        scaled = cut(21504, TT, DM)
        act_st = cut(0, H_SLOTS, SEQ)
        gate_st = cut(4096, 2, GG, HALF_TOK, GF)
        gate_ld = cut(4096, 2, SEQ, GF)
        scores = cut(4096, TT, 16, NKEYS)
        val = cut(12288, 16, TOPK)
        ixu = cut(12544, 16, TOPK).bitcast(U32)
        ixf = cut(12800, 16, TOPK)
        top = cut(13056, TT, HEADS, TOPK)
        posu = cut(13568, HK).bitcast(U32)
        halfu = cut(13696, 2, HK).bitcast(U32)
        halff = cut(13952, 2, HK)
        ids = cut(14208, 2, TT, HK)
        gsum = cut(15232, 32)
        cand = cut(15360, HEADS, TOPK, TOPK)
        picked = cut(17408, HK, TOPK)
        onehot1, onehot2 = cut(15360, 8, NKEYS), cut(16384, 8, NKEYS)
        routeT = cut(19456, 3, SEQ)
        window = cut(20992, 3, TOK)
        qT = cut(17408, 2, SEQ)
        keysT = cut(0, 16, NKEYS)
        product = cut(21504, RING, SEQ)
        gq, gk, gb, gg_, gv = (cut(4096 * n, HEADS, SEQ) for n in range(5))
        vrec = gv.rearrange("p a b -> p (a b)").rearrange("p (t d) -> p t d", t=TT)
        R0 = 20480
        e_all, dd, ee, xx = cut(R0, SEQ), cut(R0 + 512, SEQ), cut(R0 + 1024, SEQ), cut(R0 + 1536, 2, SEQ)
        qe, kdec, kdT = cut(R0 + 2560, SEQ), cut(R0 + 3072, SEQ), cut(R0 + 3584, TT, P)
        a_sb = cut(R0 + 4096, 2, SEQ)
        state = cut(R0 + 5120, 3, P)
        lbt = cut(R0 + 5504, 4, KC)
        rstd_h = cut(16384, HEADS, SEQ)
        final_gain = cut(0, DM)
        final = cut(1024, TT, DM)

        ps_ready, tile_used = sem("ps_ready"), sem("tile_used")
        freed = {who: sem(f"{who}_freed") for who in ("act", "dve", "exp", "state")}
        hi_ready, lo_ready = sem("hi_ready"), sem("lo_ready")
        landed = [sem(f"landed{n}") for n in range(RING)]
        act_stored = [sem(f"act_stored{n}") for n in range(H_SLOTS)]
        act_loaded = [sem(f"act_loaded{n}") for n in range(H_SLOTS)]
        gate_stored = [sem(f"gate_stored{n}") for n in range(2)]
        gate_loaded = [sem(f"gate_loaded{n}") for n in range(2)]
        gelu_done = sem("gelu_done")
        gate_moved = sem("gate_moved")
        gates_made = sem("gates_made")
        onehots = sem("onehots")

        def PSb(key):
            return PS[:, jobs.bank[key], :]

        def ready(eng, key):
            name, count = jobs.ready[key]
            eng.wait_ge(sem(name), count)

        def free(ins, key):
            return ins.then_inc(freed[jobs.frees[key][0]], 1)

        def was_freed(eng, key):
            frees, count = jobs.frees[key]
            eng.wait_ge(freed[frees], count)

        blocks = {
            "z": mla_t, "pq0": pq_t[0], "u0": u_t[0], "v0": v_t[0], "hg_q": hg_t, "pq1": pq_t[1],
            "u1": u_t[1], "v1": v_t[1],
        }

        block = ctx.enter_context(nc.Block())

        @block.sync
        def _(sp):
            def load_tile(n, src, slot):
                if not isinstance(n, int) or n >= RING:
                    sp.wait_ge(lo_ready, n - (RING - 1))
                sp.dma_start(w_raw[:, slot, :], src).then_inc(landed[slot], 16)

            def load_range(name, count, first=0):
                tiles = blocks[name]
                for k in range(first, first + count):
                    load_tile(BASE[name] + k, tiles[k], (BASE[name] + k) % RING)

            sp.dma_start(resid[:, :, :], x.rearrange("(t p) d -> p t d", p=P)).then_inc(sem("x_in"), 16)
            sp.dma_start(const[:, :], consts).then_inc(sem("const_in"), 16)
            sp.dma_start(gain[:, :], gains).then_inc(sem("gain_in"), 16)
            sp.dma_start(mask_bits[:, :], masks).then_inc(sem("mask_in"), 16)
            sp.dma_start(posi, pos.partition_broadcast(P)).then_inc(sem("pos_in"), 16)
            load_range("z", 25)

            def experts(layer):
                u, v = blocks[f"u{layer}"], blocks[f"v{layer}"]
                bu, bv = BASE[f"u{layer}"], BASE[f"v{layer}"]

                was_freed(sp, ("mla_out", 7) if layer == 0 else ("hg_out", 7))
                sp.dma_start(keysT, keys_t[layer]).then_inc(sem("keys_in"), 16)
                load_range(f"pq{layer}", 16)

                def store_act(c, j):
                    sp.wait_ge(gelu_done, c + (NKEYS * layer + 4 + 1))
                    sp.dma_start(acts_dram[bass.ds(c, 1)].rearrange("a p n -> (a p) n"),
                                 act_st[:, j, :]).then_inc(act_stored[j], 16)

                def store_gates(turn, b):
                    groups = HALF_TOK // 4
                    sp.wait_ge(gate_moved, turn * (2 * groups) + (b + 1) * groups + SEQ // 4 * layer + 2)
                    sp.dma_start(
                        gates_dram[:, :, bass.ds(turn * TOK + b * HALF_TOK, HALF_TOK), :]
                        .rearrange("g p t f -> p g (t f)"),
                        gate_st[:, b].rearrange("p g t f -> p g (t f)")).then_inc(gate_stored[b], 16)

                def u_turn(i, acts, gate1, gate0):
                    for j in range(UNROLL):
                        load_tile(i * UNROLL + (bu + j), u[bass.ds(i * UNROLL + j, 1)]
                                  .rearrange("a p n -> (a p) n"), (bu + j) % RING)
                        if acts:
                            store_act(i * UNROLL + (j - UNROLL), j)
                        if j == 1 and gate1:
                            store_gates(i - (ROUTED_TURN + 2), 1)
                        if j == 5 and gate0:
                            store_gates(i - (ROUTED_TURN + 1), 0)

                u_turn(0, False, False, False)
                with sp.Fori(1, ROUTED_TURN + 1) as i:
                    u_turn(i, True, False, False)
                u_turn(ROUTED_TURN + 1, True, False, True)
                with sp.Fori(ROUTED_TURN + 2, TURNS) as i:
                    u_turn(i, True, True, True)

                def load_v(c, j):
                    load_tile(c + bv, v[bass.ds(c, 1)].rearrange("a p n -> (a p) n"), (bv + j) % RING)

                for j in range(RING):
                    load_v(j, j)
                last = TURNS - ROUTED_TURN - 1
                for j in range(UNROLL):
                    if j == 1:
                        store_gates(last - 1, 1)
                    if j == 5:
                        store_gates(last, 0)
                    store_act(NKEYS - UNROLL + j, j)
                store_gates(last, 1)
                for j in range(H_SLOTS):
                    sp.wait_ge(act_stored[j], 16 * TURNS * (layer + 1))
                for b in range(2):
                    sp.wait_ge(gate_stored[b], 16 * (TURNS - ROUTED_TURN) * (layer + 1))

                def v_turn(i, first):
                    for j in range(UNROLL):
                        if not (first and j < RING):
                            load_v(i * UNROLL + j, j)
                        if j % GF == 0:
                            b = j // GF
                            if not first:
                                sp.wait_ge(sem("product_made"), i * UNROLL + (j - GF + NKEYS * layer))
                            sp.dma_start(gate_ld[:, b].rearrange("p t f -> p (t f)"),
                                         gates_dram[bass.ds(i * 2 + b, 1)]
                                         .rearrange("a p t f -> (a p) (t f)")).then_inc(gate_loaded[b], 16)
                        if not first:
                            sp.wait_ge(sem("product_made"), i * UNROLL + (j - UNROLL + 1 + NKEYS * layer))
                        sp.dma_start(act_st[:, j, :], acts_dram[bass.ds(i * UNROLL + j, 1)]
                                     .rearrange("a p n -> (a p) n")).then_inc(act_loaded[j], 16)

                v_turn(0, True)
                with sp.Fori(1, TURNS) as i:
                    v_turn(i, False)

            experts(0)
            load_range("hg_q", 40)
            experts(1)
            sp.wait_ge(sem("final_free"), 1)
            sp.dma_start(final_gain, fgain.partition_broadcast(P)).then_inc(sem("fgain_in"), 16)
            for t in range(TT):
                sp.wait_ge(sem("final_made"), t + 1)
                sp.dma_start(out[t * P:(t + 1) * P, :], final[:, t, :]).then_inc(sem("out_done"), 16)
            sp.wait_ge(sem("out_done"), 16 * TT)

        @block.gpsimd
        def _(pool):
            def low(n, slot):
                pool.wait_ge(hi_ready, n + 1)
                pool.tensor_tensor(w_lo[:, slot, :], w_raw[:, slot, :], f32(w_hi[:, slot, :]),
                                   ALU.subtract).then_inc(lo_ready, 1)

            with pool.Fori(0, N_TILES // RING) as i:
                for j in range(RING):
                    low(i * RING + j, j)
            for n in range(N_TILES // RING * RING, N_TILES):
                low(n, n % RING)

        @block.scalar
        def _(act):
            step = [0]

            def chain(ins):
                step[0] += 1
                ins.then_inc(sem("act_step"), 1)
                act.wait_ge(sem("act_step"), step[0])

            def high(n, slot, lap):
                act.wait_ge(landed[slot], lap * 16 + 16)
                if not isinstance(n, int) or n >= RING:
                    act.wait_ge(tile_used, n - (RING - 1))
                act.activation(w_hi[:, slot, :], w_raw[:, slot, :], ACT.Copy).then_inc(hi_ready, 1)

            def next_high(n):
                if n + RING < N_TILES:
                    high(n + RING, n % RING, (n + RING) // RING)

            def rstd_of_resid(k):
                if k == 0:
                    act.wait_ge(sem("x_in"), 16)
                else:
                    act.wait_ge(sem("resid_done"), k)
                for t in range(TT):
                    act.activation(scaled[:, t, :], resid[:, t, :], ACT.Square,
                                   accum_out=stat[:, t:t + 1]).then_inc(sem("squares"), 1)
                act.wait_ge(sem("mean"), k + 1)
                act.activation(stat[:, 8:12], stat[:, 4:8], ACT.Sqrt).then_inc(sem("root"), 1)

            def norm(k):
                rstd_of_resid(k)
                for c in range(KC):
                    g = G_AT[["mix0", "ffn0", "mix1", "ffn1"][k]] + c
                    ready(act, ("xT", k, c))
                    act.activation(x_hi[:, c, :], PSb(("xT", k, c)), ACT.Copy,
                                   scale=gain[:, g:g + 1]).then_inc(sem("x_high"), 1)

            for n in range(RING):
                high(n, n, 0)
            act.wait_ge(sem("gain_in"), 16)
            for n in range(2):
                act.wait_ge(sem("angle"), n + 1)
                act.activation([sinT, cosT][n], tmp[:, n, :], ACT.Sin).then_inc(sem("sines"), 1)
            act.wait_ge(sem("pos_read"), 1)
            norm(0)
            for m in range(7):
                if m < 5:
                    ready(act, ("z", m))
                    free(act.activation(zT[:, m, :], PSb(("z", m)), ACT.Copy), ("z", m))
                next_high(BASE["z"] + m)
            for n in range(2):
                act.wait_ge(sem("latent_mean"), n + 1)
                act.activation(tmp[:, n, :], tmp[:, n, :], ACT.Sqrt).then_inc(sem("latent_root"), 1)
            for m in range(5):
                act.wait_ge(sem("latent"), m + 1)
                act.activation(x_hi[:, m, :], zT[:, m, :], ACT.Copy).then_inc(sem("latent_high"), 1)
            for m in range(16):
                if m < 8:
                    ready(act, ("q_up", m))
                    free(act.activation(qn[:, m, :], PSb(("q_up", m)), ACT.Copy), ("q_up", m))
                for b in range(3 * m, 3 * m + 3):
                    if b % 8 == 7:
                        next_high(BASE["q_up"] + b // 8)
            for m in range(8):
                ready(act, ("k_up", m))
                free(act.activation(kn[:, m, :], PSb(("k_up", m)), ACT.Copy), ("k_up", m))
                if m % 4 == 3:
                    next_high(BASE["k_up"] + m // 4)
            next_high(BASE["v_up"])
            next_high(BASE["v_up"] + 1)
            for n in range(8):
                ready(act, ("v_up", n))
                free(act.activation(vtok[:, n // 2, (n % 2) * 512:(n % 2) * 512 + 512],
                                    PSb(("v_up", n)), ACT.Copy), ("v_up", n))

            def exponent(n):
                w = (n % 4 + 1) * P
                act.wait_ge(sem("bias"), n + 1)
                free(act.activation(prob[:, n % 2, 0:w], PSb(("s", n))[:, 0:w], ACT.Exp,
                                    bias=stat[:, 12 + n % 2:13 + n % 2], scale=ATT_SCALE,
                                    accum_out=stat[:, 14 + n % 2:15 + n % 2]), ("s", n))

            for n in range(2):
                exponent(n)
            for n in range(4 * HEADS):
                h, qt = n // 4, n % 4
                ready(act, ("pT", n))
                if qt == 0 and h >= 2:
                    ready(act, ("o", h - 2))
                free(act.activation(pT[:, h % 2, 0:qt + 1, qt * P:(qt + 1) * P],
                                    PSb(("pT", n))[:, 0:(qt + 1) * P].rearrange("p (j q) -> p j q", q=P),
                                    ACT.Copy), ("pT", n))
                if n + 2 < 4 * HEADS:
                    exponent(n + 2)
                if n >= 6 and (n - 6) % 4 == 0 or n == 4 * HEADS - 1:
                    for hh in ([(n - 6) // 4] if n < 4 * HEADS - 1 else [HEADS - 1]):
                        ready(act, ("o", hh))
                        act.activation(x_hi[:, hh, :], PSb(("o", hh)), ACT.Copy).then_inc(sem("o_high"), 1)
            for n in range(8):
                next_high(BASE["mla_out"] + n)

            def experts(layer):
                bu, bv, bq = BASE[f"u{layer}"], BASE[f"v{layer}"], BASE[f"pq{layer}"]
                if layer == 0:
                    act.sem_inc(gelu_done, 4)
                    act.sem_inc(gate_moved, 2)
                norm(2 * layer + 1)
                for n in range(16):
                    ready(act, (f"pq{layer}", n))
                    if n >= 2:
                        ready(act, (f"sc{layer}", n - 2))
                    free(act.activation(qT[:, n % 2, :], PSb((f"pq{layer}", n)), ACT.Copy),
                         (f"pq{layer}", n))
                    next_high(bq + n)

                def gelu(i, j):
                    c = i * UNROLL + j
                    act.wait_ge(tile_used, c + (bu + 1))
                    if layer > 0 or not isinstance(i, int) or i > 0:
                        act.wait_ge(act_stored[j], (i + TURNS * layer) * 16)
                    act.activation(act_st[:, j, :], PS[:, j % 4, :], ACT.Gelu).then_inc(gelu_done, 1)
                    high(c + (bu + RING), (bu + j) % RING,
                         i * (UNROLL // RING) + (bu + j + RING) // RING)

                def move_gates(turn, q):
                    b, k = q // (HALF_TOK // 4), q % (HALF_TOK // 4)
                    act.wait_ge(gates_made, turn * (TOK // 4) + (q + 1 + SEQ // 4 * layer + 2))
                    if k == 0 and (layer > 0 or not isinstance(turn, int)):
                        act.wait_ge(gate_stored[b], (turn + (TURNS - ROUTED_TURN) * layer) * 16)
                    act.activation(
                        gate_st[:, b].rearrange("p g t f -> p t g f")[:, 4 * k:4 * k + 4],
                        PS[:, 4 + q % 2, :].rearrange("p (t g f) -> p t g f", t=4, f=GF),
                        ACT.Copy).then_inc(gate_moved, 1)

                for j in range(UNROLL):
                    gelu(0, j)
                with act.Fori(1, ROUTED_TURN) as i:
                    for j in range(UNROLL):
                        gelu(i, j)
                act.wait_ge(sem("top_less_max"), TT * (layer + 1))
                act.activation(top, top, ACT.Exp).then_inc(sem("top_exp"), 1)

                def routed_turn(i):
                    for j in range(UNROLL):
                        gelu(i, j)
                        for q in range(j * TOK // 4 // UNROLL, (j + 1) * TOK // 4 // UNROLL):
                            move_gates(i - ROUTED_TURN, q)

                routed_turn(ROUTED_TURN)
                with act.Fori(ROUTED_TURN + 1, TURNS) as i:
                    routed_turn(i)

                def product_high(c, j):
                    act.wait_ge(sem("product_made"), c + (NKEYS * layer + 1))
                    act.wait_ge(tile_used, c + (bv - RING + 1))
                    act.activation(x_hi[:, j % RING, :], product[:, j % RING, :],
                                   ACT.Copy).then_inc(sem("product_high"), 1)

                act.wait_ge(tile_used, bv)
                for c in range(RING):
                    product_high(c, c)

                def v_turn(i, n):
                    for j in range(n):
                        high(i * UNROLL + (bv + j + RING), (bv + j) % RING,
                             i * (UNROLL // RING) + (bv + j + RING) // RING)
                        product_high(i * UNROLL + (j + RING), j)

                with act.Fori(0, TURNS - 1) as i:
                    v_turn(i, UNROLL)
                v_turn(TURNS - 1, RING)
                for c in range(NKEYS - RING, NKEYS):
                    next_high(bv + c)

            experts(0)

            norm(2)
            for n in range(8):
                ready(act, ("hg_q", n))
                free(act.activation(gq[:, n, :], PSb(("hg_q", n)), ACT.Silu), ("hg_q", n))
                next_high(BASE["hg_q"] + n)
            for n in range(8):
                ready(act, ("hg_f", n))
                ins = free(act.activation(gb[:, n, :], PSb(("hg_f", n)), ACT.Sigmoid), ("hg_f", n))
                next_high(BASE["hg_f"] + n)
            for n in range(8):
                ready(act, ("hg_g", n))
                free(act.activation(gg_[:, n, :], PSb(("hg_g", n)), ACT.Silu), ("hg_g", n))
                next_high(BASE["hg_g"] + n)
            act.wait_ge(sem("bound_less_max"), 1)
            act.activation(lbt[:, 0:2, :], lbt[:, 0:2, :], ACT.Exp).then_inc(sem("bound_exp"), 1)
            for h in range(HEADS):
                act.wait_ge(sem("forget"), h + 1)
                if h >= 2:
                    act.wait_ge(sem("cumulated"), h - 1)
                act.activation(dd if h % 2 == 0 else ee, gb[:, h, :], ACT.Ln).then_inc(sem("forget_log"), 1)
            for n in range(8):
                next_high(BASE["hg_i"] + n)
            for n in range(8):
                ready(act, ("hg_i", n))
                free(act.activation(vrec[:, n // 2, (n % 2) * 512:(n % 2) * 512 + 512],
                                    PSb(("hg_i", n)), ACT.Copy), ("hg_i", n))
            for h in range(HEADS):
                act.wait_ge(sem("cumulated"), h + 1)
                if h >= 1:
                    act.wait_ge(sem("state_done"), h)
                act.activation(e_all, gb[:, h, :], ACT.Exp).then_inc(sem("decay"), 1)
                act.wait_ge(sem("to_end"), h + 1)
                act.activation(ee, dd, ACT.Exp).then_inc(sem("level_exp"), 1)
                for lv in range(LEVELS):
                    m = P >> (lv + 1)
                    act.wait_ge(sem("level_diff"), LEVELS * h + lv + 1)
                    d4 = dd.rearrange("p (b s m) -> p b s m", s=2, m=m)
                    e4 = ee.rearrange("p (b s m) -> p b s m", s=2, m=m)
                    act.activation(e4[:, :, 0], d4[:, :, 0], ACT.Exp, scale=-1.0)\
                       .then_inc(sem("level_exp"), 1)
                    act.activation(e4[:, :, 1], d4[:, :, 1], ACT.Exp).then_inc(sem("level_exp"), 1)
                    if lv == 0:
                        ready(act, ("kd", h))
                        free(act.activation(kdT.rearrange("p a b -> p (a b)"), PSb(("kd", h)), ACT.Copy),
                             ("kd", h))
                ready(act, ("ho", h))
                free(act.activation(gq[:, h, :], PSb(("ho", h)), ACT.Copy), ("ho", h))
            for h in range(HEADS):
                act.wait_ge(sem("head_mean"), h + 1)
                act.activation(rstd_h[:, h, :], rstd_h[:, h, :], ACT.Sqrt).then_inc(sem("head_root"), 1)
            for h in range(HEADS):
                act.wait_ge(sem("gated"), h + 1)
                act.activation(x_hi[:, h, :], gq[:, h, :], ACT.Copy).then_inc(sem("gated_high"), 1)
            for n in range(8):
                next_high(BASE["hg_out"] + n)

            experts(1)
            rstd_of_resid(4)

        @block.vector
        def _(dve):
            step = [0]

            def chain(ins):
                step[0] += 1
                ins.then_inc(sem("dve_step"), 1)
                dve.wait_ge(sem("dve_step"), step[0])

            def wide(ap, shape, at):
                return ap.unsqueeze(at).broadcast_to(shape)

            def scale_resid(k):
                dve.wait_ge(sem("squares"), TT * (k + 1))
                if k == 0:
                    dve.wait_ge(sem("x_in"), 16)
                dve.tensor_scalar(stat[:, 4:8], stat[:, 0:4], 1.0 / DM, EPS, ALU.mult, ALU.add)\
                   .then_inc(sem("mean"), 1)
                dve.wait_ge(sem("root"), k + 1)
                chain(dve.reciprocal(stat[:, 0:4], stat[:, 8:12]))

            def norm(k):
                scale_resid(k)
                for t in range(TT):
                    ins = dve.tensor_scalar(scaled[:, t, :], resid[:, t, :], stat[:, t:t + 1], None, ALU.mult)
                    ins.then_inc(sem("scaled"), 1)
                for c in range(KC):
                    g = G_AT[["mix0", "ffn0", "mix1", "ffn1"][k]] + c
                    dve.wait_ge(sem("x_high"), KC * k + c + 1)
                    free(dve.scalar_tensor_tensor(x_lo[:, c, :], PSb(("xT", k, c)), gain[:, g:g + 1],
                                                  f32(x_hi[:, c, :]), ALU.mult, ALU.subtract),
                         ("xT", k, c))

            def add_to_resid(name, k):
                for n in range(8):
                    part = resid[:, n // 2, (n % 2) * 512:(n % 2) * 512 + 512]
                    ready(dve, (name, n))
                    free(dve.tensor_tensor(part, part, PSb((name, n)), ALU.add), (name, n))
                was_freed(dve, (name, 7))
                dve.sem_inc(sem("resid_done"), 1)

            dve.wait_ge(sem("pos_in"), 16)
            dve.wait_ge(sem("const_in"), 16)
            dve.wait_ge(sem("gain_in"), 16)
            angle, turns = tmp[:, 2, :], tmp[:, 3, :]
            dve.tensor_copy(turns, posi).then_inc(sem("pos_read"), 1)
            dve.wait_ge(sem("pos_read"), 1)
            chain(dve.tensor_scalar(angle, turns, const[:, C_INV:C_INV + 1], None, ALU.mult))
            for n in range(2):
                r = tmp[:, n, :]
                chain(dve.tensor_scalar(turns, angle, INV_2PI, 0.25 * n, ALU.mult, ALU.add))
                chain(dve.tensor_scalar(turns, turns, ROUNDER, None, ALU.add))
                chain(dve.tensor_scalar(turns, turns, ROUNDER, None, ALU.subtract))
                chain(dve.scalar_tensor_tensor(r, turns, -TWO_PI[0], angle, ALU.mult, ALU.add))
                chain(dve.scalar_tensor_tensor(r, turns, -TWO_PI[1], r, ALU.mult, ALU.add))
                chain(dve.scalar_tensor_tensor(r, turns, -TWO_PI[2], r, ALU.mult, ALU.add))
                if n == 1:
                    chain(dve.tensor_scalar(r, r, 0.5 * np.pi, None, ALU.add))
                dve.tensor_scalar(r, r, PI_BELOW, -PI_BELOW, ALU.min, ALU.max).then_inc(sem("angle"), 1)
            dve.wait_ge(sem("sines"), 2)
            chain(dve.tensor_scalar(sinT, sinT, const[:, C_SGN:C_SGN + 1], None, ALU.mult))

            norm(0)

            def rotate(dst, raw, swapped, key):
                if raw is not None:
                    chain(dve.tensor_tensor(dst, raw, cosT, ALU.mult))
                    return
                free(dve.tensor_tensor(tmp[:, 2, :], swapped, sinT, ALU.mult), key)
                was_freed(dve, key)
                chain(dve.tensor_tensor(dst, dst, tmp[:, 2, :], ALU.add))

            for m in range(5):
                was_freed(dve, ("z", m))
                dve.tensor_tensor(qn[:, m, :], zT[:, m, :], zT[:, m, :], ALU.mult)\
                   .then_inc(sem("latent_sq"), 1)
            ready(dve, ("z", 5))
            free(dve.tensor_tensor(kr, PSb(("z", 5)), cosT, ALU.mult), ("z", 5))
            was_freed(dve, ("z", 5))
            ready(dve, ("z", 6))
            rotate(kr, None, PSb(("z", 6)), ("z", 6))
            for n, width in enumerate((Q_LORA, KV_LORA)):
                ready(dve, ("zss", n))
                free(dve.tensor_scalar(tmp[:, n, :], PSb(("zss", n)), 1.0 / width, EPS, ALU.mult, ALU.add),
                     ("zss", n))
                was_freed(dve, ("zss", n))
                dve.sem_inc(sem("latent_mean"), 1)
            for n in range(2):
                dve.wait_ge(sem("latent_root"), n + 1)
                chain(dve.reciprocal(tmp[:, n, :], tmp[:, n, :]))
            for m in range(5):
                g = G_AT["q"] + m if m < QC else G_AT["kv"] + m - QC
                dve.scalar_tensor_tensor(zT[:, m, :], zT[:, m, :], gain[:, g:g + 1],
                                         tmp[:, 0 if m < QC else 1, :], ALU.mult, ALU.mult)\
                   .then_inc(sem("latent"), 1)
            for m in range(5):
                dve.wait_ge(sem("latent_high"), m + 1)
                dve.tensor_tensor(x_lo[:, m, :], zT[:, m, :], f32(x_hi[:, m, :]), ALU.subtract)\
                   .then_inc(sem("latent_low"), 1)
            for j in range(4):
                ready(dve, ("q_up", 8 + j))
                free(dve.tensor_tensor(qr[:, j, :], PSb(("q_up", 8 + j)), cosT, ALU.mult), ("q_up", 8 + j))
            was_freed(dve, ("q_up", 11))
            for j in range(4):
                ready(dve, ("q_up", 12 + j))
                rotate(qr[:, j, :], None, PSb(("q_up", 12 + j)), ("q_up", 12 + j))
            dve.sem_inc(sem("rotated"), 1)

            def row_max(n):
                qt = n % 4
                s = PSb(("s", n))
                ready(dve, ("s", n))
                if n >= 2:
                    was_freed(dve, ("s", n - 2))
                chain(dve.tensor_tensor(s[:, qt * P:(qt + 1) * P], s[:, qt * P:(qt + 1) * P], causal, ALU.add))
                chain(dve.tensor_reduce(stat[:, 4 + n % 2:5 + n % 2], s[:, 0:(qt + 1) * P], AX.X, ALU.max))
                dve.tensor_scalar(stat[:, 12 + n % 2:13 + n % 2], stat[:, 4 + n % 2:5 + n % 2],
                                  -ATT_SCALE, None, ALU.mult).then_inc(sem("bias"), 1)

            for n in range(2):
                row_max(n)
            for n in range(4 * HEADS):
                w = (n % 4 + 1) * P
                was_freed(dve, ("s", n))
                chain(dve.reciprocal(stat[:, 6 + n % 2:7 + n % 2], stat[:, 14 + n % 2:15 + n % 2]))
                dve.tensor_scalar(prob[:, n % 2, 0:w], prob[:, n % 2, 0:w], stat[:, 6 + n % 2:7 + n % 2],
                                  None, ALU.mult).then_inc(sem("prob"), 1)
                if n + 2 < 4 * HEADS:
                    row_max(n + 2)
                if n >= 7 and (n - 7) % 4 == 0:
                    h = (n - 7) // 4
                    dve.wait_ge(sem("o_high"), h + 1)
                    free(dve.tensor_tensor(x_lo[:, h, :], PSb(("o", h)), f32(x_hi[:, h, :]), ALU.subtract),
                         ("o", h))
            h = HEADS - 1
            dve.wait_ge(sem("o_high"), h + 1)
            free(dve.tensor_tensor(x_lo[:, h, :], PSb(("o", h)), f32(x_hi[:, h, :]), ALU.subtract), ("o", h))
            add_to_resid("mla_out", 1)

            def sixteen(values, places, source, groups):
                for half in range(2):
                    part = slice(8 * half, 8 * half + 8)
                    for g in range(groups):
                        ins = dve.max(values(g)[:, part], source(g))
                    chain(ins)
                    for g in range(groups):
                        ins = dve.max_index(places(g)[:, part], values(g)[:, part], source(g))
                    if half == 0:
                        for g in range(groups):
                            ins = dve.match_replace(source(g), values(g)[:, part], source(g), LOWEST)
                    chain(ins)

            def route(layer, t):
                sixteen(lambda g: val[:, g, :], lambda g: ixu[:, g, :], lambda g: scores[:, t, g, :], 16)
                chain(dve.tensor_copy(ixf, ixu))
                v4 = val.rearrange("p (h s) k -> p h s k", s=2)
                full = [P, HEADS, TOPK, TOPK]
                chain(dve.tensor_tensor(cand, wide(v4[:, :, 0], full, 3), wide(v4[:, :, 1], full, 2), ALU.add))
                sixteen(lambda g: top[:, t, g, :], lambda g: posu[:, g * TOPK:(g + 1) * TOPK],
                        lambda g: cand[:, g].rearrange("p a b -> p (a b)"), HEADS)
                chain(dve.tensor_scalar(halfu[:, 0, :], posu, 4, None, ALU.logical_shift_right))
                chain(dve.tensor_scalar(halfu[:, 1, :], posu, 15, None, ALU.bitwise_and))
                chain(dve.tensor_copy(halff, halfu))
                i4 = ixf.rearrange("p (h s) k -> p h s k", s=2)
                hot = cand.rearrange("p h a b -> p (h a) b")
                for s in range(2):
                    chain(dve.tensor_tensor(hot, wide(halff[:, s, :], [P, HK, TOPK], 2),
                                            wide(iota[:, 0:TOPK], [P, HK, TOPK], 1), ALU.is_equal))
                    chain(dve.tensor_tensor(picked.rearrange("p (h k) a -> p h k a", h=HEADS), cand,
                                            wide(i4[:, :, s], full, 2), ALU.mult))
                    chain(dve.tensor_reduce(ids[:, s, t, :], picked, AX.X, ALU.add))
                chain(dve.tensor_copy(gsum[:, 0:HEADS], top[:, t, :, 0]))
                dve.tensor_tensor(top[:, t], top[:, t], wide(gsum[:, 0:HEADS], [P, HEADS, TOPK], 2),
                                  ALU.subtract).then_inc(sem("top_less_max"), 1)

            def experts(layer):
                bv = BASE[f"v{layer}"]
                norm(2 * layer + 1)
                for n in range(16):
                    ready(dve, (f"sc{layer}", n))
                    free(dve.tensor_copy(scores[:, :, n, :], PSb((f"sc{layer}", n))
                                         .rearrange("p (t k) -> p t k", t=TT)), (f"sc{layer}", n))
                was_freed(dve, (f"sc{layer}", 15))
                for t in range(TT):
                    route(layer, t)
                dve.wait_ge(sem("top_less_max"), TT * (layer + 1))
                dve.sem_inc(sem("routed"), 1)
                dve.wait_ge(sem("top_exp"), layer + 1)
                flat = top.rearrange("p t h k -> p (t h) k")
                chain(dve.tensor_reduce(gsum, flat, AX.X, ALU.add))
                chain(dve.reciprocal(gsum, gsum))
                dve.tensor_tensor(flat, flat, wide(gsum, [P, TT * HEADS, TOPK], 2), ALU.mult)\
                   .then_inc(sem("gates"), 1)
                for n in range(3):
                    dve.wait_ge(sem("routeT_ps"), 3 * layer + n + 1)
                    chain(dve.tensor_copy(routeT[:, n, :], PS[:, 4 + n, :]))
                dve.sem_inc(sem("routeT"), 1)

                with dve.Fori(0, TURNS - ROUTED_TURN) as i:
                    dve.tensor_copy(window, routeT[:, :, bass.ds(i * TOK, TOK)]).then_inc(sem("window"), 1)
                    dve.wait_ge(sem("window"), i + ((TURNS - ROUTED_TURN) * layer + 1))
                    for k in range(TOK):
                        if k % 4 == 0:
                            dve.wait_ge(gates_made, i * (TOK // 4) + (k // 4 + 1 + SEQ // 4 * layer))
                        dve.tensor_scalar(onehot1[:, k % 8, :], iota, window[:, 0, k:k + 1], None, ALU.is_equal)
                        ins = dve.tensor_scalar(onehot2[:, k % 8, :], iota, window[:, 1, k:k + 1],
                                                window[:, 2, k:k + 1], ALU.is_equal, ALU.mult)
                        if k % 4 == 3:
                            ins.then_inc(onehots, 1)
                    dve.wait_ge(onehots, i * (TOK // 4) + (TOK // 4 + SEQ // 4 * layer))

                def make_product(i, j):
                    b = j // GF
                    dve.wait_ge(act_loaded[j], (i + (TURNS * layer + 1)) * 16)
                    if j % GF == 0:
                        dve.wait_ge(gate_loaded[b], (i + (TURNS * layer + 1)) * 16)
                    if not isinstance(i, int) or j >= RING:
                        dve.wait_ge(sem("product_low"), i * UNROLL + (j - RING + 1 + NKEYS * layer))
                    dve.tensor_tensor(product[:, j % RING, :], act_st[:, j, :], gate_ld[:, b, :, j % GF],
                                      ALU.mult).then_inc(sem("product_made"), 1)

                def product_low(c, j):
                    dve.wait_ge(sem("product_high"), c + (NKEYS * layer + 1))
                    dve.tensor_tensor(x_lo[:, j % RING, :], product[:, j % RING, :],
                                      f32(x_hi[:, j % RING, :]), ALU.subtract).then_inc(sem("product_low"), 1)

                make_product(0, 0)
                for j in range(1, UNROLL):
                    make_product(0, j)
                    product_low(j - 1, j - 1)
                with dve.Fori(1, TURNS) as i:
                    for j in range(UNROLL):
                        make_product(i, j)
                        product_low(i * UNROLL + (j - 1), (j - 1) % UNROLL)
                product_low(NKEYS - 1, UNROLL - 1)
                add_to_resid(f"v{layer}", 2 * layer + 2)

            experts(0)

            norm(2)
            dve.tensor_tensor(lbt[:, 2, :], gain[:, G_AT["lb0"]:G_AT["lb0"] + KC],
                              gain[:, G_AT["lb1"]:G_AT["lb1"] + KC], ALU.max).then_inc(sem("bound"), 1)
            dve.wait_ge(sem("bound"), 1)
            both = gain[:, G_AT["lb0"]:G_AT["lb0"] + 2 * KC].rearrange("p (s k) -> p s k", s=2)
            dve.tensor_tensor(lbt[:, 0:2, :], both, wide(lbt[:, 2, :], [P, 2, KC], 1), ALU.subtract)\
               .then_inc(sem("bound_less_max"), 1)
            dve.wait_ge(sem("bound_exp"), 1)
            chain(dve.tensor_tensor(lbt[:, 2, :], lbt[:, 0, :], lbt[:, 1, :], ALU.add))
            chain(dve.reciprocal(lbt[:, 2, :], lbt[:, 2, :]))
            chain(dve.tensor_tensor(lbt[:, 0:2, :], lbt[:, 0:2, :], wide(lbt[:, 2, :], [P, 2, KC], 1), ALU.mult))
            chain(dve.tensor_tensor(lbt[:, 1, :], lbt[:, 0, :], lbt[:, 1, :], ALU.add))
            chain(dve.tensor_tensor(lbt[:, 1, :], lbt[:, 1, :], lbt[:, 0, :], ALU.subtract))
            chain(dve.tensor_scalar(lbt[:, 3, :], lbt[:, 1, :], -1.0, 1.0, ALU.mult, ALU.add))
            for h in range(HEADS):
                was_freed(dve, ("hg_f", h))
                chain(dve.tensor_scalar(gb[:, h, :], gb[:, h, :], lbt[:, 3, h:h + 1], lbt[:, 1, h:h + 1],
                                        ALU.mult, ALU.add))
                chain(dve.tensor_scalar(gk[:, h, :], gb[:, h, :], -1.0, 1.0, ALU.mult, ALU.add))
                dve.tensor_scalar(gb[:, h, :], gb[:, h, :], SMALLEST_F, None, ALU.max)\
                   .then_inc(sem("forget"), 1)
            dve.wait_ge(sem("mask_in"), 16)
            for h in range(HEADS):
                dve.wait_ge(sem("forget_log"), h + 1)
                dve.tensor_tensor_scan(gb[:, h, :], keep, dd if h % 2 == 0 else ee, 0.0, ALU.mult, ALU.add)\
                   .then_inc(sem("cumulated"), 1)
            dve.wait_ge(sem("cumulated"), HEADS)

            def chunked(ap):
                return ap.rearrange("p (c t) -> p c t", t=P)

            def mask_level(h, lv):
                k = (LEVELS + 1) * h + lv
                ready(dve, ("a", h, lv))
                if k >= 2:
                    dve.wait_ge(sem("a_used"), k - 1)
                free(dve.tensor_tensor(a_sb[:, k % 2, :].rearrange("p (c t) -> p c t", t=P),
                                       PSb(("a", h, lv)).rearrange("p (c t) -> p c t", t=P),
                                       level_mask[lv].unsqueeze(1).broadcast_to([P, TT, P]), ALU.mult),
                     ("a", h, lv))

            for h in range(HEADS):
                b4 = chunked(gb[:, h, :])
                dve.tensor_tensor(chunked(dd), b4[:, :, P - 1:P].broadcast_to([P, TT, P]), b4, ALU.subtract)\
                   .then_inc(sem("to_end"), 1)
                dve.wait_ge(sem("decay"), h + 1)
                if h >= 1:
                    ready(dve, ("ho", h - 1))
                dve.tensor_tensor(qe, gq[:, h, :], e_all, ALU.mult).then_inc(sem("q_decayed"), 1)
                dve.wait_ge(sem("level_exp"), (2 * LEVELS + 1) * h + 1)
                dve.tensor_tensor(kdec, gk[:, h, :], ee, ALU.mult).then_inc(sem("k_decayed"), 1)
                for lv in range(LEVELS + 1):
                    if lv < LEVELS:
                        m = P >> (lv + 1)

                        def halves(ap):
                            return ap.rearrange("p (b s m) -> p b s m", s=2, m=m)

                        bb = gb[:, h, :].rearrange("p (b m) -> p b m", m=2 * m)
                        d3 = dd.rearrange("p (b m) -> p b m", m=2 * m)
                        dve.tensor_tensor(d3, bb, bb[:, :, m - 1:m].broadcast_to([P, SEQ // (2 * m), 2 * m]),
                                          ALU.subtract).then_inc(sem("level_diff"), 1)
                    if lv < LEVELS:
                        k = LEVELS * h + lv
                        dve.wait_ge(sem("level_exp"), (2 * LEVELS + 1) * h + 1 + 2 * (lv + 1))
                        if k >= 2:
                            ready(dve, ("a", (k - 2) // LEVELS, (k - 2) % LEVELS))
                        xo = halves(xx[:, k % 2, :])
                        dve.tensor_tensor(xo[:, :, 0], halves(gk[:, h, :])[:, :, 0], halves(ee)[:, :, 0], ALU.mult)
                        dve.tensor_tensor(xo[:, :, 1], halves(gq[:, h, :])[:, :, 1], halves(ee)[:, :, 1],
                                          ALU.mult).then_inc(sem("level_x"), 1)
                    if lv >= 1:
                        mask_level(h, lv - 1)
                ready(dve, ("st", h))
                st = PSb(("st", h))
                chain(dve.tensor_copy(state[:, 0, :], st[:, 0:P]))
                for c in (1, 2):
                    ins = dve.scalar_tensor_tensor(state[:, c, :], state[:, c - 1, :],
                                                   e_all[:, c * P + P - 1:c * P + P],
                                                   st[:, c * P:(c + 1) * P], ALU.mult, ALU.add)
                    chain(ins) if c == 1 else free(ins, ("st", h))
                was_freed(dve, ("st", h))
                dve.sem_inc(sem("state_done"), 1)
                mask_level(h, LEVELS)
            ready(dve, ("ho", HEADS - 1))
            for h in range(HEADS):
                was_freed(dve, ("ho", h))
                if h >= 2:
                    ready(dve, ("hss", h - 2))
                sq = a_sb[:, h % 2, :]
                dve.tensor_tensor(sq, gq[:, h, :], gq[:, h, :], ALU.mult).then_inc(sem("head_sq"), 1)
            for h in range(HEADS):
                ready(dve, ("hss", h))
                free(dve.tensor_scalar(rstd_h[:, h, :], PSb(("hss", h)), 1.0 / P, EPS, ALU.mult, ALU.add),
                     ("hss", h))
                was_freed(dve, ("hss", h))
                dve.sem_inc(sem("head_mean"), 1)
            for h in range(HEADS):
                dve.wait_ge(sem("head_root"), h + 1)
                chain(dve.reciprocal(rstd_h[:, h, :], rstd_h[:, h, :]))
                chain(dve.tensor_tensor(gq[:, h, :], gq[:, h, :], rstd_h[:, h, :], ALU.mult))
                g = G_AT["out"] + h
                was_freed(dve, ("hg_g", h))
                dve.scalar_tensor_tensor(gq[:, h, :], gq[:, h, :], gain[:, g:g + 1], gg_[:, h, :],
                                         ALU.mult, ALU.mult).then_inc(sem("gated"), 1)
            for h in range(HEADS):
                dve.wait_ge(sem("gated_high"), h + 1)
                dve.tensor_tensor(x_lo[:, h, :], gq[:, h, :], f32(x_hi[:, h, :]), ALU.subtract)\
                   .then_inc(sem("gated_low"), 1)
            add_to_resid("hg_out", 3)

            experts(1)

            dve.sem_inc(sem("final_free"), 1)
            scale_resid(4)
            dve.wait_ge(sem("fgain_in"), 16)
            for t in range(TT):
                dve.scalar_tensor_tensor(final[:, t, :], resid[:, t, :], stat[:, t:t + 1], final_gain,
                                         ALU.mult, ALU.mult).then_inc(sem("final_made"), 1)

        @block.tensor
        def _(pe):
            def begin(key):
                if jobs.before[key] is not None:
                    was_freed(pe, jobs.before[key])

            def end(mm, key):
                mm.then_inc(sem(jobs.ready[key][0]), 1)

            def three(ps, wh, wl, xh, xl, start, stop):
                pe.matmul(ps, wh, xh, start=start, stop=False)
                pe.matmul(ps, wh, xl, start=False, stop=False)
                return pe.matmul(ps, wl, xh, start=False, stop=stop)

            def across(ps, slot):
                for kc in range(KC):
                    w = slice(kc * P, (kc + 1) * P)
                    mm = three(ps, w_hi[:, slot, w], w_lo[:, slot, w], x_hi[:, kc, :], x_lo[:, kc, :],
                               kc == 0, kc == KC - 1)
                return mm

            def projection(name, count):
                for m in range(count):
                    n = BASE[name] + m
                    pe.wait_ge(lo_ready, n + 1)
                    begin((name, m))
                    end(across(PSb((name, m)), n % RING), (name, m))

            def token_major(name, kcs, x_at, x_wait):
                for n in range(8):
                    begin((name, n))
                for kc in range(kcs):
                    tile = BASE[name] + kc
                    pe.wait_ge(lo_ready, tile + 1)
                    x_wait(kc)
                    rows(lambda n: PSb((name, n)), tile % RING, x_at + kc, kc == 0, kc == kcs - 1,
                         (lambda mm, n: end(mm, (name, n))) if kc == kcs - 1 else None)

            def rows(bank, slot, xc, start, stop, signal):
                for n in range(8):
                    t, w = slice(n // 2 * P, n // 2 * P + P), slice(n % 2 * 512, n % 2 * 512 + 512)
                    mm = three(bank(n), x_hi[:, xc, t], x_lo[:, xc, t], w_hi[:, slot, w],
                               w_lo[:, slot, w], start, stop)
                    if signal:
                        signal(mm, n)
                if not signal:
                    mm.then_inc(tile_used, 1)

            def norm(k):
                pe.wait_ge(sem("scaled"), TT * (k + 1))
                for c in range(KC):
                    begin(("xT", k, c))
                    for t in range(TT):
                        mm = pe.transpose(PSb(("xT", k, c))[:, t * P:(t + 1) * P],
                                          scaled[:, t, c * P:(c + 1) * P], ident)
                    end(mm, ("xT", k, c))
                was_freed(pe, ("xT", k, KC - 1))

            pe.wait_ge(sem("const_in"), 16)
            norm(0)
            projection("z", 7)
            for n, ms in enumerate((range(0, QC), range(QC, QC + VC))):
                begin(("zss", n))
                for m in ms:
                    pe.wait_ge(sem("latent_sq"), m + 1)
                    mm = pe.matmul(PSb(("zss", n)), ones, qn[:, m, :], start=m == ms[0], stop=m == ms[-1])
                end(mm, ("zss", n))
            pe.wait_ge(sem("latent_low"), 5)

            def blocks_of(name, count, kcs, x_at):
                for m in range(count):
                    begin((name, m))
                    for kc in range(kcs):
                        b = kcs * m + kc
                        n = BASE[name] + b // 8
                        w = slice(b % 8 * P, b % 8 * P + P)
                        if b % 8 == 0:
                            pe.wait_ge(lo_ready, n + 1)
                        mm = three(PSb((name, m)), w_hi[:, n % RING, w], w_lo[:, n % RING, w],
                                   x_hi[:, x_at + kc, :], x_lo[:, x_at + kc, :], kc == 0, kc == kcs - 1)
                        if b % 8 == 7 and kc < kcs - 1:
                            mm.then_inc(tile_used, 1)
                    end(mm, (name, m))

            blocks_of("q_up", 16, QC, 0)
            blocks_of("k_up", 8, VC, QC)
            token_major("v_up", VC, QC, lambda kc: None)

            pe.wait_ge(sem("rotated"), 1)
            was_freed(pe, ("v_up", 7))
            for n in range(4 * HEADS + 2):
                if n < 4 * HEADS:
                    h, qt = n // 4, n % 4
                    w, q, part = (qt + 1) * P, slice(qt * P, qt * P + P), slice(h % 2 * 64, h % 2 * 64 + 64)
                    begin(("s", n))
                    s = PSb(("s", n))[:, 0:w]
                    pe.matmul(s, qn[:, h, q], kn[:, h, 0:w], start=True, stop=False)
                    end(pe.matmul(s, qr[part, h // 2, q], kr[part, 0:w], start=False, stop=True), ("s", n))
                if n >= 2:
                    k = n - 2
                    h, qt = k // 4, k % 4
                    pe.wait_ge(sem("prob"), k + 1)
                    begin(("pT", k))
                    for j in range(qt + 1):
                        mm = pe.transpose(PSb(("pT", k))[:, j * P:(j + 1) * P],
                                          prob[:, k % 2, j * P:(j + 1) * P], ident)
                    end(mm, ("pT", k))
                    if qt == 3:
                        begin(("o", h))
                        was_freed(pe, ("pT", k))
                        for j in range(TT):
                            mm = pe.matmul(PSb(("o", h))[:, j * P:SEQ], vtok[:, j, h * P:(h + 1) * P],
                                           pT[:, h % 2, j, j * P:SEQ], start=j == 0, stop=j == TT - 1)
                        end(mm, ("o", h))
            token_major("mla_out", 8, 0, lambda kc: was_freed(pe, ("o", kc)))

            def experts(layer):
                bu, bv, bq = BASE[f"u{layer}"], BASE[f"v{layer}"], BASE[f"pq{layer}"]
                if layer == 0:
                    pe.sem_inc(gates_made, 2)
                norm(2 * layer + 1)
                pe.wait_ge(sem("keys_in"), 16 * (layer + 1))
                for n in range(17):
                    if n < 16:
                        key = (f"pq{layer}", n)
                        pe.wait_ge(lo_ready, bq + n + 1)
                        begin(key)
                        end(across(PSb(key), (bq + n) % RING), key)
                    if n >= 1:
                        key = (f"sc{layer}", n - 1)
                        begin(key)
                        was_freed(pe, (f"pq{layer}", n - 1))
                        for t in range(TT):
                            mm = pe.matmul(PSb(key)[:, t * P:(t + 1) * P], qT[:, (n - 1) % 2, t * P:(t + 1) * P],
                                           keysT[:, n - 1, :], start=True, stop=True)
                        end(mm, key)
                was_freed(pe, (f"sc{layer}", 15))

                def u_tile(i, j):
                    c = i * UNROLL + j
                    pe.wait_ge(lo_ready, c + (bu + 1))
                    pe.wait_ge(gelu_done, c + (NKEYS * layer + 1))
                    across(PS[:, j % 4, :], (bu + j) % RING).then_inc(tile_used, 1)

                with pe.Fori(0, ROUTED_TURN) as i:
                    for j in range(UNROLL):
                        u_tile(i, j)
                for n in range(3):
                    pe.wait_ge(*((sem("routed"), layer + 1) if n < 2 else (sem("gates"), layer + 1)))
                    for t in range(TT):
                        src = ids[:, n, t, :] if n < 2 else top[:, t].rearrange("p h k -> p (h k)")
                        mm = pe.transpose(PS[:, 4 + n, t * P:(t + 1) * P], src, ident)
                    mm.then_inc(sem("routeT_ps"), 1)
                pe.wait_ge(sem("routeT"), layer + 1)

                def spread(turn, q):
                    pe.wait_ge(onehots, turn * (TOK // 4) + (q + 1 + SEQ // 4 * layer))
                    pe.wait_ge(gate_moved, turn * (TOK // 4) + (q + 1 + SEQ // 4 * layer))
                    for k in range(4):
                        s = (4 * q + k) % 8
                        mm = pe.matmul(PS[:, 4 + q % 2, k * P:(k + 1) * P], onehot1[:, s, :],
                                       onehot2[:, s, :], start=True, stop=True)
                    mm.then_inc(gates_made, 1)

                with pe.Fori(ROUTED_TURN, TURNS) as i:
                    for j in range(UNROLL):
                        u_tile(i, j)
                        for q in range(j * TOK // 4 // UNROLL, (j + 1) * TOK // 4 // UNROLL):
                            spread(i - ROUTED_TURN, q)
                pe.wait_ge(gelu_done, NKEYS * (layer + 1) + 4)
                pe.wait_ge(gate_moved, SEQ // 4 * (layer + 1) + 2)

                def v_tile(i, j, start=False, signal=None):
                    c = i * UNROLL + j
                    pe.wait_ge(lo_ready, c + (bv + 1))
                    pe.wait_ge(sem("product_low"), c + (NKEYS * layer + 1))
                    rows(lambda n: PSb((f"v{layer}", n)), (bv + j) % RING, j % RING, start,
                         signal is not None, signal)

                for j in range(UNROLL):
                    v_tile(0, j, start=j == 0)
                with pe.Fori(1, TURNS - 1) as i:
                    for j in range(UNROLL):
                        v_tile(i, j)
                for j in range(UNROLL):
                    v_tile(TURNS - 1, j, signal=(lambda mm, n: end(mm, (f"v{layer}", n)))
                           if j == UNROLL - 1 else None)

            experts(0)

            norm(2)
            projection("hg_q", 8)
            projection("hg_f", 8)
            projection("hg_g", 8)
            token_major("hg_i", 8, 0, lambda kc: None)
            was_freed(pe, ("hg_i", 7))

            def level(h, lv):
                begin(("a", h, lv))
                k = LEVELS * h + lv
                if lv < LEVELS:
                    pe.wait_ge(sem("level_x"), k + 1)
                for c in range(TT):
                    t = slice(c * P, (c + 1) * P)
                    lhs, rhs = (xx[:, k % 2, t],) * 2 if lv < LEVELS else (gk[:, h, t], gq[:, h, t])
                    mm = pe.matmul(PSb(("a", h, lv))[:, t], lhs, rhs, start=True, stop=True)
                end(mm, ("a", h, lv))

            def level_values(h, lv):
                was_freed(pe, ("a", h, lv))
                for c in range(TT):
                    t = slice(c * P, (c + 1) * P)
                    mm = pe.matmul(PSb(("ho", h))[:, t], vrec[:, c, h * P:(h + 1) * P],
                                   a_sb[:, ((LEVELS + 1) * h + lv) % 2, t],
                                   start=lv == 0 and c == 0, stop=False,
                                   skip_group_check=True)
                mm.then_inc(sem("a_used"), 1)

            for h in range(HEADS):
                begin(("kd", h))
                pe.wait_ge(sem("k_decayed"), h + 1)
                for c in range(TT):
                    mm = pe.transpose(PSb(("kd", h))[:, c * P:(c + 1) * P], kdec[:, c * P:(c + 1) * P], ident)
                end(mm, ("kd", h))
                begin(("ho", h))
                for lv in range(LEVELS + 1):
                    if lv == 1:
                        begin(("st", h))
                        was_freed(pe, ("kd", h))
                        for c in range(TT - 1):
                            mm = pe.matmul(PSb(("st", h))[:, c * P:(c + 1) * P], kdT[:, c, :],
                                           vrec[:, c, h * P:(h + 1) * P], start=True, stop=True)
                        end(mm, ("st", h))
                    level(h, lv)
                    if lv >= 1:
                        level_values(h, lv - 1)
                level_values(h, LEVELS)
                pe.wait_ge(sem("state_done"), h + 1)
                pe.wait_ge(sem("q_decayed"), h + 1)
                for c in range(1, TT):
                    t = slice(c * P, (c + 1) * P)
                    mm = pe.matmul(PSb(("ho", h))[:, t], state[:, c - 1, :], qe[:, t], start=False,
                                   stop=c == TT - 1, skip_group_check=True)
                end(mm, ("ho", h))
            for h in range(HEADS):
                begin(("hss", h))
                pe.wait_ge(sem("head_sq"), h + 1)
                end(pe.matmul(PSb(("hss", h)), ones, a_sb[:, h % 2, :], start=True, stop=True), ("hss", h))
            token_major("hg_out", 8, 0, lambda kc: pe.wait_ge(sem("gated_low"), kc + 1))

            experts(1)


def _constants():
    c = np.zeros((P, C_COLS), np.float32)
    c[:, C_ID:C_ID + P] = np.eye(P)
    c[:, C_ONE:C_ONE + P] = 1.0
    c[:, C_IOTA:C_IOTA + P] = np.arange(P)
    c[:, C_CAUSAL:C_CAUSAL + P] = np.where(np.arange(P)[None, :] <= np.arange(P)[:, None], 0.0, -1e30)
    row = np.arange(P) % ROPE
    inv = np.float32(THETA) ** (-np.arange(0, ROPE, 2, dtype=np.float32) / np.float32(ROPE))
    c[:, C_INV] = inv[row % (ROPE // 2)]
    c[:, C_SGN] = np.where(row < ROPE // 2, -1.0, 1.0)
    m = np.zeros((P, SEQ + 8 * P), np.float32)
    m[:, 0:SEQ] = (np.arange(SEQ) % P != 0)
    s, t = np.arange(P)[:, None], np.arange(P)[None, :]
    for lv in range(LEVELS):
        half = P >> (lv + 1)
        m[:, SEQ + P * lv:SEQ + P * (lv + 1)] = ((s // (2 * half) == t // (2 * half))
                                                 & (s // half % 2 == 0) & (t // half % 2 == 1))
    m[:, SEQ + P * LEVELS:] = (s == t)
    return c, np.where(m > 0, 0x3F80, 0).astype(np.uint16)


def _across_tiles(w):
    n = w.shape[1]
    return w.reshape(KC, P, n // P, P).transpose(2, 1, 0, 3).reshape(n // P, P, KC * P)


def _block_tiles(w):
    k, n = w.shape
    b = w.reshape(k // P, P, n // P, P).transpose(2, 0, 1, 3).reshape(-1, 8, P, P)
    return b.transpose(0, 2, 1, 3).reshape(-1, P, 8 * P)


def _columns(g):
    return g.reshape(-1, P).T


def kernel(**inputs):
    import concourse.bacc as _bacc
    from concourse import mybir as _mybir
    from concourse.bass_utils import run_bass_kernel_spmd as _run

    a = {k: np.asarray(v) for k, v in inputs.items()}
    cat = np.concatenate
    w_in = a["mla_w_in"][0]
    r = w_in[:, Q_LORA + KV_LORA:]
    swap = cat([r[:, ROPE // 2:], r[:, :ROPE // 2]], 1)
    z = cat([w_in[:, :Q_LORA + KV_LORA], r, r, swap, swap], 1)
    q_up = a["mla_w_q_up"][0].reshape(Q_LORA, HEADS, NOPE + ROPE)
    qr = q_up[:, :, NOPE:]
    qs = cat([qr[:, :, ROPE // 2:], qr[:, :, :ROPE // 2]], 2)
    q_all = cat([q_up[:, :, :NOPE].reshape(Q_LORA, -1), qr.reshape(Q_LORA, -1), qs.reshape(Q_LORA, -1)], 1)
    kv_up = a["mla_w_kv_up"][0].reshape(KV_LORA, HEADS, 2 * P)
    mla_t = cat([_across_tiles(z), _block_tiles(q_all), _block_tiles(kv_up[:, :, :P].reshape(KV_LORA, -1)),
                 kv_up[:, :, P:].reshape(VC, P, DM), a["mla_w_out"][0].reshape(8, P, DM)], 0)
    hg = a["hg_w_in"][0]
    hg_t = cat([_across_tiles(hg[:, :2 * DM]), _across_tiles(hg[:, 3 * DM:]),
                hg[:, 2 * DM:3 * DM].reshape(8, P, DM), a["hg_w_out"][0].reshape(8, P, DM)], 0)
    pq_t = np.stack([_across_tiles(w) for w in a["peer_w_q"]])
    keys = a["peer_sub_keys"].reshape(2, 16, NKEYS, P).transpose(0, 3, 1, 2)
    u_t = a["peer_u"].reshape(2, NKEYS, NKEYS, KC, P).transpose(0, 2, 4, 3, 1).reshape(2, NKEYS, P, DM)
    v_t = a["peer_v"].reshape(2, NKEYS, NKEYS, DM).transpose(0, 2, 1, 3)
    gains = cat([_columns(g) for g in (a["ln_mix"][0], a["ln_ffn"][0], a["ln_mix"][1], a["ln_ffn"][1],
                                       a["mla_q_norm"][0], a["mla_kv_norm"][0], a["hg_out_norm"][0],
                                       a["hg_lb"][0], a["hg_lb"][1])], 1)
    consts, masks = _constants()
    arrays = {
        "x": a["x"][0], "pos": a["positions"], "consts": consts, "masks": masks, "gains": gains,
        "fgain": a["ln_final"][None], "mla_t": mla_t, "hg_t": hg_t, "pq_t": pq_t, "keys_t": keys,
        "u_t": u_t, "v_t": v_t,
    }
    arrays = {f"in_{k}": np.ascontiguousarray(v) for k, v in arrays.items()}
    nc = _bacc.Bacc("TRN2", target_bir_lowering=False, num_devices=1)
    args = [nc.dram_tensor(k, v.shape, _mybir.dt.from_np(v.dtype), kind="ExternalInput").ap()
            for k, v in arrays.items()]
    args.append(nc.dram_tensor("out_0", (SEQ, DM), _mybir.dt.float32, kind="ExternalOutput").ap())
    model(nc, *args)
    got = _run(nc, [arrays], core_ids=[0]).results[0]["out_0"]
    return got.reshape(1, SEQ, DM)
```

```python
from contextlib import ExitStack

import numpy as np

import concourse.bass as bass
from concourse import mybir

ALU = mybir.AluOpType
ACT = mybir.ActivationFunctionType
AX = mybir.AxisListType
F32 = mybir.dt.float32
F32R = mybir.dt.float32r
BF16 = mybir.dt.bfloat16
F16 = mybir.dt.float16
I32 = mybir.dt.int32
U32 = mybir.dt.uint32

P = 128
SEQ, DM = 512, 1024
TT = SEQ // P
KC = DM // P
HEADS = 8
EPS = 1e-6
Q_LORA, KV_LORA, NOPE, ROPE = 384, 256, 128, 64
QC, VC = Q_LORA // P, KV_LORA // P
ATT_SCALE = float(NOPE + ROPE) ** -0.5
THETA = 10000.0
NKEYS, TOPK = 128, 16
HK = HEADS * TOPK
LEVELS = 7
LOWEST = -3.0e38
SMALLEST_F = 2.0 ** -63
INV_2PI = 1.0 / (2.0 * np.pi)
ROUNDER = 12582912.0
TWO_PI = [6.28125, 0.0019350051879882812]
TWO_PI.append(2.0 * np.pi - TWO_PI[0] - TWO_PI[1])
PI_BELOW = 3.1415925

RING = 4
UNROLL = 8
TURNS = NKEYS // UNROLL
ROUTED_TURN = TURNS // 2
TOK = SEQ // (TURNS - ROUTED_TURN)
HALF_TOK = TOK // 2
GF = 4
GG = NKEYS // GF
H_SLOTS = UNROLL

STREAM = [("z", 7), ("q_up", 6), ("k_up", 2), ("v_up", 2), ("mla_out", 8),
          ("pq0", 16), ("u0", NKEYS), ("v0", NKEYS),
          ("hg_q", 8), ("hg_f", 8), ("hg_g", 8), ("hg_i", 8), ("hg_out", 8),
          ("pq1", 16), ("u1", NKEYS), ("v1", NKEYS)]
BASE, N_TILES = {}, 0
for _name, _n in STREAM:
    BASE[_name] = N_TILES
    N_TILES += _n

C_ID, C_ONE, C_IOTA, C_CAUSAL, C_INV, C_SGN, C_COLS = 0, 128, 256, 384, 512, 513, 514
G_NAMES = [("mix0", KC), ("ffn0", KC), ("mix1", KC), ("ffn1", KC), ("q", QC), ("kv", VC), ("out", KC),
           ("lb0", KC), ("lb1", KC)]
G_AT, G_COLS = {}, 0
for _name, _n in G_NAMES:
    G_AT[_name] = G_COLS
    G_COLS += _n

ARENA = 26112
M_LEVEL, M_IOTA, M_COLS = SEQ, SEQ + 8 * P, SEQ + 9 * P
GATE_UNIT = 4096.0


class Banks:

    def __init__(self):
        self.bank, self.before, self.ready, self.frees = {}, {}, {}, {}
        self.signals = 0
        self.count = {"act": 0, "dve": 0, "exp": 0, "state": 0, "kd": 0, "sum": 0}
        self.turn, self.last = {}, {}

    def add(self, key, frees, tile=None, banks=tuple(range(8))):
        n = self.turn.get(banks, 0)
        self.turn[banks] = n + 1
        bank = self.bank[key] = banks[n % len(banks)]
        self.before[key] = self.last.get(bank)
        self.last[bank] = key
        if tile is None:
            self.signals += 1
            self.ready[key] = ("ps_ready", self.signals)
        else:
            self.ready[key] = ("tile_used", tile + 1)
        self.count[frees] += 1
        self.frees[key] = (frees, self.count[frees])


def recurrence():
    for n in range(8 * HEADS + 2):
        h, p = divmod(n, 8)
        if n < 8 * HEADS:
            if p == 1:
                yield "kd", h, 0
            yield "a", h, p
            if p == 2:
                yield "st", h, 0
        if n >= 2:
            yield ("values", *divmod(n - 2, 8))
            if (n - 2) % 8 == 7:
                yield "ho", (n - 2) // 8, 0
        if n % 8 == 0 and n >= 16:
            yield "hss", n // 8 - 2, 0
    yield "hss", HEADS - 1, 0


def plan():
    b = Banks()

    def norm(k):
        for c in range(KC):
            b.add(("xT", k, c), "dve")

    def eight(name, last_tile, frees):
        for n in range(8):
            b.add((name, n), frees, last_tile if n == 7 else None)

    norm(0)
    for m in range(7):
        b.add(("z", m), "dve" if m >= 5 else "act", BASE["z"] + m)
    b.add(("zss", 0), "dve")
    b.add(("zss", 1), "dve")
    for m in range(16):
        end = 3 * m + 2
        b.add(("q_up", m), "act" if m < 8 else "dve", BASE["q_up"] + end // 8 if end % 8 == 7 else None)
    for m in range(8):
        end = 2 * m + 1
        b.add(("k_up", m), "act", BASE["k_up"] + end // 8 if end % 8 == 7 else None)
    eight("v_up", BASE["v_up"] + VC - 1, "act")
    for n in range(4 * HEADS + 2):
        if n < 4 * HEADS:
            b.add(("s", n), "exp", None, (0, 1, 2))
        if n >= 2:
            b.add(("pT", n - 2), "act", None, (3, 4, 5))
            if n % 4 == 1:
                b.add(("o", (n - 2) // 4), "dve", None, (6, 7))
    eight("mla_out", BASE["mla_out"] + 7, "dve")

    def peer(layer):
        norm(2 * layer + 1)
        for n in range(17):
            if n < 16:
                b.add((f"pq{layer}", n), "act", BASE[f"pq{layer}"] + n)
            if n >= 1:
                b.add((f"sc{layer}", n - 1), "dve")
        eight(f"v{layer}", BASE[f"v{layer}"] + NKEYS - 1, "dve")

    peer(0)
    norm(2)
    for n in range(8):
        b.add(("hg_q", n), "act", BASE["hg_q"] + n)
    for n in range(8):
        b.add(("hg_f", n), "act", BASE["hg_f"] + n)
    for n in range(8):
        b.add(("hg_g", n), "act", BASE["hg_g"] + n)
    eight("hg_i", BASE["hg_i"] + 7, "act")
    for what, h, p in recurrence():
        if what == "a":
            b.add(("a", h, p), "dve", None, (0, 1, 2, 3))
        elif what != "values":
            b.add((what, h), *{"kd": ("kd", None, (4,)), "st": ("state", None, (5,)),
                               "ho": ("act", None, (6, 7)), "hss": ("sum", None, (5,))}[what])
    eight("hg_out", BASE["hg_out"] + 7, "dve")
    peer(1)
    return b


def model(nc, x, pos, consts, masks, gains, fgain, mla_t, hg_t, pq_t, keys_t, u_t, v_t, out):
    jobs = plan()
    ctx = ExitStack()
    with ctx:
        def sb(name, shape, dt=F32):
            return ctx.enter_context(nc.sbuf_tensor(name, shape, dt))

        sems = {}

        def sem(name):
            if name not in sems:
                sems[name] = ctx.enter_context(nc.semaphore(name))
            return sems[name]

        acts_dram = nc.dram_tensor("acts_dram", [NKEYS, P, SEQ], F32, kind="Internal").ap()
        gates_dram = nc.dram_tensor("gates_dram", [GG, P, SEQ, GF], F32, kind="Internal").ap()

        PS = ctx.enter_context(nc.psum_tensor("PS", [P, 8, 512], F32))
        w_raw = sb("w_raw", [P, RING, 1024])
        w_hi = sb("w_hi", [P, RING, 1024], F32R)
        w_lo = sb("w_lo", [P, RING, 1024], F32R)
        x_hi = sb("x_hi", [P, KC, SEQ], F32R)
        x_lo = sb("x_lo", [P, KC, SEQ], F32R)
        resid = sb("resid", [P, TT, DM])
        const = sb("const", [P, C_COLS])
        mask_bits = sb("mask_bits", [P, M_COLS], mybir.dt.uint16)
        mask = mask_bits[:, :].bitcast(BF16)
        gain = sb("gain", [P, G_COLS])
        stat = sb("stat", [P, 16])
        arena = sb("arena", [P, ARENA])

        ident = const[:, C_ID:C_ID + P]
        ones = const[:, C_ONE:C_ONE + P]
        iota = const[:, C_IOTA:C_IOTA + P]
        causal = const[:, C_CAUSAL:C_CAUSAL + P]
        keep = mask[:, 0:SEQ]
        iota16 = mask[:, M_IOTA:M_IOTA + P]
        level_mask = [mask[:, SEQ + P * n:SEQ + P * (n + 1)] for n in range(8)]

        def f32(ap):
            return ap.bitcast(F32)

        def cut(offset, *shape):
            n = int(np.prod(shape))
            ap = arena[:, offset:offset + n]
            if len(shape) == 1:
                return ap
            names = "abcd"[:len(shape)]
            return ap.rearrange(f"p ({' '.join(names)}) -> p {' '.join(names)}", **dict(zip(names, shape)))

        zT = cut(0, 7, SEQ)
        cosT, sinT = cut(3584, SEQ), cut(4096, SEQ)
        tmp = cut(4608, 4, SEQ)
        qn, kn = cut(6656, HEADS, SEQ), cut(10752, HEADS, SEQ)
        qr, kr = cut(14848, 4, SEQ), cut(16896, SEQ)
        vtok = cut(17408, TT, DM)
        pT = cut(21504, 2, TT, SEQ)
        prob = cut(0, 2, SEQ)
        posi = cut(21504, SEQ).bitcast(I32)
        scaled = cut(21504, TT, DM)
        act_st = cut(0, H_SLOTS, SEQ)
        gate_st = cut(4096, 2, GG, HALF_TOK, GF)
        gate_ld = cut(4096, 2, SEQ, GF)
        scores = cut(4096, TT, 16, NKEYS)
        val = cut(12288, 16, TOPK)
        ixu = cut(12544, 16, TOPK).bitcast(U32)
        ixf = cut(12800, 16, TOPK)
        top = cut(13056, TT, HEADS, TOPK)
        posu = cut(13568, HK).bitcast(U32)
        halfu = cut(13696, 2, HK).bitcast(U32)
        halff = cut(13952, 2, HK)
        ids = cut(14208, 2, TT, HK)
        gsum = cut(15232, 32)
        cand = cut(15360, HEADS, TOPK, TOPK)
        picked = cut(17408, HK, TOPK)
        onehot1 = cut(15360, 512).bitcast(F16).rearrange("p (s k) -> p s k", s=8)
        onehot2 = cut(15872, 1024).bitcast(F16).rearrange("p (s w k) -> p s w k", s=8, w=2)
        gate16 = cut(17408, SEQ // 2).bitcast(F16)
        routeT = cut(19456, 4, SEQ)
        window = cut(21504, 4, TOK)
        qT = cut(17408, 2, SEQ)
        keysT = cut(0, 16, NKEYS)
        product = cut(21504, RING, SEQ)
        gq, gk, gb, gg_, gv = (cut(4096 * n, HEADS, SEQ) for n in range(5))
        vrec = gv.rearrange("p a b -> p (a b)").rearrange("p (t d) -> p t d", t=TT)
        R0 = 20480
        e_all, diff, xx = cut(R0, 2, SEQ), cut(R0 + 1024, 2, SEQ), cut(R0 + 2048, 2, SEQ)
        kdec, kdT = cut(R0 + 3072, SEQ), cut(R0 + 3584, TT, P)
        a_sb = cut(R0 + 4096, 2, SEQ)
        state = cut(R0 + 5120, 3, P)
        lbt = cut(R0 + 5504, 4, KC)
        final_gain = cut(0, DM)
        final = cut(1024, TT, DM)

        ps_ready, tile_used = sem("ps_ready"), sem("tile_used")
        freed = {who: sem(f"{who}_freed") for who in ("act", "dve", "exp", "state", "kd", "sum")}
        hi_ready, lo_ready = sem("hi_ready"), sem("lo_ready")
        landed = [sem(f"landed{n}") for n in range(RING)]
        act_stored = [sem(f"act_stored{n}") for n in range(H_SLOTS)]
        act_loaded = [sem(f"act_loaded{n}") for n in range(H_SLOTS)]
        gate_stored = [sem(f"gate_stored{n}") for n in range(2)]
        gate_loaded = [sem(f"gate_loaded{n}") for n in range(2)]
        gelu_done = sem("gelu_done")
        gate_moved = sem("gate_moved")
        gates_made = sem("gates_made")
        onehots = sem("onehots")

        def PSb(key):
            return PS[:, jobs.bank[key], :]

        def ready(eng, key):
            name, count = jobs.ready[key]
            eng.wait_ge(sem(name), count)

        def free(ins, key):
            return ins.then_inc(freed[jobs.frees[key][0]], 1)

        def was_freed(eng, key):
            frees, count = jobs.frees[key]
            eng.wait_ge(freed[frees], count)

        blocks = {
            "z": mla_t, "pq0": pq_t[0], "u0": u_t[0], "v0": v_t[0], "hg_q": hg_t, "pq1": pq_t[1],
            "u1": u_t[1], "v1": v_t[1],
        }

        block = ctx.enter_context(nc.Block())

        @block.sync
        def _(sp):
            def load_tile(n, src, slot):
                if not isinstance(n, int) or n >= RING:
                    sp.wait_ge(lo_ready, n - (RING - 1))
                sp.dma_start(w_raw[:, slot, :], src).then_inc(landed[slot], 16)

            def load_range(name, count, first=0):
                tiles = blocks[name]
                for k in range(first, first + count):
                    load_tile(BASE[name] + k, tiles[k], (BASE[name] + k) % RING)

            sp.dma_start(resid[:, :, :], x.rearrange("(t p) d -> p t d", p=P)).then_inc(sem("x_in"), 16)
            sp.dma_start(const[:, :], consts).then_inc(sem("const_in"), 16)
            sp.dma_start(gain[:, :], gains).then_inc(sem("gain_in"), 16)
            sp.dma_start(mask_bits[:, :], masks).then_inc(sem("mask_in"), 16)
            sp.dma_start(posi, pos.partition_broadcast(P)).then_inc(sem("pos_in"), 16)
            load_range("z", 25)

            def experts(layer):
                u, v = blocks[f"u{layer}"], blocks[f"v{layer}"]
                bu, bv = BASE[f"u{layer}"], BASE[f"v{layer}"]

                was_freed(sp, ("mla_out", 7) if layer == 0 else ("hg_out", 7))
                sp.dma_start(keysT, keys_t[layer]).then_inc(sem("keys_in"), 16)
                load_range(f"pq{layer}", 16)

                def store_act(c, j):
                    sp.wait_ge(gelu_done, c + (NKEYS * layer + 4 + 1))
                    sp.dma_start(acts_dram[bass.ds(c, 1)].rearrange("a p n -> (a p) n"),
                                 act_st[:, j, :]).then_inc(act_stored[j], 16)

                def store_gates(turn, b):
                    groups = HALF_TOK // 4
                    sp.wait_ge(gate_moved, turn * (2 * groups) + (b + 1) * groups + SEQ // 4 * layer + 2)
                    sp.dma_start(
                        gates_dram[:, :, bass.ds(turn * TOK + b * HALF_TOK, HALF_TOK), :]
                        .rearrange("g p t f -> p g (t f)"),
                        gate_st[:, b].rearrange("p g t f -> p g (t f)")).then_inc(gate_stored[b], 16)

                def u_turn(i, acts, gate1, gate0):
                    for j in range(UNROLL):
                        load_tile(i * UNROLL + (bu + j), u[bass.ds(i * UNROLL + j, 1)]
                                  .rearrange("a p n -> (a p) n"), (bu + j) % RING)
                        if acts:
                            store_act(i * UNROLL + (j - UNROLL), j)
                        if j == 1 and gate1:
                            store_gates(i - (ROUTED_TURN + 2), 1)
                        if j == 5 and gate0:
                            store_gates(i - (ROUTED_TURN + 1), 0)

                u_turn(0, False, False, False)
                with sp.Fori(1, ROUTED_TURN + 1) as i:
                    u_turn(i, True, False, False)
                u_turn(ROUTED_TURN + 1, True, False, True)
                with sp.Fori(ROUTED_TURN + 2, TURNS) as i:
                    u_turn(i, True, True, True)

                def load_v(c, j):
                    load_tile(c + bv, v[bass.ds(c, 1)].rearrange("a p n -> (a p) n"), (bv + j) % RING)

                for j in range(RING):
                    load_v(j, j)
                last = TURNS - ROUTED_TURN - 1
                for j in range(UNROLL):
                    if j == 1:
                        store_gates(last - 1, 1)
                    if j == 5:
                        store_gates(last, 0)
                    store_act(NKEYS - UNROLL + j, j)
                store_gates(last, 1)
                for j in range(H_SLOTS):
                    sp.wait_ge(act_stored[j], 16 * TURNS * (layer + 1))
                for b in range(2):
                    sp.wait_ge(gate_stored[b], 16 * (TURNS - ROUTED_TURN) * (layer + 1))

                def v_turn(i, first):
                    for j in range(UNROLL):
                        if not (first and j < RING):
                            load_v(i * UNROLL + j, j)
                        if j % GF == 0:
                            b = j // GF
                            if not first:
                                sp.wait_ge(sem("product_made"), i * UNROLL + (j - GF + NKEYS * layer))
                            sp.dma_start(gate_ld[:, b].rearrange("p t f -> p (t f)"),
                                         gates_dram[bass.ds(i * 2 + b, 1)]
                                         .rearrange("a p t f -> (a p) (t f)")).then_inc(gate_loaded[b], 16)
                        if not first:
                            sp.wait_ge(sem("product_made"), i * UNROLL + (j - UNROLL + 1 + NKEYS * layer))
                        sp.dma_start(act_st[:, j, :], acts_dram[bass.ds(i * UNROLL + j, 1)]
                                     .rearrange("a p n -> (a p) n")).then_inc(act_loaded[j], 16)

                v_turn(0, True)
                with sp.Fori(1, TURNS) as i:
                    v_turn(i, False)

            experts(0)
            load_range("hg_q", 40)
            experts(1)
            sp.wait_ge(sem("final_free"), 1)
            sp.dma_start(final_gain, fgain.partition_broadcast(P)).then_inc(sem("fgain_in"), 16)
            for t in range(TT):
                sp.wait_ge(sem("final_made"), t + 1)
                sp.dma_start(out[t * P:(t + 1) * P, :], final[:, t, :]).then_inc(sem("out_done"), 16)
            sp.wait_ge(sem("out_done"), 16 * TT)

        @block.gpsimd
        def _(pool):
            def low(n, slot):
                pool.wait_ge(hi_ready, n + 1)
                pool.tensor_tensor(w_lo[:, slot, :], w_raw[:, slot, :], f32(w_hi[:, slot, :]),
                                   ALU.subtract).then_inc(lo_ready, 1)

            with pool.Fori(0, N_TILES // RING) as i:
                for j in range(RING):
                    low(i * RING + j, j)
            for n in range(N_TILES // RING * RING, N_TILES):
                low(n, n % RING)

        @block.scalar
        def _(act):
            step = [0]

            def chain(ins):
                step[0] += 1
                ins.then_inc(sem("act_step"), 1)
                act.wait_ge(sem("act_step"), step[0])

            def high(n, slot, lap):
                act.wait_ge(landed[slot], lap * 16 + 16)
                if not isinstance(n, int) or n >= RING:
                    act.wait_ge(tile_used, n - (RING - 1))
                act.activation(w_hi[:, slot, :], w_raw[:, slot, :], ACT.Copy).then_inc(hi_ready, 1)

            def next_high(n):
                if n + RING < N_TILES:
                    high(n + RING, n % RING, (n + RING) // RING)

            def rstd_of_resid(k):
                if k == 0:
                    act.wait_ge(sem("x_in"), 16)
                for t in range(TT):
                    if k >= 1:
                        act.wait_ge(sem("resid_done"), TT * (k - 1) + t + 1)
                    act.activation(scaled[:, t, :], resid[:, t, :], ACT.Square,
                                   accum_out=stat[:, t:t + 1]).then_inc(sem("squares"), 1)
                for t in range(TT):
                    act.wait_ge(sem("mean"), TT * k + t + 1)
                    act.activation(stat[:, 8 + t:9 + t], stat[:, 4 + t:5 + t], ACT.Sqrt)\
                       .then_inc(sem("root"), 1)

            def norm(k):
                rstd_of_resid(k)
                for c in range(KC):
                    g = G_AT[["mix0", "ffn0", "mix1", "ffn1"][k]] + c
                    ready(act, ("xT", k, c))
                    act.activation(x_hi[:, c, :], PSb(("xT", k, c)), ACT.Copy,
                                   scale=gain[:, g:g + 1]).then_inc(sem("x_high"), 1)

            for n in range(RING):
                high(n, n, 0)
            act.wait_ge(sem("gain_in"), 16)
            for n in range(2):
                act.wait_ge(sem("angle"), n + 1)
                act.activation([sinT, cosT][n], tmp[:, n, :], ACT.Sin).then_inc(sem("sines"), 1)
            act.wait_ge(sem("pos_read"), 1)
            norm(0)
            for m in range(7):
                if m < 5:
                    ready(act, ("z", m))
                    free(act.activation(zT[:, m, :], PSb(("z", m)), ACT.Copy), ("z", m))
                next_high(BASE["z"] + m)
            for n in range(2):
                act.wait_ge(sem("latent_mean"), n + 1)
                act.activation(tmp[:, n, :], tmp[:, n, :], ACT.Sqrt).then_inc(sem("latent_root"), 1)
            for m in range(5):
                act.wait_ge(sem("latent"), m + 1)
                act.activation(x_hi[:, m, :], zT[:, m, :], ACT.Copy).then_inc(sem("latent_high"), 1)
            for m in range(16):
                if m < 8:
                    ready(act, ("q_up", m))
                    free(act.activation(qn[:, m, :], PSb(("q_up", m)), ACT.Copy), ("q_up", m))
                for b in range(3 * m, 3 * m + 3):
                    if b % 8 == 7:
                        next_high(BASE["q_up"] + b // 8)
            for m in range(8):
                ready(act, ("k_up", m))
                free(act.activation(kn[:, m, :], PSb(("k_up", m)), ACT.Copy), ("k_up", m))
                if m % 4 == 3:
                    next_high(BASE["k_up"] + m // 4)
            next_high(BASE["v_up"])
            next_high(BASE["v_up"] + 1)
            for n in range(8):
                ready(act, ("v_up", n))
                free(act.activation(vtok[:, n // 2, (n % 2) * 512:(n % 2) * 512 + 512],
                                    PSb(("v_up", n)), ACT.Copy), ("v_up", n))

            def exponent(n):
                w = (n % 4 + 1) * P
                act.wait_ge(sem("bias"), n + 1)
                free(act.activation(prob[:, n % 2, 0:w], PSb(("s", n))[:, 0:w], ACT.Exp,
                                    bias=stat[:, 12 + n % 2:13 + n % 2], scale=ATT_SCALE,
                                    accum_out=stat[:, 14 + n % 2:15 + n % 2]), ("s", n))

            for n in range(2):
                exponent(n)
            for n in range(4 * HEADS):
                h, qt = n // 4, n % 4
                ready(act, ("pT", n))
                if qt == 0 and h >= 2:
                    ready(act, ("o", h - 2))
                free(act.activation(pT[:, h % 2, 0:qt + 1, qt * P:(qt + 1) * P],
                                    PSb(("pT", n))[:, 0:(qt + 1) * P].rearrange("p (j q) -> p j q", q=P),
                                    ACT.Copy), ("pT", n))
                if n + 2 < 4 * HEADS:
                    exponent(n + 2)
                if n >= 6 and (n - 6) % 4 == 0 or n == 4 * HEADS - 1:
                    for hh in ([(n - 6) // 4] if n < 4 * HEADS - 1 else [HEADS - 1]):
                        ready(act, ("o", hh))
                        act.activation(x_hi[:, hh, :], PSb(("o", hh)), ACT.Copy).then_inc(sem("o_high"), 1)
            for n in range(8):
                next_high(BASE["mla_out"] + n)

            def experts(layer):
                bu, bv, bq = BASE[f"u{layer}"], BASE[f"v{layer}"], BASE[f"pq{layer}"]
                if layer == 0:
                    act.sem_inc(gelu_done, 4)
                    act.sem_inc(gate_moved, 2)
                norm(2 * layer + 1)
                for n in range(16):
                    ready(act, (f"pq{layer}", n))
                    if n >= 2:
                        ready(act, (f"sc{layer}", n - 2))
                    free(act.activation(qT[:, n % 2, :], PSb((f"pq{layer}", n)), ACT.Copy),
                         (f"pq{layer}", n))
                    next_high(bq + n)

                def gelu(i, j):
                    c = i * UNROLL + j
                    act.wait_ge(tile_used, c + (bu + 1))
                    if layer > 0 or not isinstance(i, int) or i > 0:
                        act.wait_ge(act_stored[j], (i + TURNS * layer) * 16)
                    act.activation(act_st[:, j, :], PS[:, j % 4, :], ACT.Gelu).then_inc(gelu_done, 1)
                    high(c + (bu + RING), (bu + j) % RING,
                         i * (UNROLL // RING) + (bu + j + RING) // RING)

                def move_gates(turn, q):
                    b, k = q // (HALF_TOK // 4), q % (HALF_TOK // 4)
                    act.wait_ge(gates_made, turn * (TOK // 4) + (q + 1 + SEQ // 4 * layer + 2))
                    if k == 0 and (layer > 0 or not isinstance(turn, int)):
                        act.wait_ge(gate_stored[b], (turn + (TURNS - ROUTED_TURN) * layer) * 16)
                    act.activation(
                        gate_st[:, b].rearrange("p g t f -> p t g f")[:, 4 * k:4 * k + 4],
                        PS[:, 4 + q % 2, :].rearrange("p (t g f) -> p t g f", t=4, f=GF),
                        ACT.Copy, scale=1.0 / GATE_UNIT).then_inc(gate_moved, 1)

                for j in range(UNROLL):
                    gelu(0, j)
                with act.Fori(1, ROUTED_TURN) as i:
                    for j in range(UNROLL):
                        gelu(i, j)
                act.wait_ge(sem("top_less_max"), TT * (layer + 1))
                act.activation(top, top, ACT.Exp).then_inc(sem("top_exp"), 1)

                def routed_turn(i):
                    for j in range(UNROLL):
                        gelu(i, j)
                        for q in range(j * TOK // 4 // UNROLL, (j + 1) * TOK // 4 // UNROLL):
                            move_gates(i - ROUTED_TURN, q)

                routed_turn(ROUTED_TURN)
                with act.Fori(ROUTED_TURN + 1, TURNS) as i:
                    routed_turn(i)

                def product_high(c, j):
                    act.wait_ge(sem("product_made"), c + (NKEYS * layer + 1))
                    act.wait_ge(tile_used, c + (bv - RING + 1))
                    act.activation(x_hi[:, j % RING, :], product[:, j % RING, :],
                                   ACT.Copy).then_inc(sem("product_high"), 1)

                act.wait_ge(tile_used, bv)
                for c in range(RING):
                    product_high(c, c)

                def v_turn(i, n):
                    for j in range(n):
                        high(i * UNROLL + (bv + j + RING), (bv + j) % RING,
                             i * (UNROLL // RING) + (bv + j + RING) // RING)
                        product_high(i * UNROLL + (j + RING), j)

                with act.Fori(0, TURNS - 1) as i:
                    v_turn(i, UNROLL)
                v_turn(TURNS - 1, RING)
                for c in range(NKEYS - RING, NKEYS):
                    next_high(bv + c)

            experts(0)

            norm(2)
            for n in range(8):
                ready(act, ("hg_q", n))
                free(act.activation(gq[:, n, :], PSb(("hg_q", n)), ACT.Silu), ("hg_q", n))
                next_high(BASE["hg_q"] + n)
            for n in range(8):
                ready(act, ("hg_f", n))
                ins = free(act.activation(gb[:, n, :], PSb(("hg_f", n)), ACT.Sigmoid), ("hg_f", n))
                next_high(BASE["hg_f"] + n)
            for n in range(8):
                ready(act, ("hg_g", n))
                free(act.activation(gg_[:, n, :], PSb(("hg_g", n)), ACT.Silu), ("hg_g", n))
                next_high(BASE["hg_g"] + n)
            act.wait_ge(sem("bound_less_max"), 1)
            act.activation(lbt[:, 0:2, :], lbt[:, 0:2, :], ACT.Exp).then_inc(sem("bound_exp"), 1)
            for h in range(HEADS):
                act.wait_ge(sem("forget"), h + 1)
                if h >= 2:
                    act.wait_ge(sem("cumulated"), h - 1)
                act.activation(diff[:, h % 2, :], gb[:, h, :], ACT.Ln).then_inc(sem("forget_log"), 1)
            for n in range(8):
                next_high(BASE["hg_i"] + n)
            for n in range(8):
                ready(act, ("hg_i", n))
                free(act.activation(vrec[:, n // 2, (n % 2) * 512:(n % 2) * 512 + 512],
                                    PSb(("hg_i", n)), ACT.Copy), ("hg_i", n))
            def head_out(h):
                ready(act, ("ho", h))
                free(act.activation(gq[:, h, :], PSb(("ho", h)), ACT.Copy), ("ho", h))

            for h in range(HEADS):
                act.wait_ge(sem("cumulated"), h + 1)
                if h >= 2:
                    was_freed(act, ("st", h - 2))
                    act.wait_ge(sem("q_decayed"), h - 1)
                act.activation(e_all[:, h % 2, :], gb[:, h, :], ACT.Exp).then_inc(sem("decay"), 1)
                for k in range(8):
                    n = 8 * h + k
                    act.wait_ge(sem("level_diff"), n + 1)
                    d = diff[:, n % 2, :]
                    if k == 0:
                        act.activation(d, d, ACT.Exp).then_inc(sem("level_exp"), 1)
                        continue
                    d4 = d.rearrange("p (b s m) -> p b s m", s=2, m=P >> k)
                    act.activation(d4[:, :, 0], d4[:, :, 0], ACT.Exp, scale=-1.0)
                    act.activation(d4[:, :, 1], d4[:, :, 1], ACT.Exp).then_inc(sem("level_exp"), 1)
                    if k == 2:
                        ready(act, ("kd", h))
                        free(act.activation(kdT.rearrange("p a b -> p (a b)"), PSb(("kd", h)), ACT.Copy),
                             ("kd", h))
                    if k == 3 and h >= 1:
                        head_out(h - 1)
            head_out(HEADS - 1)
            for h in range(HEADS):
                was_freed(act, ("hss", h))
                act.activation(gk[:, h, :], gk[:, h, :], ACT.Sqrt).then_inc(sem("head_root"), 1)
            for h in range(HEADS):
                act.wait_ge(sem("gated"), h + 1)
                act.activation(x_hi[:, h, :], gq[:, h, :], ACT.Copy).then_inc(sem("gated_high"), 1)
            for n in range(8):
                next_high(BASE["hg_out"] + n)

            experts(1)
            rstd_of_resid(4)

        @block.vector
        def _(dve):
            step = [0]

            def chain(ins):
                step[0] += 1
                ins.then_inc(sem("dve_step"), 1)
                dve.wait_ge(sem("dve_step"), step[0])

            def wide(ap, shape, at):
                return ap.unsqueeze(at).broadcast_to(shape)

            def mean_square(k, t):
                dve.wait_ge(sem("squares"), TT * k + t + 1)
                dve.tensor_scalar(stat[:, 4 + t:5 + t], stat[:, t:t + 1], 1.0 / DM, EPS, ALU.mult, ALU.add)\
                   .then_inc(sem("mean"), 1)

            def reciprocal_root(k, t):
                dve.wait_ge(sem("root"), TT * k + t + 1)
                chain(dve.reciprocal(stat[:, t:t + 1], stat[:, 8 + t:9 + t]))

            def norm(k):
                if k == 0:
                    dve.wait_ge(sem("x_in"), 16)
                for t in range(TT):
                    mean_square(k, t)
                for t in range(TT):
                    reciprocal_root(k, t)
                    ins = dve.tensor_scalar(scaled[:, t, :], resid[:, t, :], stat[:, t:t + 1], None, ALU.mult)
                    ins.then_inc(sem("scaled"), 1)
                for c in range(KC):
                    g = G_AT[["mix0", "ffn0", "mix1", "ffn1"][k]] + c
                    dve.wait_ge(sem("x_high"), KC * k + c + 1)
                    free(dve.scalar_tensor_tensor(x_lo[:, c, :], PSb(("xT", k, c)), gain[:, g:g + 1],
                                                  f32(x_hi[:, c, :]), ALU.mult, ALU.subtract),
                         ("xT", k, c))

            def add_to_resid(name, k):
                for n in range(8):
                    part = resid[:, n // 2, (n % 2) * 512:(n % 2) * 512 + 512]
                    ready(dve, (name, n))
                    free(dve.tensor_tensor(part, part, PSb((name, n)), ALU.add), (name, n))
                    if n % 2 == 1:
                        was_freed(dve, (name, n))
                        dve.sem_inc(sem("resid_done"), 1)

            dve.wait_ge(sem("pos_in"), 16)
            dve.wait_ge(sem("const_in"), 16)
            dve.wait_ge(sem("gain_in"), 16)
            angle, turns = tmp[:, 2, :], tmp[:, 3, :]
            dve.tensor_copy(turns, posi).then_inc(sem("pos_read"), 1)
            dve.wait_ge(sem("pos_read"), 1)
            chain(dve.tensor_scalar(angle, turns, const[:, C_INV:C_INV + 1], None, ALU.mult))
            for n in range(2):
                r = tmp[:, n, :]
                chain(dve.tensor_scalar(turns, angle, INV_2PI, 0.25 * n, ALU.mult, ALU.add))
                chain(dve.tensor_scalar(turns, turns, ROUNDER, None, ALU.add))
                chain(dve.tensor_scalar(turns, turns, ROUNDER, None, ALU.subtract))
                chain(dve.scalar_tensor_tensor(r, turns, -TWO_PI[0], angle, ALU.mult, ALU.add))
                chain(dve.scalar_tensor_tensor(r, turns, -TWO_PI[1], r, ALU.mult, ALU.add))
                chain(dve.scalar_tensor_tensor(r, turns, -TWO_PI[2], r, ALU.mult, ALU.add))
                if n == 1:
                    chain(dve.tensor_scalar(r, r, 0.5 * np.pi, None, ALU.add))
                dve.tensor_scalar(r, r, PI_BELOW, -PI_BELOW, ALU.min, ALU.max).then_inc(sem("angle"), 1)
            dve.wait_ge(sem("sines"), 2)
            chain(dve.tensor_scalar(sinT, sinT, const[:, C_SGN:C_SGN + 1], None, ALU.mult))

            norm(0)

            def rotate(dst, raw, swapped, key):
                if raw is not None:
                    chain(dve.tensor_tensor(dst, raw, cosT, ALU.mult))
                    return
                free(dve.tensor_tensor(tmp[:, 2, :], swapped, sinT, ALU.mult), key)
                was_freed(dve, key)
                chain(dve.tensor_tensor(dst, dst, tmp[:, 2, :], ALU.add))

            for m in range(5):
                was_freed(dve, ("z", m))
                dve.tensor_tensor(qn[:, m, :], zT[:, m, :], zT[:, m, :], ALU.mult)\
                   .then_inc(sem("latent_sq"), 1)
            ready(dve, ("z", 5))
            free(dve.tensor_tensor(kr, PSb(("z", 5)), cosT, ALU.mult), ("z", 5))
            was_freed(dve, ("z", 5))
            ready(dve, ("z", 6))
            rotate(kr, None, PSb(("z", 6)), ("z", 6))
            for n, width in enumerate((Q_LORA, KV_LORA)):
                ready(dve, ("zss", n))
                free(dve.tensor_scalar(tmp[:, n, :], PSb(("zss", n)), 1.0 / width, EPS, ALU.mult, ALU.add),
                     ("zss", n))
                was_freed(dve, ("zss", n))
                dve.sem_inc(sem("latent_mean"), 1)
            for n in range(2):
                dve.wait_ge(sem("latent_root"), n + 1)
                chain(dve.reciprocal(tmp[:, n, :], tmp[:, n, :]))
            for m in range(5):
                g = G_AT["q"] + m if m < QC else G_AT["kv"] + m - QC
                dve.scalar_tensor_tensor(zT[:, m, :], zT[:, m, :], gain[:, g:g + 1],
                                         tmp[:, 0 if m < QC else 1, :], ALU.mult, ALU.mult)\
                   .then_inc(sem("latent"), 1)
            for m in range(5):
                dve.wait_ge(sem("latent_high"), m + 1)
                dve.tensor_tensor(x_lo[:, m, :], zT[:, m, :], f32(x_hi[:, m, :]), ALU.subtract)\
                   .then_inc(sem("latent_low"), 1)
            for j in range(4):
                ready(dve, ("q_up", 8 + j))
                free(dve.tensor_tensor(qr[:, j, :], PSb(("q_up", 8 + j)), cosT, ALU.mult), ("q_up", 8 + j))
            was_freed(dve, ("q_up", 11))
            for j in range(4):
                ready(dve, ("q_up", 12 + j))
                rotate(qr[:, j, :], None, PSb(("q_up", 12 + j)), ("q_up", 12 + j))
            dve.sem_inc(sem("rotated"), 1)

            def row_max(n):
                qt = n % 4
                s = PSb(("s", n))
                ready(dve, ("s", n))
                if n >= 2:
                    was_freed(dve, ("s", n - 2))
                chain(dve.tensor_tensor(s[:, qt * P:(qt + 1) * P], s[:, qt * P:(qt + 1) * P], causal, ALU.add))
                chain(dve.tensor_reduce(stat[:, 4 + n % 2:5 + n % 2], s[:, 0:(qt + 1) * P], AX.X, ALU.max))
                dve.tensor_scalar(stat[:, 12 + n % 2:13 + n % 2], stat[:, 4 + n % 2:5 + n % 2],
                                  -ATT_SCALE, None, ALU.mult).then_inc(sem("bias"), 1)

            for n in range(2):
                row_max(n)
            for n in range(4 * HEADS):
                w = (n % 4 + 1) * P
                was_freed(dve, ("s", n))
                chain(dve.reciprocal(stat[:, 6 + n % 2:7 + n % 2], stat[:, 14 + n % 2:15 + n % 2]))
                dve.tensor_scalar(prob[:, n % 2, 0:w], prob[:, n % 2, 0:w], stat[:, 6 + n % 2:7 + n % 2],
                                  None, ALU.mult).then_inc(sem("prob"), 1)
                if n + 2 < 4 * HEADS:
                    row_max(n + 2)
                if n >= 7 and (n - 7) % 4 == 0:
                    h = (n - 7) // 4
                    dve.wait_ge(sem("o_high"), h + 1)
                    free(dve.tensor_tensor(x_lo[:, h, :], PSb(("o", h)), f32(x_hi[:, h, :]), ALU.subtract),
                         ("o", h))
            h = HEADS - 1
            dve.wait_ge(sem("o_high"), h + 1)
            free(dve.tensor_tensor(x_lo[:, h, :], PSb(("o", h)), f32(x_hi[:, h, :]), ALU.subtract), ("o", h))
            add_to_resid("mla_out", 1)

            def sixteen(values, places, source, groups):
                for half in range(2):
                    part = slice(8 * half, 8 * half + 8)
                    for g in range(groups):
                        ins = dve.max(values(g)[:, part], source(g))
                    chain(ins)
                    for g in range(groups):
                        ins = dve.max_index(places(g)[:, part], values(g)[:, part], source(g))
                    if half == 0:
                        for g in range(groups):
                            ins = dve.match_replace(source(g), values(g)[:, part], source(g), LOWEST)
                    chain(ins)

            def route(layer, t):
                sixteen(lambda g: val[:, g, :], lambda g: ixu[:, g, :], lambda g: scores[:, t, g, :], 16)
                chain(dve.tensor_copy(ixf, ixu))
                v4 = val.rearrange("p (h s) k -> p h s k", s=2)
                full = [P, HEADS, TOPK, TOPK]
                chain(dve.tensor_tensor(cand, wide(v4[:, :, 0], full, 3), wide(v4[:, :, 1], full, 2), ALU.add))
                sixteen(lambda g: top[:, t, g, :], lambda g: posu[:, g * TOPK:(g + 1) * TOPK],
                        lambda g: cand[:, g].rearrange("p a b -> p (a b)"), HEADS)
                chain(dve.tensor_scalar(halfu[:, 0, :], posu, 4, None, ALU.logical_shift_right))
                chain(dve.tensor_scalar(halfu[:, 1, :], posu, 15, None, ALU.bitwise_and))
                chain(dve.tensor_copy(halff, halfu))
                i4 = ixf.rearrange("p (h s) k -> p h s k", s=2)
                hot = cand.rearrange("p h a b -> p (h a) b")
                for s in range(2):
                    chain(dve.tensor_tensor(hot, wide(halff[:, s, :], [P, HK, TOPK], 2),
                                            wide(iota[:, 0:TOPK], [P, HK, TOPK], 1), ALU.is_equal))
                    chain(dve.tensor_tensor(picked.rearrange("p (h k) a -> p h k a", h=HEADS), cand,
                                            wide(i4[:, :, s], full, 2), ALU.mult))
                    chain(dve.tensor_reduce(ids[:, s, t, :], picked, AX.X, ALU.add))
                chain(dve.tensor_copy(gsum[:, 0:HEADS], top[:, t, :, 0]))
                dve.tensor_tensor(top[:, t], top[:, t], wide(gsum[:, 0:HEADS], [P, HEADS, TOPK], 2),
                                  ALU.subtract).then_inc(sem("top_less_max"), 1)

            def experts(layer):
                bv = BASE[f"v{layer}"]
                norm(2 * layer + 1)
                for n in range(16):
                    ready(dve, (f"sc{layer}", n))
                    free(dve.tensor_copy(scores[:, :, n, :], PSb((f"sc{layer}", n))
                                         .rearrange("p (t k) -> p t k", t=TT)), (f"sc{layer}", n))
                was_freed(dve, (f"sc{layer}", 15))
                for t in range(TT):
                    route(layer, t)
                dve.wait_ge(sem("top_less_max"), TT * (layer + 1))
                dve.sem_inc(sem("routed"), 1)
                dve.wait_ge(sem("top_exp"), layer + 1)
                flat = top.rearrange("p t h k -> p (t h) k")
                chain(dve.tensor_reduce(gsum, flat, AX.X, ALU.add))
                chain(dve.reciprocal(gsum, gsum))
                dve.tensor_tensor(flat, flat, wide(gsum, [P, TT * HEADS, TOPK], 2), ALU.mult)\
                   .then_inc(sem("gates"), 1)
                for n in range(2):
                    dve.wait_ge(sem("routeT_ps"), 3 * layer + n + 1)
                    chain(dve.tensor_copy(routeT[:, n, :], PS[:, 4 + n, :]))
                dve.wait_ge(sem("routeT_ps"), 3 * layer + 3)
                chain(dve.tensor_scalar(gate16, PS[:, 6, :], GATE_UNIT, None, ALU.mult))
                chain(dve.tensor_copy(routeT[:, 2, :], gate16))
                chain(dve.scalar_tensor_tensor(routeT[:, 3, :], PS[:, 6, :], GATE_UNIT, routeT[:, 2, :],
                                               ALU.mult, ALU.subtract))
                dve.sem_inc(sem("routeT"), 1)

                with dve.Fori(0, TURNS - ROUTED_TURN) as i:
                    dve.tensor_copy(window, routeT[:, :, bass.ds(i * TOK, TOK)]).then_inc(sem("window"), 1)
                    dve.wait_ge(sem("window"), i + ((TURNS - ROUTED_TURN) * layer + 1))
                    for k in range(TOK):
                        if k % 4 == 0:
                            dve.wait_ge(gates_made, i * (TOK // 4) + (k // 4 + 1 + SEQ // 4 * layer))
                        dve.tensor_scalar(onehot1[:, k % 8, :], iota16, window[:, 0, k:k + 1], None,
                                          ALU.is_equal)
                        for w in range(2):
                            ins = dve.tensor_scalar(onehot2[:, k % 8, w, :], iota16, window[:, 1, k:k + 1],
                                                    window[:, 2 + w, k:k + 1], ALU.is_equal, ALU.mult)
                        if k % 4 == 3:
                            ins.then_inc(onehots, 1)
                    dve.wait_ge(onehots, i * (TOK // 4) + (TOK // 4 + SEQ // 4 * layer))

                def make_product(i, j):
                    b = j // GF
                    dve.wait_ge(act_loaded[j], (i + (TURNS * layer + 1)) * 16)
                    if j % GF == 0:
                        dve.wait_ge(gate_loaded[b], (i + (TURNS * layer + 1)) * 16)
                    if not isinstance(i, int) or j >= RING:
                        dve.wait_ge(sem("product_low"), i * UNROLL + (j - RING + 1 + NKEYS * layer))
                    dve.tensor_tensor(product[:, j % RING, :], act_st[:, j, :], gate_ld[:, b, :, j % GF],
                                      ALU.mult).then_inc(sem("product_made"), 1)

                def product_low(c, j):
                    dve.wait_ge(sem("product_high"), c + (NKEYS * layer + 1))
                    dve.tensor_tensor(x_lo[:, j % RING, :], product[:, j % RING, :],
                                      f32(x_hi[:, j % RING, :]), ALU.subtract).then_inc(sem("product_low"), 1)

                make_product(0, 0)
                for j in range(1, UNROLL):
                    make_product(0, j)
                    product_low(j - 1, j - 1)
                with dve.Fori(1, TURNS) as i:
                    for j in range(UNROLL):
                        make_product(i, j)
                        product_low(i * UNROLL + (j - 1), (j - 1) % UNROLL)
                product_low(NKEYS - 1, UNROLL - 1)
                add_to_resid(f"v{layer}", 2 * layer + 2)

            experts(0)

            norm(2)
            dve.tensor_tensor(lbt[:, 2, :], gain[:, G_AT["lb0"]:G_AT["lb0"] + KC],
                              gain[:, G_AT["lb1"]:G_AT["lb1"] + KC], ALU.max).then_inc(sem("bound"), 1)
            dve.wait_ge(sem("bound"), 1)
            both = gain[:, G_AT["lb0"]:G_AT["lb0"] + 2 * KC].rearrange("p (s k) -> p s k", s=2)
            dve.tensor_tensor(lbt[:, 0:2, :], both, wide(lbt[:, 2, :], [P, 2, KC], 1), ALU.subtract)\
               .then_inc(sem("bound_less_max"), 1)
            dve.wait_ge(sem("bound_exp"), 1)
            chain(dve.tensor_tensor(lbt[:, 2, :], lbt[:, 0, :], lbt[:, 1, :], ALU.add))
            chain(dve.reciprocal(lbt[:, 2, :], lbt[:, 2, :]))
            chain(dve.tensor_tensor(lbt[:, 0:2, :], lbt[:, 0:2, :], wide(lbt[:, 2, :], [P, 2, KC], 1), ALU.mult))
            chain(dve.tensor_tensor(lbt[:, 1, :], lbt[:, 0, :], lbt[:, 1, :], ALU.add))
            chain(dve.tensor_tensor(lbt[:, 1, :], lbt[:, 1, :], lbt[:, 0, :], ALU.subtract))
            chain(dve.tensor_scalar(lbt[:, 3, :], lbt[:, 1, :], -1.0, 1.0, ALU.mult, ALU.add))
            for h in range(HEADS):
                was_freed(dve, ("hg_f", h))
                chain(dve.tensor_scalar(gb[:, h, :], gb[:, h, :], lbt[:, 3, h:h + 1], lbt[:, 1, h:h + 1],
                                        ALU.mult, ALU.add))
                chain(dve.tensor_scalar(gk[:, h, :], gb[:, h, :], -1.0, 1.0, ALU.mult, ALU.add))
                dve.tensor_scalar(gb[:, h, :], gb[:, h, :], SMALLEST_F, None, ALU.max)\
                   .then_inc(sem("forget"), 1)
            dve.wait_ge(sem("mask_in"), 16)
            for h in range(HEADS):
                dve.wait_ge(sem("forget_log"), h + 1)
                dve.tensor_tensor_scan(gb[:, h, :], keep, diff[:, h % 2, :], 0.0, ALU.mult, ALU.add)\
                   .then_inc(sem("cumulated"), 1)
            dve.wait_ge(sem("cumulated"), HEADS)

            def chunked(ap):
                return ap.rearrange("p (c t) -> p c t", t=P)

            def take_diff(n):
                h, k = divmod(n, 8)
                if n >= 2:
                    if (n - 2) % 8 == 0:
                        dve.wait_ge(sem("k_decayed"), (n - 2) // 8 + 1)
                    else:
                        dve.wait_ge(sem("level_x"), (n - 2) // 8 * LEVELS + (n - 2) % 8)
                d = diff[:, n % 2, :]
                if k == 0:
                    b4 = chunked(gb[:, h, :])
                    ins = dve.tensor_tensor(chunked(d), b4[:, :, P - 1:P].broadcast_to([P, TT, P]), b4,
                                            ALU.subtract)
                else:
                    m = P >> k
                    bb = gb[:, h, :].rearrange("p (b m) -> p b m", m=2 * m)
                    ins = dve.tensor_tensor(d.rearrange("p (b m) -> p b m", m=2 * m), bb,
                                            bb[:, :, m - 1:m].broadcast_to([P, SEQ // (2 * m), 2 * m]),
                                            ALU.subtract)
                ins.then_inc(sem("level_diff"), 1)

            def scale_level(n):
                h, k = divmod(n, 8)
                d = diff[:, n % 2, :]
                dve.wait_ge(sem("level_exp"), n + 1)
                if k == 0:
                    dve.tensor_tensor(kdec, gk[:, h, :], d, ALU.mult).then_inc(sem("k_decayed"), 1)
                    return
                x = h * LEVELS + k - 1
                if x >= 2:
                    ready(dve, ("a", (x - 2) // LEVELS, (x - 2) % LEVELS + 1))

                def halves(ap):
                    return ap.rearrange("p (b s m) -> p b s m", s=2, m=P >> k)

                for half, src in enumerate((gk, gq)):
                    ins = dve.tensor_tensor(halves(xx[:, x % 2, :])[:, :, half],
                                            halves(src[:, h, :])[:, :, half], halves(d)[:, :, half], ALU.mult)
                ins.then_inc(sem("level_x"), 1)

            def mask_level(n):
                h, p = divmod(n, 8)
                ready(dve, ("a", h, p))
                if n >= 2:
                    dve.wait_ge(sem("a_used"), n - 1)
                free(dve.tensor_tensor(chunked(a_sb[:, n % 2, :]), chunked(PSb(("a", h, p))),
                                       level_mask[(p - 1) % 8].unsqueeze(1).broadcast_to([P, TT, P]),
                                       ALU.mult), ("a", h, p))

            def states(h):
                ready(dve, ("st", h))
                st = PSb(("st", h))
                if h >= 1:
                    ready(dve, ("ho", h - 1))
                chain(dve.tensor_copy(state[:, 0, :], st[:, 0:P]))
                for c in (1, 2):
                    ins = dve.scalar_tensor_tensor(state[:, c, :], state[:, c - 1, :],
                                                   e_all[:, h % 2, c * P + P - 1:c * P + P],
                                                   st[:, c * P:(c + 1) * P], ALU.mult, ALU.add)
                    chain(ins) if c == 1 else free(ins, ("st", h))

            def head_square(h):
                was_freed(dve, ("ho", h))
                dve.tensor_tensor(gk[:, h, :], gq[:, h, :], gq[:, h, :], ALU.mult).then_inc(sem("head_sq"), 1)
                dve.wait_ge(sem("head_sq"), h + 1)
                was_freed(dve, ("hg_g", h))
                g = G_AT["out"] + h
                chain(dve.scalar_tensor_tensor(gq[:, h, :], gq[:, h, :], gain[:, g:g + 1], gg_[:, h, :],
                                               ALU.mult, ALU.mult))

            def head_mean(h):
                ready(dve, ("hss", h))
                free(dve.tensor_scalar(gk[:, h, :], PSb(("hss", h)), 1.0 / P, EPS, ALU.mult, ALU.add),
                     ("hss", h))

            def gated_low(h):
                dve.wait_ge(sem("gated_high"), h + 1)
                dve.tensor_tensor(x_lo[:, h, :], gq[:, h, :], f32(x_hi[:, h, :]), ALU.subtract)\
                   .then_inc(sem("gated_low"), 1)

            take_diff(0)
            for n in range(8 * HEADS):
                h, k = divmod(n, 8)
                if n + 1 < 8 * HEADS:
                    take_diff(n + 1)
                scale_level(n)
                if n >= 1:
                    mask_level(n - 1)
                if k == 1 and h >= 2:
                    head_mean(h - 2)
                if k == 4 and h >= 1:
                    head_square(h - 1)
                if k == 5:
                    dve.wait_ge(sem("decay"), h + 1)
                    states(h)
                if k == 7:
                    dve.wait_ge(sem("level_x"), (h + 1) * LEVELS)
                    dve.tensor_tensor(gq[:, h, :], gq[:, h, :], e_all[:, h % 2, :], ALU.mult)\
                       .then_inc(sem("q_decayed"), 1)
            mask_level(8 * HEADS - 1)
            head_mean(HEADS - 2)
            head_square(HEADS - 1)
            head_mean(HEADS - 1)
            for h in range(HEADS):
                dve.wait_ge(sem("head_root"), h + 1)
                chain(dve.reciprocal(gk[:, h, :], gk[:, h, :]))
                dve.tensor_tensor(gq[:, h, :], gq[:, h, :], gk[:, h, :], ALU.mult).then_inc(sem("gated"), 1)
                if h >= 1:
                    gated_low(h - 1)
            gated_low(HEADS - 1)
            add_to_resid("hg_out", 3)

            experts(1)

            dve.sem_inc(sem("final_free"), 1)
            for t in range(TT):
                mean_square(4, t)
            dve.wait_ge(sem("fgain_in"), 16)
            for t in range(TT):
                reciprocal_root(4, t)
                dve.scalar_tensor_tensor(final[:, t, :], resid[:, t, :], stat[:, t:t + 1], final_gain,
                                         ALU.mult, ALU.mult).then_inc(sem("final_made"), 1)

        @block.tensor
        def _(pe):
            def begin(key):
                if jobs.before[key] is not None:
                    was_freed(pe, jobs.before[key])

            def end(mm, key):
                mm.then_inc(sem(jobs.ready[key][0]), 1)

            def three(ps, wh, wl, xh, xl, start, stop):
                pe.matmul(ps, wh, xh, start=start, stop=False)
                pe.matmul(ps, wh, xl, start=False, stop=False)
                return pe.matmul(ps, wl, xh, start=False, stop=stop)

            def across(ps, slot):
                for kc in range(KC):
                    w = slice(kc * P, (kc + 1) * P)
                    mm = three(ps, w_hi[:, slot, w], w_lo[:, slot, w], x_hi[:, kc, :], x_lo[:, kc, :],
                               kc == 0, kc == KC - 1)
                return mm

            def projection(name, count):
                for m in range(count):
                    n = BASE[name] + m
                    pe.wait_ge(lo_ready, n + 1)
                    begin((name, m))
                    end(across(PSb((name, m)), n % RING), (name, m))

            def token_major(name, kcs, x_at, x_wait):
                for n in range(8):
                    begin((name, n))
                for kc in range(kcs):
                    tile = BASE[name] + kc
                    pe.wait_ge(lo_ready, tile + 1)
                    x_wait(kc)
                    rows(lambda n: PSb((name, n)), tile % RING, x_at + kc, kc == 0, kc == kcs - 1,
                         (lambda mm, n: end(mm, (name, n))) if kc == kcs - 1 else None)

            def rows(bank, slot, xc, start, stop, signal):
                for n in range(8):
                    t, w = slice(n // 2 * P, n // 2 * P + P), slice(n % 2 * 512, n % 2 * 512 + 512)
                    mm = three(bank(n), x_hi[:, xc, t], x_lo[:, xc, t], w_hi[:, slot, w],
                               w_lo[:, slot, w], start, stop)
                    if signal:
                        signal(mm, n)
                if not signal:
                    mm.then_inc(tile_used, 1)

            def norm(k):
                for t in range(TT):
                    pe.wait_ge(sem("scaled"), TT * k + t + 1)
                    for c in range(KC):
                        if t == 0:
                            begin(("xT", k, c))
                        mm = pe.transpose(PSb(("xT", k, c))[:, t * P:(t + 1) * P],
                                          scaled[:, t, c * P:(c + 1) * P], ident)
                        if t == TT - 1:
                            end(mm, ("xT", k, c))
                was_freed(pe, ("xT", k, KC - 1))

            pe.wait_ge(sem("const_in"), 16)
            norm(0)
            projection("z", 7)
            for n, ms in enumerate((range(0, QC), range(QC, QC + VC))):
                begin(("zss", n))
                for m in ms:
                    pe.wait_ge(sem("latent_sq"), m + 1)
                    mm = pe.matmul(PSb(("zss", n)), ones, qn[:, m, :], start=m == ms[0], stop=m == ms[-1])
                end(mm, ("zss", n))
            pe.wait_ge(sem("latent_low"), 5)

            def blocks_of(name, count, kcs, x_at):
                for m in range(count):
                    begin((name, m))
                    for kc in range(kcs):
                        b = kcs * m + kc
                        n = BASE[name] + b // 8
                        w = slice(b % 8 * P, b % 8 * P + P)
                        if b % 8 == 0:
                            pe.wait_ge(lo_ready, n + 1)
                        mm = three(PSb((name, m)), w_hi[:, n % RING, w], w_lo[:, n % RING, w],
                                   x_hi[:, x_at + kc, :], x_lo[:, x_at + kc, :], kc == 0, kc == kcs - 1)
                        if b % 8 == 7 and kc < kcs - 1:
                            mm.then_inc(tile_used, 1)
                    end(mm, (name, m))

            blocks_of("q_up", 16, QC, 0)
            blocks_of("k_up", 8, VC, QC)
            token_major("v_up", VC, QC, lambda kc: None)

            pe.wait_ge(sem("rotated"), 1)
            was_freed(pe, ("v_up", 7))
            for n in range(4 * HEADS + 2):
                if n < 4 * HEADS:
                    h, qt = n // 4, n % 4
                    w, q, part = (qt + 1) * P, slice(qt * P, qt * P + P), slice(h % 2 * 64, h % 2 * 64 + 64)
                    begin(("s", n))
                    s = PSb(("s", n))[:, 0:w]
                    pe.matmul(s, qn[:, h, q], kn[:, h, 0:w], start=True, stop=False)
                    end(pe.matmul(s, qr[part, h // 2, q], kr[part, 0:w], start=False, stop=True), ("s", n))
                if n >= 2:
                    k = n - 2
                    h, qt = k // 4, k % 4
                    pe.wait_ge(sem("prob"), k + 1)
                    begin(("pT", k))
                    for j in range(qt + 1):
                        mm = pe.transpose(PSb(("pT", k))[:, j * P:(j + 1) * P],
                                          prob[:, k % 2, j * P:(j + 1) * P], ident)
                    end(mm, ("pT", k))
                    if qt == 3:
                        begin(("o", h))
                        was_freed(pe, ("pT", k))
                        for j in range(TT):
                            mm = pe.matmul(PSb(("o", h))[:, j * P:SEQ], vtok[:, j, h * P:(h + 1) * P],
                                           pT[:, h % 2, j, j * P:SEQ], start=j == 0, stop=j == TT - 1)
                        end(mm, ("o", h))
            token_major("mla_out", 8, 0, lambda kc: was_freed(pe, ("o", kc)))

            def experts(layer):
                bu, bv, bq = BASE[f"u{layer}"], BASE[f"v{layer}"], BASE[f"pq{layer}"]
                if layer == 0:
                    pe.sem_inc(gates_made, 2)
                norm(2 * layer + 1)
                pe.wait_ge(sem("keys_in"), 16 * (layer + 1))
                for n in range(17):
                    if n < 16:
                        key = (f"pq{layer}", n)
                        pe.wait_ge(lo_ready, bq + n + 1)
                        begin(key)
                        end(across(PSb(key), (bq + n) % RING), key)
                    if n >= 1:
                        key = (f"sc{layer}", n - 1)
                        begin(key)
                        was_freed(pe, (f"pq{layer}", n - 1))
                        for t in range(TT):
                            mm = pe.matmul(PSb(key)[:, t * P:(t + 1) * P], qT[:, (n - 1) % 2, t * P:(t + 1) * P],
                                           keysT[:, n - 1, :], start=True, stop=True)
                        end(mm, key)
                was_freed(pe, (f"sc{layer}", 15))

                def u_tile(i, j):
                    c = i * UNROLL + j
                    pe.wait_ge(lo_ready, c + (bu + 1))
                    pe.wait_ge(gelu_done, c + (NKEYS * layer + 1))
                    across(PS[:, j % 4, :], (bu + j) % RING).then_inc(tile_used, 1)

                with pe.Fori(0, ROUTED_TURN) as i:
                    for j in range(UNROLL):
                        u_tile(i, j)
                for n in range(3):
                    pe.wait_ge(*((sem("routed"), layer + 1) if n < 2 else (sem("gates"), layer + 1)))
                    for t in range(TT):
                        src = ids[:, n, t, :] if n < 2 else top[:, t].rearrange("p h k -> p (h k)")
                        mm = pe.transpose(PS[:, 4 + n, t * P:(t + 1) * P], src, ident)
                    mm.then_inc(sem("routeT_ps"), 1)
                pe.wait_ge(sem("routeT"), layer + 1)

                def spread(turn, q):
                    pe.wait_ge(onehots, turn * (TOK // 4) + (q + 1 + SEQ // 4 * layer))
                    pe.wait_ge(gate_moved, turn * (TOK // 4) + (q + 1 + SEQ // 4 * layer))
                    for k in range(4):
                        s = (4 * q + k) % 8
                        for w in range(2):
                            mm = pe.matmul(PS[:, 4 + q % 2, k * P:(k + 1) * P], onehot1[:, s, :],
                                           onehot2[:, s, w, :], start=w == 0, stop=w == 1)
                    mm.then_inc(gates_made, 1)

                with pe.Fori(ROUTED_TURN, TURNS) as i:
                    for j in range(UNROLL):
                        u_tile(i, j)
                        for q in range(j * TOK // 4 // UNROLL, (j + 1) * TOK // 4 // UNROLL):
                            spread(i - ROUTED_TURN, q)
                pe.wait_ge(gelu_done, NKEYS * (layer + 1) + 4)
                pe.wait_ge(gate_moved, SEQ // 4 * (layer + 1) + 2)

                def v_tile(i, j, start=False, signal=None):
                    c = i * UNROLL + j
                    pe.wait_ge(lo_ready, c + (bv + 1))
                    pe.wait_ge(sem("product_low"), c + (NKEYS * layer + 1))
                    rows(lambda n: PSb((f"v{layer}", n)), (bv + j) % RING, j % RING, start,
                         signal is not None, signal)

                for j in range(UNROLL):
                    v_tile(0, j, start=j == 0)
                with pe.Fori(1, TURNS - 1) as i:
                    for j in range(UNROLL):
                        v_tile(i, j)
                for j in range(UNROLL):
                    v_tile(TURNS - 1, j, signal=(lambda mm, n: end(mm, (f"v{layer}", n)))
                           if j == UNROLL - 1 else None)

            experts(0)

            norm(2)
            projection("hg_q", 8)
            projection("hg_f", 8)
            projection("hg_g", 8)
            token_major("hg_i", 8, 0, lambda kc: None)
            was_freed(pe, ("hg_i", 7))

            for what, h, p in recurrence():
                if what == "kd":
                    begin(("kd", h))
                    pe.wait_ge(sem("k_decayed"), h + 1)
                    for c in range(TT):
                        mm = pe.transpose(PSb(("kd", h))[:, c * P:(c + 1) * P], kdec[:, c * P:(c + 1) * P],
                                          ident)
                    end(mm, ("kd", h))
                elif what == "a":
                    begin(("a", h, p))
                    x = h * LEVELS + p - 1
                    if p:
                        pe.wait_ge(sem("level_x"), x + 1)
                    for c in range(TT):
                        t = slice(c * P, (c + 1) * P)
                        lhs, rhs = (xx[:, x % 2, t],) * 2 if p else (gk[:, h, t], gq[:, h, t])
                        mm = pe.matmul(PSb(("a", h, p))[:, t], lhs, rhs, start=True, stop=True)
                    end(mm, ("a", h, p))
                elif what == "st":
                    begin(("st", h))
                    was_freed(pe, ("kd", h))
                    for c in range(TT - 1):
                        mm = pe.matmul(PSb(("st", h))[:, c * P:(c + 1) * P], kdT[:, c, :],
                                       vrec[:, c, h * P:(h + 1) * P], start=True, stop=True)
                    end(mm, ("st", h))
                elif what == "hss":
                    begin(("hss", h))
                    pe.wait_ge(sem("head_sq"), h + 1)
                    end(pe.matmul(PSb(("hss", h)), ones, gk[:, h, :], start=True, stop=True), ("hss", h))
                elif what == "values":
                    if p == 0:
                        begin(("ho", h))
                    was_freed(pe, ("a", h, p))
                    for c in range(TT):
                        t = slice(c * P, (c + 1) * P)
                        mm = pe.matmul(PSb(("ho", h))[:, t], vrec[:, c, h * P:(h + 1) * P],
                                       a_sb[:, (8 * h + p) % 2, t], start=p == 0 and c == 0, stop=False,
                                       skip_group_check=True)
                    mm.then_inc(sem("a_used"), 1)
                else:
                    was_freed(pe, ("st", h))
                    pe.wait_ge(sem("q_decayed"), h + 1)
                    for c in range(1, TT):
                        t = slice(c * P, (c + 1) * P)
                        mm = pe.matmul(PSb(("ho", h))[:, t], state[:, c - 1, :], gq[:, h, t], start=False,
                                       stop=c == TT - 1, skip_group_check=True)
                    end(mm, ("ho", h))
            token_major("hg_out", 8, 0, lambda kc: pe.wait_ge(sem("gated_low"), kc + 1))

            experts(1)


def _constants():
    c = np.zeros((P, C_COLS), np.float32)
    c[:, C_ID:C_ID + P] = np.eye(P)
    c[:, C_ONE:C_ONE + P] = 1.0
    c[:, C_IOTA:C_IOTA + P] = np.arange(P)
    c[:, C_CAUSAL:C_CAUSAL + P] = np.where(np.arange(P)[None, :] <= np.arange(P)[:, None], 0.0, -1e30)
    row = np.arange(P) % ROPE
    inv = np.float32(THETA) ** (-np.arange(0, ROPE, 2, dtype=np.float32) / np.float32(ROPE))
    c[:, C_INV] = inv[row % (ROPE // 2)]
    c[:, C_SGN] = np.where(row < ROPE // 2, -1.0, 1.0)
    m = np.zeros((P, M_COLS), np.float32)
    m[:, 0:SEQ] = (np.arange(SEQ) % P != 0)
    s, t = np.arange(P)[:, None], np.arange(P)[None, :]
    for lv in range(LEVELS):
        half = P >> (lv + 1)
        m[:, SEQ + P * lv:SEQ + P * (lv + 1)] = ((s // (2 * half) == t // (2 * half))
                                                 & (s // half % 2 == 0) & (t // half % 2 == 1))
    m[:, SEQ + P * LEVELS:M_IOTA] = (s == t)
    m[:, M_IOTA:] = np.arange(P)
    return c, (m.view(np.uint32) >> 16).astype(np.uint16)


def _across_tiles(w):
    n = w.shape[1]
    return w.reshape(KC, P, n // P, P).transpose(2, 1, 0, 3).reshape(n // P, P, KC * P)


def _block_tiles(w):
    k, n = w.shape
    b = w.reshape(k // P, P, n // P, P).transpose(2, 0, 1, 3).reshape(-1, 8, P, P)
    return b.transpose(0, 2, 1, 3).reshape(-1, P, 8 * P)


def _columns(g):
    return g.reshape(-1, P).T


def kernel(**inputs):
    import concourse.bacc as _bacc
    from concourse import mybir as _mybir
    from concourse.bass_utils import run_bass_kernel_spmd as _run

    a = {k: np.asarray(v) for k, v in inputs.items()}
    cat = np.concatenate
    w_in = a["mla_w_in"][0]
    r = w_in[:, Q_LORA + KV_LORA:]
    swap = cat([r[:, ROPE // 2:], r[:, :ROPE // 2]], 1)
    z = cat([w_in[:, :Q_LORA + KV_LORA], r, r, swap, swap], 1)
    q_up = a["mla_w_q_up"][0].reshape(Q_LORA, HEADS, NOPE + ROPE)
    qr = q_up[:, :, NOPE:]
    qs = cat([qr[:, :, ROPE // 2:], qr[:, :, :ROPE // 2]], 2)
    q_all = cat([q_up[:, :, :NOPE].reshape(Q_LORA, -1), qr.reshape(Q_LORA, -1), qs.reshape(Q_LORA, -1)], 1)
    kv_up = a["mla_w_kv_up"][0].reshape(KV_LORA, HEADS, 2 * P)
    mla_t = cat([_across_tiles(z), _block_tiles(q_all), _block_tiles(kv_up[:, :, :P].reshape(KV_LORA, -1)),
                 kv_up[:, :, P:].reshape(VC, P, DM), a["mla_w_out"][0].reshape(8, P, DM)], 0)
    hg = a["hg_w_in"][0]
    hg_t = cat([_across_tiles(hg[:, :2 * DM]), _across_tiles(hg[:, 3 * DM:]),
                hg[:, 2 * DM:3 * DM].reshape(8, P, DM), a["hg_w_out"][0].reshape(8, P, DM)], 0)
    pq_t = np.stack([_across_tiles(w) for w in a["peer_w_q"]])
    keys = a["peer_sub_keys"].reshape(2, 16, NKEYS, P).transpose(0, 3, 1, 2)
    u_t = a["peer_u"].reshape(2, NKEYS, NKEYS, KC, P).transpose(0, 2, 4, 3, 1).reshape(2, NKEYS, P, DM)
    v_t = a["peer_v"].reshape(2, NKEYS, NKEYS, DM).transpose(0, 2, 1, 3)
    gains = cat([_columns(g) for g in (a["ln_mix"][0], a["ln_ffn"][0], a["ln_mix"][1], a["ln_ffn"][1],
                                       a["mla_q_norm"][0], a["mla_kv_norm"][0], a["hg_out_norm"][0],
                                       a["hg_lb"][0], a["hg_lb"][1])], 1)
    consts, masks = _constants()
    arrays = {
        "x": a["x"][0], "pos": a["positions"], "consts": consts, "masks": masks, "gains": gains,
        "fgain": a["ln_final"][None], "mla_t": mla_t, "hg_t": hg_t, "pq_t": pq_t, "keys_t": keys,
        "u_t": u_t, "v_t": v_t,
    }
    arrays = {f"in_{k}": np.ascontiguousarray(v) for k, v in arrays.items()}
    nc = _bacc.Bacc("TRN2", target_bir_lowering=False, num_devices=1)
    args = [nc.dram_tensor(k, v.shape, _mybir.dt.from_np(v.dtype), kind="ExternalInput").ap()
            for k, v in arrays.items()]
    args.append(nc.dram_tensor("out_0", (SEQ, DM), _mybir.dt.float32, kind="ExternalOutput").ap())
    model(nc, *args)
    got = _run(nc, [arrays], core_ids=[0]).results[0]["out_0"]
    return got.reshape(1, SEQ, DM)
```

```python
from contextlib import ExitStack

import numpy as np

import concourse.bass as bass
from concourse import mybir

ALU = mybir.AluOpType
ACT = mybir.ActivationFunctionType
AX = mybir.AxisListType
F32 = mybir.dt.float32
F32R = mybir.dt.float32r
BF16 = mybir.dt.bfloat16
F16 = mybir.dt.float16
I32 = mybir.dt.int32
U32 = mybir.dt.uint32

P = 128
SEQ, DM = 512, 1024
TT = SEQ // P
KC = DM // P
HEADS = 8
EPS = 1e-6
Q_LORA, KV_LORA, NOPE, ROPE = 384, 256, 128, 64
QC, VC = Q_LORA // P, KV_LORA // P
ATT_SCALE = float(NOPE + ROPE) ** -0.5
THETA = 10000.0
NKEYS, TOPK = 128, 16
HK = HEADS * TOPK
AHEAD = 3
LEVELS = 7
LOWEST = -3.0e38
SMALLEST_F = 2.0 ** -63
INV_2PI = 1.0 / (2.0 * np.pi)
ROUNDER = 12582912.0
TWO_PI = [6.28125, 0.0019350051879882812]
TWO_PI.append(2.0 * np.pi - TWO_PI[0] - TWO_PI[1])
PI_BELOW = 3.1415925

RING = 4
UNROLL = 8
TURNS = NKEYS // UNROLL
ROUTED_TURN = TURNS // 2
TOK = SEQ // (TURNS - ROUTED_TURN)
HALF_TOK = TOK // 2
QUADS = TOK // 4
GF = 4
GG = NKEYS // GF
H_SLOTS = UNROLL

STREAM = [("z", 7), ("q_up", 6), ("k_up", 2), ("v_up", 2), ("mla_out", 8),
          ("pq0", 16), ("u0", NKEYS), ("v0", NKEYS),
          ("hg_q", 8), ("hg_f", 8), ("hg_g", 8), ("hg_i", 8), ("hg_out", 8),
          ("pq1", 16), ("u1", NKEYS), ("v1", NKEYS)]
BASE, N_TILES = {}, 0
for _name, _n in STREAM:
    BASE[_name] = N_TILES
    N_TILES += _n

C_ID, C_ONE, C_IOTA, C_CAUSAL, C_INV, C_SGN, C_COLS = 0, 128, 256, 384, 512, 513, 514
G_NAMES = [("mix0", KC), ("ffn0", KC), ("mix1", KC), ("ffn1", KC), ("q", QC), ("kv", VC), ("out", KC),
           ("lb0", KC), ("lb1", KC)]
G_AT, G_COLS = {}, 0
for _name, _n in G_NAMES:
    G_AT[_name] = G_COLS
    G_COLS += _n

ARENA = 26112
M_LEVEL, M_IOTA, M_COLS = SEQ, SEQ + 8 * P, SEQ + 9 * P
GATE_UNIT = 4096.0


def quads_before(j):
    return range(QUADS * j // UNROLL, QUADS * (j + 1) // UNROLL)


class Banks:

    def __init__(self):
        self.bank, self.before, self.ready, self.frees = {}, {}, {}, {}
        self.signals = 0
        self.count = {"act": 0, "dve": 0, "exp": 0, "state": 0, "kd": 0, "sum": 0}
        self.turn, self.last = {}, {}

    def add(self, key, frees, tile=None, banks=tuple(range(8))):
        n = self.turn.get(banks, 0)
        self.turn[banks] = n + 1
        bank = self.bank[key] = banks[n % len(banks)]
        self.before[key] = self.last.get(bank)
        self.last[bank] = key
        if tile is None:
            self.signals += 1
            self.ready[key] = ("ps_ready", self.signals)
        else:
            self.ready[key] = ("tile_used", tile + 1)
        self.count[frees] += 1
        self.frees[key] = (frees, self.count[frees])


def recurrence():
    for n in range(8 * HEADS + 2):
        h, p = divmod(n, 8)
        if n < 8 * HEADS:
            if p == 1:
                yield "kd", h, 0
            yield "a", h, p
            if p == 2:
                yield "st", h, 0
        if n >= 2:
            yield ("values", *divmod(n - 2, 8))
            if (n - 2) % 8 == 7:
                yield "ho", (n - 2) // 8, 0
        if n % 8 == 0 and n >= 16:
            yield "hss", n // 8 - 2, 0
    yield "hss", HEADS - 1, 0


def plan():
    b = Banks()

    def norm(k):
        for c in range(KC):
            b.add(("xT", k, c), "dve")

    def eight(name, last_tile, frees):
        for n in range(8):
            b.add((name, n), frees, last_tile if n == 7 else None)

    norm(0)
    for m in range(7):
        if m == 6:
            b.add(("zss", 0), "dve")
            b.add(("zss", 1), "dve")
        b.add(("z", m), "dve" if m >= 5 else "act", BASE["z"] + m)
    for m in range(16):
        end = 3 * m + 2
        b.add(("q_up", m), "act" if m < 8 else "dve", BASE["q_up"] + end // 8 if end % 8 == 7 else None)
    for m in range(8):
        end = 2 * m + 1
        b.add(("k_up", m), "act", BASE["k_up"] + end // 8 if end % 8 == 7 else None)
    eight("v_up", BASE["v_up"] + VC - 1, "act")
    for n in range(4 * HEADS + AHEAD + 1):
        if n < 4 * HEADS:
            b.add(("s", n), "exp", None, (0, 1, 2, 3))
        if AHEAD <= n < 4 * HEADS + AHEAD:
            b.add(("pT", n - AHEAD), "act", None, (4, 5))
        if n > AHEAD and (n - AHEAD) % 4 == 0:
            b.add(("o", (n - AHEAD) // 4 - 1), "dve", None, (6, 7))
    eight("mla_out", BASE["mla_out"] + 7, "dve")

    def peer(layer):
        norm(2 * layer + 1)
        for n in range(17):
            if n < 16:
                b.add((f"pq{layer}", n), "act", BASE[f"pq{layer}"] + n)
            if n >= 1:
                b.add((f"sc{layer}", n - 1), "dve")
        eight(f"v{layer}", BASE[f"v{layer}"] + NKEYS - 1, "dve")

    peer(0)
    norm(2)
    for n in range(8):
        b.add(("hg_q", n), "act", BASE["hg_q"] + n)
    for n in range(8):
        b.add(("hg_f", n), "act", BASE["hg_f"] + n)
    for n in range(8):
        b.add(("hg_g", n), "act", BASE["hg_g"] + n)
    eight("hg_i", BASE["hg_i"] + 7, "act")
    for what, h, p in recurrence():
        if what == "a":
            b.add(("a", h, p), "dve", None, (0, 1, 2, 3))
        elif what != "values":
            b.add((what, h), *{"kd": ("kd", None, (4,)), "st": ("state", None, (5,)),
                               "ho": ("act", None, (6, 7)), "hss": ("sum", None, (5,))}[what])
    eight("hg_out", BASE["hg_out"] + 7, "dve")
    peer(1)
    return b


def model(nc, x, pos, consts, masks, gains, fgain, mla_t, hg_t, pq_t, keys_t, u_t, v_t, out):
    jobs = plan()
    ctx = ExitStack()
    with ctx:
        def sb(name, shape, dt=F32):
            return ctx.enter_context(nc.sbuf_tensor(name, shape, dt))

        sems = {}

        def sem(name):
            if name not in sems:
                sems[name] = ctx.enter_context(nc.semaphore(name))
            return sems[name]

        acts_dram = nc.dram_tensor("acts_dram", [NKEYS, P, SEQ], F32, kind="Internal").ap()
        gates_dram = nc.dram_tensor("gates_dram", [GG, P, SEQ, GF], F32, kind="Internal").ap()

        PS = ctx.enter_context(nc.psum_tensor("PS", [P, 8, 512], F32))
        w_raw = sb("w_raw", [P, RING, 1024])
        w_hi = sb("w_hi", [P, RING, 1024], F32R)
        w_lo = sb("w_lo", [P, RING, 1024], F32R)
        x_hi = sb("x_hi", [P, KC, SEQ], F32R)
        x_lo = sb("x_lo", [P, KC, SEQ], F32R)
        resid = sb("resid", [P, TT, DM])
        const = sb("const", [P, C_COLS])
        mask_bits = sb("mask_bits", [P, M_COLS], mybir.dt.uint16)
        mask = mask_bits[:, :].bitcast(BF16)
        gain = sb("gain", [P, G_COLS])
        stat = sb("stat", [P, 16])
        arena = sb("arena", [P, ARENA])

        row_top, row_rec, row_bias, row_sum = (
            [stat[:, AHEAD * n + k:AHEAD * n + k + 1] for k in range(AHEAD)] for n in range(4))
        ident = const[:, C_ID:C_ID + P]
        ones = const[:, C_ONE:C_ONE + P]
        iota = const[:, C_IOTA:C_IOTA + P]
        causal = const[:, C_CAUSAL:C_CAUSAL + P]
        keep = mask[:, 0:SEQ]
        iota16 = mask[:, M_IOTA:M_IOTA + P]
        level_mask = [mask[:, SEQ + P * n:SEQ + P * (n + 1)] for n in range(8)]

        def f32(ap):
            return ap.bitcast(F32)

        def cut(offset, *shape):
            n = int(np.prod(shape))
            ap = arena[:, offset:offset + n]
            if len(shape) == 1:
                return ap
            names = "abcd"[:len(shape)]
            return ap.rearrange(f"p ({' '.join(names)}) -> p {' '.join(names)}", **dict(zip(names, shape)))

        zT = cut(0, 7, SEQ)
        cosT, sinT = cut(3584, SEQ), cut(4096, SEQ)
        tmp = cut(4608, 4, SEQ)
        qn, kn = cut(6656, HEADS, SEQ), cut(10752, HEADS, SEQ)
        qr, kr = cut(14848, 4, SEQ), cut(16896, SEQ)
        vtok = cut(17408, TT, DM)
        pT = cut(21504, 2, TT, SEQ)
        prob = cut(0, AHEAD, SEQ)
        posi = tmp[:, 1, :].bitcast(I32)
        scaled = cut(21504, TT, DM)
        act_st = cut(0, H_SLOTS, SEQ)
        gate_st = cut(4096, 2, GG, HALF_TOK, GF)
        gate_ld = cut(4096, 2, SEQ, GF)
        scores = cut(4096, TT, 16, NKEYS)
        val = cut(12288, 16, TOPK)
        ixu = cut(12544, 16, TOPK).bitcast(U32)
        ixf = cut(12800, 16, TOPK)
        top = cut(13056, TT, HEADS, TOPK)
        posu = cut(13568, HK).bitcast(U32)
        halfu = cut(13696, 2, HK).bitcast(U32)
        halff = cut(13952, 2, HK)
        ids = cut(14208, 2, TT, HK)
        gsum = cut(15232, 32)
        cand = cut(15360, HEADS, TOPK, TOPK)
        picked = cut(17408, HK, TOPK)
        onehot1 = cut(15360, 512).bitcast(F16).rearrange("p (s k) -> p s k", s=8)
        onehot2 = cut(15872, 1024).bitcast(F16).rearrange("p (s w k) -> p s w k", s=8, w=2)
        gate16 = cut(17408, SEQ // 2).bitcast(F16)
        routeT = cut(19456, 4, SEQ)
        window = cut(21504, 4, TOK)
        qT = cut(17408, 2, SEQ)
        keysT = cut(0, 16, NKEYS)
        product = cut(21504, RING, SEQ)
        gq, gk, gb, gg_, gv = (cut(4096 * n, HEADS, SEQ) for n in range(5))
        vrec = gv.rearrange("p a b -> p (a b)").rearrange("p (t d) -> p t d", t=TT)
        R0 = 20480
        e_all, diff, xx = cut(R0, 2, SEQ), cut(R0 + 1024, 2, SEQ), cut(R0 + 2048, 2, SEQ)
        kdec, kdT = cut(R0 + 3072, SEQ), cut(R0 + 3584, TT, P)
        a_sb = cut(R0 + 4096, 2, SEQ)
        state = cut(R0 + 5120, 3, P)
        lbt = cut(R0 + 5504, 4, KC)
        final_gain = cut(0, DM)
        final = cut(1024, TT, DM)

        ps_ready, tile_used = sem("ps_ready"), sem("tile_used")
        freed = {who: sem(f"{who}_freed") for who in ("act", "dve", "exp", "state", "kd", "sum")}
        hi_ready, lo_ready = sem("hi_ready"), sem("lo_ready")
        landed = [sem(f"landed{n}") for n in range(RING)]
        x_in = [sem(f"x_in{t}") for t in range(TT)]
        act_stored = [sem(f"act_stored{n}") for n in range(H_SLOTS)]
        act_loaded = [sem(f"act_loaded{n}") for n in range(H_SLOTS)]
        gate_stored = [sem(f"gate_stored{n}") for n in range(2)]
        gate_loaded = [sem(f"gate_loaded{n}") for n in range(2)]
        gelu_done = sem("gelu_done")
        gate_moved = sem("gate_moved")
        gates_made = sem("gates_made")
        onehots = sem("onehots")

        def chunked(ap):
            return ap.rearrange("p (c t) -> p c t", t=P)

        def PSb(key):
            return PS[:, jobs.bank[key], :]

        def ready(eng, key):
            name, count = jobs.ready[key]
            eng.wait_ge(sem(name), count)

        def free(ins, key):
            return ins.then_inc(freed[jobs.frees[key][0]], 1)

        def was_freed(eng, key):
            frees, count = jobs.frees[key]
            eng.wait_ge(freed[frees], count)

        blocks = {
            "z": mla_t, "pq0": pq_t[0], "u0": u_t[0], "v0": v_t[0], "hg_q": hg_t, "pq1": pq_t[1],
            "u1": u_t[1], "v1": v_t[1],
        }

        block = ctx.enter_context(nc.Block())

        @block.sync
        def _(sp):
            def load_tile(n, src, slot):
                if not isinstance(n, int) or n >= RING:
                    sp.wait_ge(lo_ready, n - (RING - 1))
                sp.dma_start(w_raw[:, slot, :], src).then_inc(landed[slot], 16)

            def load_range(name, count, first=0):
                tiles = blocks[name]
                for k in range(first, first + count):
                    load_tile(BASE[name] + k, tiles[k], (BASE[name] + k) % RING)

            for t in range(TT):
                sp.dma_start(resid[:, t, :], x[t * P:(t + 1) * P, :]).then_inc(x_in[t], 16)
            sp.dma_start(const[:, :], consts).then_inc(sem("const_in"), 16)
            sp.dma_start(gain[:, :], gains).then_inc(sem("gain_in"), 16)
            load_range("z", 2)
            sp.dma_start(posi, pos.partition_broadcast(P)).then_inc(sem("pos_in"), 16)
            load_range("z", 23, 2)
            sp.dma_start(mask_bits[:, :], masks).then_inc(sem("mask_in"), 16)

            def experts(layer):
                u, v = blocks[f"u{layer}"], blocks[f"v{layer}"]
                bu, bv = BASE[f"u{layer}"], BASE[f"v{layer}"]

                load_range(f"pq{layer}", RING)
                was_freed(sp, ("mla_out", 7) if layer == 0 else ("hg_out", 7))
                sp.dma_start(keysT, keys_t[layer]).then_inc(sem("keys_in"), 16)
                load_range(f"pq{layer}", 16 - RING, RING)

                def store_act(c, j):
                    sp.wait_ge(gelu_done, c + (NKEYS * layer + 4 + 1))
                    sp.dma_start(acts_dram[bass.ds(c, 1)].rearrange("a p n -> (a p) n"),
                                 act_st[:, j, :]).then_inc(act_stored[j], 16)

                def store_gates(turn, b):
                    groups = HALF_TOK // 4
                    sp.wait_ge(gate_moved, turn * (2 * groups) + (b + 1) * groups + SEQ // 4 * layer + 2)
                    sp.dma_start(
                        gates_dram[:, :, bass.ds(turn * TOK + b * HALF_TOK, HALF_TOK), :]
                        .rearrange("g p t f -> p g (t f)"),
                        gate_st[:, b].rearrange("p g t f -> p g (t f)")).then_inc(gate_stored[b], 16)

                def u_turn(i, acts, gates):
                    for j in range(UNROLL):
                        load_tile(i * UNROLL + (bu + j), u[bass.ds(i * UNROLL + j, 1)]
                                  .rearrange("a p n -> (a p) n"), (bu + j) % RING)
                        if acts:
                            store_act(i * UNROLL + (j - UNROLL), j)
                        if gates and j in (UNROLL - 3, UNROLL - 1):
                            store_gates(i - (ROUTED_TURN + 1), 0 if j == UNROLL - 3 else 1)

                u_turn(0, False, False)
                with sp.Fori(1, ROUTED_TURN + 1) as i:
                    u_turn(i, True, False)
                with sp.Fori(ROUTED_TURN + 1, TURNS) as i:
                    u_turn(i, True, True)

                def load_v(c, j):
                    load_tile(c + bv, v[bass.ds(c, 1)].rearrange("a p n -> (a p) n"), (bv + j) % RING)

                for j in range(RING):
                    load_v(j, j)
                last = TURNS - ROUTED_TURN - 1
                for j in range(UNROLL):
                    if j in (UNROLL - 3, UNROLL - 1):
                        store_gates(last, 0 if j == UNROLL - 3 else 1)
                    store_act(NKEYS - UNROLL + j, j)

                def load_act(i, j):
                    sp.dma_start(act_st[:, j, :], acts_dram[bass.ds(i * UNROLL + j, 1)]
                                 .rearrange("a p n -> (a p) n")).then_inc(act_loaded[j], 16)

                def load_gate(i, b):
                    sp.dma_start(gate_ld[:, b].rearrange("p t f -> p (t f)"),
                                 gates_dram[bass.ds(i * 2 + b, 1)]
                                 .rearrange("a p t f -> (a p) (t f)")).then_inc(gate_loaded[b], 16)

                def v_turn(i):
                    for j in range(UNROLL):
                        load_v(i * UNROLL + j, j)
                        if j % GF == 0:
                            sp.wait_ge(sem("product_made"), i * UNROLL + (j - GF + NKEYS * layer))
                            load_gate(i, j // GF)
                        sp.wait_ge(sem("product_made"), i * UNROLL + (j - UNROLL + 1 + NKEYS * layer))
                        load_act(i, j)

                for j in range(UNROLL):
                    if j == GF:
                        for b in range(2):
                            sp.wait_ge(gate_stored[b], 16 * (TURNS - ROUTED_TURN) * (layer + 1))
                        for b in range(2):
                            load_gate(0, b)
                    sp.wait_ge(act_stored[j], 16 * TURNS * (layer + 1))
                    load_act(0, j)
                for j in range(RING, UNROLL):
                    load_v(j, j)
                with sp.Fori(1, TURNS) as i:
                    v_turn(i)

            experts(0)
            load_range("hg_q", 40)
            experts(1)
            sp.wait_ge(sem("final_free"), 1)
            sp.dma_start(final_gain, fgain.partition_broadcast(P)).then_inc(sem("fgain_in"), 16)
            for t in range(TT):
                sp.wait_ge(sem("final_made"), t + 1)
                sp.dma_start(out[t * P:(t + 1) * P, :], final[:, t, :]).then_inc(sem("out_done"), 16)
            sp.wait_ge(sem("out_done"), 16 * TT)

        @block.gpsimd
        def _(pool):
            def low(n, slot):
                pool.wait_ge(hi_ready, n + 1)
                pool.tensor_tensor(w_lo[:, slot, :], w_raw[:, slot, :], f32(w_hi[:, slot, :]),
                                   ALU.subtract).then_inc(lo_ready, 1)

            def take_diff(n):
                h, k = divmod(n, 8)
                if n >= 2:
                    if (n - 2) % 8 == 0:
                        pool.wait_ge(sem("k_decayed"), (n - 2) // 8 + 1)
                    else:
                        pool.wait_ge(sem("level_x"), (n - 2) // 8 * LEVELS + (n - 2) % 8)
                d = diff[:, n % 2, :]
                if k == 0:
                    b4 = chunked(gb[:, h, :])
                    ins = pool.tensor_tensor(chunked(d), b4[:, :, P - 1:P].broadcast_to([P, TT, P]), b4,
                                             ALU.subtract)
                else:
                    m = P >> k
                    bb = gb[:, h, :].rearrange("p (b m) -> p b m", m=2 * m)
                    ins = pool.tensor_tensor(d.rearrange("p (b m) -> p b m", m=2 * m), bb,
                                             bb[:, :, m - 1:m].broadcast_to([P, SEQ // (2 * m), 2 * m]),
                                             ALU.subtract)
                ins.then_inc(sem("level_diff"), 1)

            turns = (BASE["hg_out"] + RING - 1) // RING
            with pool.Fori(0, turns) as i:
                for j in range(RING):
                    low(i * RING + j, j)
            pool.wait_ge(sem("cumulated"), HEADS)
            for n in range(2):
                take_diff(n)
            for n in range(turns * RING, BASE["hg_out"] + RING):
                low(n, n % RING)
            for n in range(2, 8 * HEADS):
                take_diff(n)
            for n in range(BASE["hg_out"] + RING, (turns + 2) * RING):
                low(n, n % RING)
            with pool.Fori(turns + 2, N_TILES // RING) as i:
                for j in range(RING):
                    low(i * RING + j, j)
            for n in range(N_TILES // RING * RING, N_TILES):
                low(n, n % RING)

        @block.scalar
        def _(act):
            step = [0]

            def chain(ins):
                step[0] += 1
                ins.then_inc(sem("act_step"), 1)
                act.wait_ge(sem("act_step"), step[0])

            def high(n, slot, lap):
                act.wait_ge(landed[slot], lap * 16 + 16)
                if not isinstance(n, int) or n >= RING:
                    act.wait_ge(tile_used, n - (RING - 1))
                act.activation(w_hi[:, slot, :], w_raw[:, slot, :], ACT.Copy).then_inc(hi_ready, 1)

            def next_high(n):
                if n + RING < N_TILES:
                    high(n + RING, n % RING, (n + RING) // RING)

            def rstd_of_resid(k):
                for t in range(TT + 1):
                    if t < TT:
                        if k >= 1:
                            act.wait_ge(sem("resid_done"), TT * (k - 1) + t + 1)
                        else:
                            act.wait_ge(x_in[t], 16)
                        act.activation(scaled[:, t, :], resid[:, t, :], ACT.Square,
                                       accum_out=stat[:, t:t + 1]).then_inc(sem("squares"), 1)
                    if t >= 1:
                        act.wait_ge(sem("mean"), TT * k + t)
                        act.activation(stat[:, 7 + t:8 + t], stat[:, 3 + t:4 + t], ACT.Sqrt)\
                           .then_inc(sem("root"), 1)

            def norm(k, last_tile=None):
                rstd_of_resid(k)
                if k == 0:
                    for n in range(RING):
                        high(n, n, 0)
                    act.wait_ge(sem("gain_in"), 16)
                else:
                    next_high(last_tile)
                for c in range(KC):
                    g = G_AT[["mix0", "ffn0", "mix1", "ffn1"][k]] + c
                    ready(act, ("xT", k, c))
                    act.activation(x_hi[:, c, :], PSb(("xT", k, c)), ACT.Copy,
                                   scale=gain[:, g:g + 1]).then_inc(sem("x_high"), 1)

            norm(0)
            for n in range(2):
                act.wait_ge(sem("angle"), n + 1)
                act.activation([sinT, cosT][n], tmp[:, n, :], ACT.Sin).then_inc(sem("sines"), 1)
            for m in range(7):
                if m < 5:
                    ready(act, ("z", m))
                    free(act.activation(zT[:, m, :], PSb(("z", m)), ACT.Copy), ("z", m))
                next_high(BASE["z"] + m)
                if m == 5:
                    for n in range(2):
                        act.wait_ge(sem("latent_mean"), n + 1)
                        act.activation(tmp[:, n, :], tmp[:, n, :], ACT.Sqrt)\
                           .then_inc(sem("latent_root"), 1)
            ready(act, ("z", 6))
            for m in range(5):
                act.wait_ge(sem("latent"), m + 1)
                act.activation(x_hi[:, m, :], zT[:, m, :], ACT.Copy).then_inc(sem("latent_high"), 1)
            for m in range(16):
                if m < 8:
                    ready(act, ("q_up", m))
                    free(act.activation(qn[:, m, :], PSb(("q_up", m)), ACT.Copy), ("q_up", m))
                for b in range(3 * m, 3 * m + 3):
                    if b % 8 == 7:
                        next_high(BASE["q_up"] + b // 8)
            for m in range(8):
                ready(act, ("k_up", m))
                free(act.activation(kn[:, m, :], PSb(("k_up", m)), ACT.Copy), ("k_up", m))
                if m % 4 == 3:
                    next_high(BASE["k_up"] + m // 4)
            next_high(BASE["v_up"])
            next_high(BASE["v_up"] + 1)
            for n in range(8):
                ready(act, ("v_up", n))
                free(act.activation(vtok[:, n // 2, (n % 2) * 512:(n % 2) * 512 + 512],
                                    PSb(("v_up", n)), ACT.Copy), ("v_up", n))

            def exponent(n):
                w = (n % 4 + 1) * P
                act.wait_ge(sem("bias"), n + 1)
                if n >= AHEAD:
                    ready(act, ("pT", n - AHEAD))
                k = n % AHEAD
                free(act.activation(prob[:, k, 0:w], PSb(("s", n))[:, 0:w], ACT.Exp, bias=row_bias[k],
                                    scale=ATT_SCALE, accum_out=row_sum[k]), ("s", n))

            def head_high(h):
                ready(act, ("o", h))
                act.activation(x_hi[:, h, :], PSb(("o", h)), ACT.Copy).then_inc(sem("o_high"), 1)

            for n in range(AHEAD):
                exponent(n)
            for n in range(4 * HEADS):
                h, qt = n // 4, n % 4
                ready(act, ("pT", n))
                if qt == 0 and h >= 2:
                    ready(act, ("o", h - 2))
                free(act.activation(pT[:, h % 2, 0:qt + 1, qt * P:(qt + 1) * P],
                                    PSb(("pT", n))[:, 0:(qt + 1) * P].rearrange("p (j q) -> p j q", q=P),
                                    ACT.Copy), ("pT", n))
                if n + AHEAD < 4 * HEADS:
                    exponent(n + AHEAD)
                if n >= 5 and (n - 5) % 4 == 0:
                    head_high((n - 5) // 4)
            head_high(HEADS - 1)
            for n in range(7):
                next_high(BASE["mla_out"] + n)

            def experts(layer):
                bu, bv, bq = BASE[f"u{layer}"], BASE[f"v{layer}"], BASE[f"pq{layer}"]
                if layer == 0:
                    act.sem_inc(gelu_done, 4)
                    act.sem_inc(gate_moved, 2)
                norm(2 * layer + 1, bq - 1)
                for n in range(16):
                    ready(act, (f"pq{layer}", n))
                    if n >= 2:
                        ready(act, (f"sc{layer}", n - 2))
                    free(act.activation(qT[:, n % 2, :], PSb((f"pq{layer}", n)), ACT.Copy),
                         (f"pq{layer}", n))
                    next_high(bq + n)

                def gelu(i, j):
                    c = i * UNROLL + j
                    act.wait_ge(tile_used, c + (bu + 1))
                    if layer > 0 or not isinstance(i, int) or i > 0:
                        act.wait_ge(act_stored[j], (i + TURNS * layer) * 16)
                    act.activation(act_st[:, j, :], PS[:, j % 4, :], ACT.Gelu).then_inc(gelu_done, 1)
                    high(c + (bu + RING), (bu + j) % RING,
                         i * (UNROLL // RING) + (bu + j + RING) // RING)

                def move_gates(turn, q):
                    b, k = q // (HALF_TOK // 4), q % (HALF_TOK // 4)
                    act.wait_ge(gates_made, turn * (TOK // 4) + (q + 1 + SEQ // 4 * layer + 2))
                    if k == 0 and (layer > 0 or not isinstance(turn, int)):
                        act.wait_ge(gate_stored[b], (turn + (TURNS - ROUTED_TURN) * layer) * 16)
                    act.activation(
                        gate_st[:, b].rearrange("p g t f -> p t g f")[:, 4 * k:4 * k + 4],
                        PS[:, 4 + q % 2, :].rearrange("p (t g f) -> p t g f", t=4, f=GF),
                        ACT.Copy, scale=1.0 / GATE_UNIT).then_inc(gate_moved, 1)

                for j in range(UNROLL):
                    gelu(0, j)
                with act.Fori(1, ROUTED_TURN - 1) as i:
                    for j in range(UNROLL):
                        gelu(i, j)
                act.wait_ge(sem("top_less_max"), TT * (layer + 1))
                act.activation(top, top, ACT.Exp).then_inc(sem("top_exp"), 1)
                for j in range(UNROLL):
                    gelu(ROUTED_TURN - 1, j)

                def routed_turn(i):
                    for j in range(UNROLL):
                        for q in quads_before(j):
                            move_gates(i - ROUTED_TURN, q)
                        gelu(i, j)

                routed_turn(ROUTED_TURN)
                with act.Fori(ROUTED_TURN + 1, TURNS) as i:
                    routed_turn(i)

                def product_high(c, j):
                    act.wait_ge(sem("product_made"), c + (NKEYS * layer + 1))
                    act.wait_ge(tile_used, c + (bv - RING + 1))
                    act.activation(x_hi[:, j % RING, :], product[:, j % RING, :],
                                   ACT.Copy).then_inc(sem("product_high"), 1)

                act.wait_ge(tile_used, bv)
                for c in range(RING):
                    product_high(c, c)

                def v_turn(i, n):
                    for j in range(n):
                        high(i * UNROLL + (bv + j + RING), (bv + j) % RING,
                             i * (UNROLL // RING) + (bv + j + RING) // RING)
                        product_high(i * UNROLL + (j + RING), j)

                with act.Fori(0, TURNS - 1) as i:
                    v_turn(i, UNROLL)
                v_turn(TURNS - 1, RING)
                for c in range(NKEYS - RING, NKEYS - 1):
                    next_high(bv + c)

            experts(0)

            norm(2, BASE["v0"] + NKEYS - 1)
            for n in range(8):
                ready(act, ("hg_q", n))
                free(act.activation(gq[:, n, :], PSb(("hg_q", n)), ACT.Silu), ("hg_q", n))
                next_high(BASE["hg_q"] + n)
            for n in range(8):
                ready(act, ("hg_f", n))
                ins = free(act.activation(gb[:, n, :], PSb(("hg_f", n)), ACT.Sigmoid), ("hg_f", n))
                next_high(BASE["hg_f"] + n)
            for n in range(8):
                ready(act, ("hg_g", n))
                free(act.activation(gg_[:, n, :], PSb(("hg_g", n)), ACT.Silu), ("hg_g", n))
                next_high(BASE["hg_g"] + n)
            act.wait_ge(sem("bound_less_max"), 1)
            act.activation(lbt[:, 0:2, :], lbt[:, 0:2, :], ACT.Exp).then_inc(sem("bound_exp"), 1)
            for h in range(HEADS):
                act.wait_ge(sem("forget"), h + 1)
                if h >= 2:
                    act.wait_ge(sem("cumulated"), h - 1)
                act.activation(diff[:, h % 2, :], gb[:, h, :], ACT.Ln).then_inc(sem("forget_log"), 1)
            for n in range(8):
                next_high(BASE["hg_i"] + n)
            for n in range(8):
                ready(act, ("hg_i", n))
                free(act.activation(vrec[:, n // 2, (n % 2) * 512:(n % 2) * 512 + 512],
                                    PSb(("hg_i", n)), ACT.Copy), ("hg_i", n))
            def head_out(h):
                ready(act, ("ho", h))
                free(act.activation(gq[:, h, :], PSb(("ho", h)), ACT.Copy), ("ho", h))

            for h in range(HEADS):
                act.wait_ge(sem("cumulated"), h + 1)
                if h >= 2:
                    was_freed(act, ("st", h - 2))
                    act.wait_ge(sem("q_decayed"), h - 1)
                act.activation(e_all[:, h % 2, :], gb[:, h, :], ACT.Exp).then_inc(sem("decay"), 1)
                for k in range(8):
                    n = 8 * h + k
                    act.wait_ge(sem("level_diff"), n + 1)
                    d = diff[:, n % 2, :]
                    if k == 0:
                        act.activation(d, d, ACT.Exp).then_inc(sem("level_exp"), 1)
                        continue
                    d4 = d.rearrange("p (b s m) -> p b s m", s=2, m=P >> k)
                    act.activation(d4[:, :, 0], d4[:, :, 0], ACT.Exp, scale=-1.0)
                    act.activation(d4[:, :, 1], d4[:, :, 1], ACT.Exp).then_inc(sem("level_exp"), 1)
                    if k == 2:
                        ready(act, ("kd", h))
                        free(act.activation(kdT.rearrange("p a b -> p (a b)"), PSb(("kd", h)), ACT.Copy),
                             ("kd", h))
                    if k == 3 and h >= 1:
                        head_out(h - 1)
            head_out(HEADS - 1)
            for h in range(HEADS):
                was_freed(act, ("hss", h))
                act.activation(gk[:, h, :], gk[:, h, :], ACT.Sqrt).then_inc(sem("head_root"), 1)
            for h in range(HEADS):
                act.wait_ge(sem("gated"), h + 1)
                act.activation(x_hi[:, h, :], gq[:, h, :], ACT.Copy).then_inc(sem("gated_high"), 1)
            for n in range(7):
                next_high(BASE["hg_out"] + n)

            experts(1)
            rstd_of_resid(4)

        @block.vector
        def _(dve):
            step = [0]

            def chain(ins):
                step[0] += 1
                ins.then_inc(sem("dve_step"), 1)
                dve.wait_ge(sem("dve_step"), step[0])

            def wide(ap, shape, at):
                return ap.unsqueeze(at).broadcast_to(shape)

            def mean_square(k, t):
                dve.wait_ge(sem("squares"), TT * k + t + 1)
                dve.tensor_scalar(stat[:, 4 + t:5 + t], stat[:, t:t + 1], 1.0 / DM, EPS, ALU.mult, ALU.add)\
                   .then_inc(sem("mean"), 1)

            def reciprocal_root(k, t):
                dve.wait_ge(sem("root"), TT * k + t + 1)
                chain(dve.reciprocal(stat[:, t:t + 1], stat[:, 8 + t:9 + t]))

            def scale_rows(k, t):
                reciprocal_root(k, t)
                dve.tensor_scalar(scaled[:, t, :], resid[:, t, :], stat[:, t:t + 1], None, ALU.mult)\
                   .then_inc(sem("scaled"), 1)

            def norm(k, name=None, scale=scale_rows):
                for t in range(TT + 2):
                    if name is not None and t < TT:
                        add_to_resid(name, t)
                    if 1 <= t <= TT:
                        mean_square(k, t - 1)
                    if t >= 2:
                        scale(k, t - 2)
                if scale is not scale_rows:
                    return
                for c in range(KC):
                    g = G_AT[["mix0", "ffn0", "mix1", "ffn1"][k]] + c
                    dve.wait_ge(sem("x_high"), KC * k + c + 1)
                    free(dve.scalar_tensor_tensor(x_lo[:, c, :], PSb(("xT", k, c)), gain[:, g:g + 1],
                                                  f32(x_hi[:, c, :]), ALU.mult, ALU.subtract),
                         ("xT", k, c))

            def add_to_resid(name, t):
                for n in (2 * t, 2 * t + 1):
                    part = resid[:, t, (n % 2) * 512:(n % 2) * 512 + 512]
                    ready(dve, (name, n))
                    free(dve.tensor_tensor(part, part, PSb((name, n)), ALU.add), (name, n))
                was_freed(dve, (name, 2 * t + 1))
                dve.sem_inc(sem("resid_done"), 1)

            norm(0)

            dve.wait_ge(sem("pos_in"), 16)
            dve.wait_ge(sem("const_in"), 16)
            angle, turns = tmp[:, 2, :], tmp[:, 3, :]
            dve.tensor_copy(turns, posi).then_inc(sem("pos_read"), 1)
            dve.wait_ge(sem("pos_read"), 1)
            chain(dve.tensor_scalar(angle, turns, const[:, C_INV:C_INV + 1], None, ALU.mult))
            for n in range(2):
                r = tmp[:, n, :]
                chain(dve.tensor_scalar(turns, angle, INV_2PI, 0.25 * n, ALU.mult, ALU.add))
                chain(dve.tensor_scalar(turns, turns, ROUNDER, None, ALU.add))
                chain(dve.tensor_scalar(turns, turns, ROUNDER, None, ALU.subtract))
                chain(dve.scalar_tensor_tensor(r, turns, -TWO_PI[0], angle, ALU.mult, ALU.add))
                chain(dve.scalar_tensor_tensor(r, turns, -TWO_PI[1], r, ALU.mult, ALU.add))
                chain(dve.scalar_tensor_tensor(r, turns, -TWO_PI[2], r, ALU.mult, ALU.add))
                if n == 1:
                    chain(dve.tensor_scalar(r, r, 0.5 * np.pi, None, ALU.add))
                dve.tensor_scalar(r, r, PI_BELOW, -PI_BELOW, ALU.min, ALU.max).then_inc(sem("angle"), 1)
            dve.wait_ge(sem("sines"), 2)
            chain(dve.tensor_scalar(sinT, sinT, const[:, C_SGN:C_SGN + 1], None, ALU.mult))

            def rotate(dst, raw, swapped, key):
                if raw is not None:
                    chain(dve.tensor_tensor(dst, raw, cosT, ALU.mult))
                    return
                free(dve.tensor_tensor(tmp[:, 2, :], swapped, sinT, ALU.mult), key)
                was_freed(dve, key)
                chain(dve.tensor_tensor(dst, dst, tmp[:, 2, :], ALU.add))

            for m in range(5):
                was_freed(dve, ("z", m))
                dve.tensor_tensor(qn[:, m, :], zT[:, m, :], zT[:, m, :], ALU.mult)\
                   .then_inc(sem("latent_sq"), 1)
            ready(dve, ("z", 5))
            free(dve.tensor_tensor(kr, PSb(("z", 5)), cosT, ALU.mult), ("z", 5))
            for n, width in enumerate((Q_LORA, KV_LORA)):
                ready(dve, ("zss", n))
                free(dve.tensor_scalar(tmp[:, n, :], PSb(("zss", n)), 1.0 / width, EPS, ALU.mult, ALU.add),
                     ("zss", n))
                was_freed(dve, ("zss", n))
                dve.sem_inc(sem("latent_mean"), 1)
            for n in range(2):
                dve.wait_ge(sem("latent_root"), n + 1)
                chain(dve.reciprocal(tmp[:, n, :], tmp[:, n, :]))
            for m in range(5):
                g = G_AT["q"] + m if m < QC else G_AT["kv"] + m - QC
                dve.scalar_tensor_tensor(zT[:, m, :], zT[:, m, :], gain[:, g:g + 1],
                                         tmp[:, 0 if m < QC else 1, :], ALU.mult, ALU.mult)\
                   .then_inc(sem("latent"), 1)
            ready(dve, ("z", 6))
            for m in range(5):
                dve.wait_ge(sem("latent_high"), m + 1)
                dve.tensor_tensor(x_lo[:, m, :], zT[:, m, :], f32(x_hi[:, m, :]), ALU.subtract)\
                   .then_inc(sem("latent_low"), 1)
            was_freed(dve, ("z", 5))
            rotate(kr, None, PSb(("z", 6)), ("z", 6))
            for j in range(4):
                ready(dve, ("q_up", 8 + j))
                free(dve.tensor_tensor(qr[:, j, :], PSb(("q_up", 8 + j)), cosT, ALU.mult), ("q_up", 8 + j))
            was_freed(dve, ("q_up", 11))
            for j in range(4):
                ready(dve, ("q_up", 12 + j))
                rotate(qr[:, j, :], None, PSb(("q_up", 12 + j)), ("q_up", 12 + j))
            dve.sem_inc(sem("rotated"), 1)

            def row_max(n):
                qt = n % 4
                s = PSb(("s", n))
                ready(dve, ("s", n))
                if n >= AHEAD:
                    was_freed(dve, ("s", n - AHEAD))
                chain(dve.tensor_tensor(s[:, qt * P:(qt + 1) * P], s[:, qt * P:(qt + 1) * P], causal, ALU.add))
                chain(dve.tensor_reduce(row_top[n % AHEAD], s[:, 0:(qt + 1) * P], AX.X, ALU.max))
                dve.tensor_scalar(row_bias[n % AHEAD], row_top[n % AHEAD], -ATT_SCALE, None, ALU.mult)\
                   .then_inc(sem("bias"), 1)

            for n in range(AHEAD):
                row_max(n)
            for n in range(4 * HEADS):
                w = (n % 4 + 1) * P
                was_freed(dve, ("s", n))
                k = n % AHEAD
                chain(dve.reciprocal(row_rec[k], row_sum[k]))
                dve.tensor_scalar(prob[:, k, 0:w], prob[:, k, 0:w], row_rec[k], None, ALU.mult)\
                   .then_inc(sem("prob"), 1)
                if n + AHEAD < 4 * HEADS:
                    row_max(n + AHEAD)
                if n >= 6 and (n - 6) % 4 == 0:
                    h = (n - 6) // 4
                    dve.wait_ge(sem("o_high"), h + 1)
                    free(dve.tensor_tensor(x_lo[:, h, :], PSb(("o", h)), f32(x_hi[:, h, :]), ALU.subtract),
                         ("o", h))
            h = HEADS - 1
            dve.wait_ge(sem("o_high"), h + 1)
            free(dve.tensor_tensor(x_lo[:, h, :], PSb(("o", h)), f32(x_hi[:, h, :]), ALU.subtract), ("o", h))
            def sixteen(values, places, source, groups):
                for half in range(2):
                    part = slice(8 * half, 8 * half + 8)
                    for g in range(groups):
                        ins = dve.max(values(g)[:, part], source(g))
                    chain(ins)
                    for g in range(groups):
                        ins = dve.max_index(places(g)[:, part], values(g)[:, part], source(g))
                    if half == 0:
                        for g in range(groups):
                            ins = dve.match_replace(source(g), values(g)[:, part], source(g), LOWEST)
                    chain(ins)

            def route(layer, t):
                sixteen(lambda g: val[:, g, :], lambda g: ixu[:, g, :], lambda g: scores[:, t, g, :], 16)
                chain(dve.tensor_copy(ixf, ixu))
                v4 = val.rearrange("p (h s) k -> p h s k", s=2)
                full = [P, HEADS, TOPK, TOPK]
                chain(dve.tensor_tensor(cand, wide(v4[:, :, 0], full, 3), wide(v4[:, :, 1], full, 2), ALU.add))
                sixteen(lambda g: top[:, t, g, :], lambda g: posu[:, g * TOPK:(g + 1) * TOPK],
                        lambda g: cand[:, g].rearrange("p a b -> p (a b)"), HEADS)
                chain(dve.tensor_scalar(halfu[:, 0, :], posu, 4, None, ALU.logical_shift_right))
                chain(dve.tensor_scalar(halfu[:, 1, :], posu, 15, None, ALU.bitwise_and))
                chain(dve.tensor_copy(halff, halfu))
                i4 = ixf.rearrange("p (h s) k -> p h s k", s=2)
                hot = cand.rearrange("p h a b -> p (h a) b")
                for s in range(2):
                    chain(dve.tensor_tensor(hot, wide(halff[:, s, :], [P, HK, TOPK], 2),
                                            wide(iota[:, 0:TOPK], [P, HK, TOPK], 1), ALU.is_equal))
                    chain(dve.tensor_tensor(picked.rearrange("p (h k) a -> p h k a", h=HEADS), cand,
                                            wide(i4[:, :, s], full, 2), ALU.mult))
                    chain(dve.tensor_reduce(ids[:, s, t, :], picked, AX.X, ALU.add))
                chain(dve.tensor_copy(gsum[:, 0:HEADS], top[:, t, :, 0]))
                dve.tensor_tensor(top[:, t], top[:, t], wide(gsum[:, 0:HEADS], [P, HEADS, TOPK], 2),
                                  ALU.subtract).then_inc(sem("top_less_max"), 1)

            def experts(layer):
                bv = BASE[f"v{layer}"]
                norm(2 * layer + 1, "mla_out" if layer == 0 else "hg_out")
                for n in range(16):
                    ready(dve, (f"sc{layer}", n))
                    free(dve.tensor_copy(scores[:, :, n, :], PSb((f"sc{layer}", n))
                                         .rearrange("p (t k) -> p t k", t=TT)), (f"sc{layer}", n))
                was_freed(dve, (f"sc{layer}", 15))
                for t in range(TT):
                    route(layer, t)
                dve.wait_ge(sem("top_less_max"), TT * (layer + 1))
                dve.sem_inc(sem("routed"), 1)
                dve.wait_ge(sem("top_exp"), layer + 1)
                flat = top.rearrange("p t h k -> p (t h) k")
                chain(dve.tensor_reduce(gsum, flat, AX.X, ALU.add))
                chain(dve.reciprocal(gsum, gsum))
                dve.tensor_tensor(flat, flat, wide(gsum, [P, TT * HEADS, TOPK], 2), ALU.mult)\
                   .then_inc(sem("gates"), 1)
                for n in range(2):
                    dve.wait_ge(sem("routeT_ps"), 3 * layer + n + 1)
                    chain(dve.tensor_copy(routeT[:, n, :], PS[:, 4 + n, :]))
                dve.wait_ge(sem("routeT_ps"), 3 * layer + 3)
                chain(dve.tensor_scalar(gate16, PS[:, 6, :], GATE_UNIT, None, ALU.mult))
                chain(dve.tensor_copy(routeT[:, 2, :], gate16))
                chain(dve.scalar_tensor_tensor(routeT[:, 3, :], PS[:, 6, :], GATE_UNIT, routeT[:, 2, :],
                                               ALU.mult, ALU.subtract))
                dve.sem_inc(sem("routeT"), 1)

                with dve.Fori(0, TURNS - ROUTED_TURN) as i:
                    dve.tensor_copy(window, routeT[:, :, bass.ds(i * TOK, TOK)]).then_inc(sem("window"), 1)
                    dve.wait_ge(sem("window"), i + ((TURNS - ROUTED_TURN) * layer + 1))
                    for k in range(TOK):
                        if k % 4 == 0:
                            dve.wait_ge(gates_made, i * (TOK // 4) + (k // 4 + 1 + SEQ // 4 * layer))
                        dve.tensor_scalar(onehot1[:, k % 8, :], iota16, window[:, 0, k:k + 1], None,
                                          ALU.is_equal)
                        for w in range(2):
                            ins = dve.tensor_scalar(onehot2[:, k % 8, w, :], iota16, window[:, 1, k:k + 1],
                                                    window[:, 2 + w, k:k + 1], ALU.is_equal, ALU.mult)
                        if k % 4 == 3:
                            ins.then_inc(onehots, 1)
                    dve.wait_ge(onehots, i * (TOK // 4) + (TOK // 4 + SEQ // 4 * layer))

                def make_product(i, j):
                    b = j // GF
                    dve.wait_ge(act_loaded[j], (i + (TURNS * layer + 1)) * 16)
                    if j % GF == 0:
                        dve.wait_ge(gate_loaded[b], (i + (TURNS * layer + 1)) * 16)
                    if not isinstance(i, int) or j >= RING:
                        dve.wait_ge(sem("product_low"), i * UNROLL + (j - RING + 1 + NKEYS * layer))
                    dve.tensor_tensor(product[:, j % RING, :], act_st[:, j, :], gate_ld[:, b, :, j % GF],
                                      ALU.mult).then_inc(sem("product_made"), 1)

                def product_low(c, j):
                    dve.wait_ge(sem("product_high"), c + (NKEYS * layer + 1))
                    dve.tensor_tensor(x_lo[:, j % RING, :], product[:, j % RING, :],
                                      f32(x_hi[:, j % RING, :]), ALU.subtract).then_inc(sem("product_low"), 1)

                make_product(0, 0)
                for j in range(1, UNROLL):
                    make_product(0, j)
                    product_low(j - 1, j - 1)
                with dve.Fori(1, TURNS) as i:
                    for j in range(UNROLL):
                        make_product(i, j)
                        product_low(i * UNROLL + (j - 1), (j - 1) % UNROLL)
                product_low(NKEYS - 1, UNROLL - 1)

            experts(0)

            norm(2, "v0")
            dve.tensor_tensor(lbt[:, 2, :], gain[:, G_AT["lb0"]:G_AT["lb0"] + KC],
                              gain[:, G_AT["lb1"]:G_AT["lb1"] + KC], ALU.max).then_inc(sem("bound"), 1)
            dve.wait_ge(sem("bound"), 1)
            both = gain[:, G_AT["lb0"]:G_AT["lb0"] + 2 * KC].rearrange("p (s k) -> p s k", s=2)
            dve.tensor_tensor(lbt[:, 0:2, :], both, wide(lbt[:, 2, :], [P, 2, KC], 1), ALU.subtract)\
               .then_inc(sem("bound_less_max"), 1)
            dve.wait_ge(sem("bound_exp"), 1)
            chain(dve.tensor_tensor(lbt[:, 2, :], lbt[:, 0, :], lbt[:, 1, :], ALU.add))
            chain(dve.reciprocal(lbt[:, 2, :], lbt[:, 2, :]))
            chain(dve.tensor_tensor(lbt[:, 0:2, :], lbt[:, 0:2, :], wide(lbt[:, 2, :], [P, 2, KC], 1), ALU.mult))
            chain(dve.tensor_tensor(lbt[:, 1, :], lbt[:, 0, :], lbt[:, 1, :], ALU.add))
            chain(dve.tensor_tensor(lbt[:, 1, :], lbt[:, 1, :], lbt[:, 0, :], ALU.subtract))
            chain(dve.tensor_scalar(lbt[:, 3, :], lbt[:, 1, :], -1.0, 1.0, ALU.mult, ALU.add))
            for h in range(HEADS):
                was_freed(dve, ("hg_f", h))
                chain(dve.tensor_scalar(gb[:, h, :], gb[:, h, :], lbt[:, 3, h:h + 1], lbt[:, 1, h:h + 1],
                                        ALU.mult, ALU.add))
                chain(dve.tensor_scalar(gk[:, h, :], gb[:, h, :], -1.0, 1.0, ALU.mult, ALU.add))
                dve.tensor_scalar(gb[:, h, :], gb[:, h, :], SMALLEST_F, None, ALU.max)\
                   .then_inc(sem("forget"), 1)
            dve.wait_ge(sem("mask_in"), 16)
            for h in range(HEADS):
                dve.wait_ge(sem("forget_log"), h + 1)
                dve.tensor_tensor_scan(gb[:, h, :], keep, diff[:, h % 2, :], 0.0, ALU.mult, ALU.add)\
                   .then_inc(sem("cumulated"), 1)
            dve.wait_ge(sem("cumulated"), HEADS)

            def scale_level(n):
                h, k = divmod(n, 8)
                d = diff[:, n % 2, :]
                dve.wait_ge(sem("level_exp"), n + 1)
                if k == 0:
                    dve.tensor_tensor(kdec, gk[:, h, :], d, ALU.mult).then_inc(sem("k_decayed"), 1)
                    return
                x = h * LEVELS + k - 1
                if x >= 2:
                    ready(dve, ("a", (x - 2) // LEVELS, (x - 2) % LEVELS + 1))

                def halves(ap):
                    return ap.rearrange("p (b s m) -> p b s m", s=2, m=P >> k)

                for half, src in enumerate((gk, gq)):
                    ins = dve.tensor_tensor(halves(xx[:, x % 2, :])[:, :, half],
                                            halves(src[:, h, :])[:, :, half], halves(d)[:, :, half], ALU.mult)
                ins.then_inc(sem("level_x"), 1)

            def mask_level(n):
                h, p = divmod(n, 8)
                ready(dve, ("a", h, p))
                if n >= 2:
                    dve.wait_ge(sem("a_used"), n - 1)
                free(dve.tensor_tensor(chunked(a_sb[:, n % 2, :]), chunked(PSb(("a", h, p))),
                                       level_mask[(p - 1) % 8].unsqueeze(1).broadcast_to([P, TT, P]),
                                       ALU.mult), ("a", h, p))

            def states(h):
                ready(dve, ("st", h))
                st = PSb(("st", h))
                if h >= 1:
                    ready(dve, ("ho", h - 1))
                chain(dve.tensor_copy(state[:, 0, :], st[:, 0:P]))
                for c in (1, 2):
                    ins = dve.scalar_tensor_tensor(state[:, c, :], state[:, c - 1, :],
                                                   e_all[:, h % 2, c * P + P - 1:c * P + P],
                                                   st[:, c * P:(c + 1) * P], ALU.mult, ALU.add)
                    chain(ins) if c == 1 else free(ins, ("st", h))

            def head_square(h):
                was_freed(dve, ("ho", h))
                dve.tensor_tensor(gk[:, h, :], gq[:, h, :], gq[:, h, :], ALU.mult).then_inc(sem("head_sq"), 1)
                dve.wait_ge(sem("head_sq"), h + 1)
                was_freed(dve, ("hg_g", h))
                g = G_AT["out"] + h
                chain(dve.scalar_tensor_tensor(gq[:, h, :], gq[:, h, :], gain[:, g:g + 1], gg_[:, h, :],
                                               ALU.mult, ALU.mult))

            def head_mean(h):
                ready(dve, ("hss", h))
                free(dve.tensor_scalar(gk[:, h, :], PSb(("hss", h)), 1.0 / P, EPS, ALU.mult, ALU.add),
                     ("hss", h))

            def gated_low(h):
                dve.wait_ge(sem("gated_high"), h + 1)
                dve.tensor_tensor(x_lo[:, h, :], gq[:, h, :], f32(x_hi[:, h, :]), ALU.subtract)\
                   .then_inc(sem("gated_low"), 1)

            for n in range(8 * HEADS):
                h, k = divmod(n, 8)
                scale_level(n)
                if n >= 2:
                    mask_level(n - 2)
                if k == 1 and h >= 2:
                    head_mean(h - 2)
                if k == 4 and h >= 1:
                    head_square(h - 1)
                if k == 5:
                    dve.wait_ge(sem("decay"), h + 1)
                    states(h)
                if k == 7:
                    dve.wait_ge(sem("level_x"), (h + 1) * LEVELS)
                    dve.tensor_tensor(gq[:, h, :], gq[:, h, :], e_all[:, h % 2, :], ALU.mult)\
                       .then_inc(sem("q_decayed"), 1)
            mask_level(8 * HEADS - 2)
            mask_level(8 * HEADS - 1)
            head_mean(HEADS - 2)
            head_square(HEADS - 1)
            head_mean(HEADS - 1)
            for h in range(HEADS):
                dve.wait_ge(sem("head_root"), h + 1)
                chain(dve.reciprocal(gk[:, h, :], gk[:, h, :]))
                dve.tensor_tensor(gq[:, h, :], gq[:, h, :], gk[:, h, :], ALU.mult).then_inc(sem("gated"), 1)
                if h >= 1:
                    gated_low(h - 1)
            gated_low(HEADS - 1)
            experts(1)

            dve.wait_ge(sem("product_made"), 2 * NKEYS)
            dve.sem_inc(sem("final_free"), 1)

            def scale_final(k, t):
                if t == 0:
                    dve.wait_ge(sem("fgain_in"), 16)
                reciprocal_root(k, t)
                dve.scalar_tensor_tensor(final[:, t, :], resid[:, t, :], stat[:, t:t + 1], final_gain,
                                         ALU.mult, ALU.mult).then_inc(sem("final_made"), 1)

            norm(4, "v1", scale_final)

        @block.tensor
        def _(pe):
            def begin(key):
                if jobs.before[key] is not None:
                    was_freed(pe, jobs.before[key])

            def end(mm, key):
                mm.then_inc(sem(jobs.ready[key][0]), 1)

            def three(ps, wh, wl, xh, xl, start, stop):
                pe.matmul(ps, wh, xh, start=start, stop=False)
                pe.matmul(ps, wh, xl, start=False, stop=False)
                return pe.matmul(ps, wl, xh, start=False, stop=stop)

            def across(ps, slot, normed=None):
                for kc in range(KC):
                    if normed is not None:
                        was_freed(pe, ("xT", normed, kc))
                    w = slice(kc * P, (kc + 1) * P)
                    mm = three(ps, w_hi[:, slot, w], w_lo[:, slot, w], x_hi[:, kc, :], x_lo[:, kc, :],
                               kc == 0, kc == KC - 1)
                return mm

            def projection(name, m, normed=None):
                n = BASE[name] + m
                pe.wait_ge(lo_ready, n + 1)
                begin((name, m))
                end(across(PSb((name, m)), n % RING, normed if m == 0 else None), (name, m))

            def token_major(name, kcs, x_at, x_wait):
                for kc in range(kcs):
                    tile = BASE[name] + kc
                    pe.wait_ge(lo_ready, tile + 1)
                    x_wait(kc)
                    rows(lambda n: PSb((name, n)), tile % RING, x_at + kc, kc == 0, kc == kcs - 1,
                         (lambda mm, n: end(mm, (name, n))) if kc == kcs - 1 else None,
                         (lambda n: begin((name, n))) if kc == 0 else None)

            def rows(bank, slot, xc, start, stop, signal, first=None):
                for n in range(8):
                    if first:
                        first(n)
                    t, w = slice(n // 2 * P, n // 2 * P + P), slice(n % 2 * 512, n % 2 * 512 + 512)
                    mm = three(bank(n), x_hi[:, xc, t], x_lo[:, xc, t], w_hi[:, slot, w],
                               w_lo[:, slot, w], start, stop)
                    if signal:
                        signal(mm, n)
                if not signal:
                    mm.then_inc(tile_used, 1)

            def norm(k):
                for t in range(TT):
                    pe.wait_ge(sem("scaled"), TT * k + t + 1)
                    for c in range(KC):
                        if t == 0:
                            begin(("xT", k, c))
                        mm = pe.transpose(PSb(("xT", k, c))[:, t * P:(t + 1) * P],
                                          scaled[:, t, c * P:(c + 1) * P], ident)
                        if t == TT - 1:
                            end(mm, ("xT", k, c))

            pe.wait_ge(sem("const_in"), 16)
            norm(0)
            for k in range(6):
                projection("z", k, 0)
            for n, ms in enumerate((range(0, QC), range(QC, QC + VC))):
                begin(("zss", n))
                for m in ms:
                    pe.wait_ge(sem("latent_sq"), m + 1)
                    mm = pe.matmul(PSb(("zss", n)), ones, qn[:, m, :], start=m == ms[0], stop=m == ms[-1])
                end(mm, ("zss", n))
            projection("z", 6)

            def blocks_of(name, count, kcs, x_at):
                for m in range(count):
                    begin((name, m))
                    for kc in range(kcs):
                        b = kcs * m + kc
                        n = BASE[name] + b // 8
                        w = slice(b % 8 * P, b % 8 * P + P)
                        if name == "q_up" and m == 0:
                            pe.wait_ge(sem("latent_low"), kc + 1)
                        if b % 8 == 0:
                            pe.wait_ge(lo_ready, n + 1)
                        mm = three(PSb((name, m)), w_hi[:, n % RING, w], w_lo[:, n % RING, w],
                                   x_hi[:, x_at + kc, :], x_lo[:, x_at + kc, :], kc == 0, kc == kcs - 1)
                        if b % 8 == 7 and kc < kcs - 1:
                            mm.then_inc(tile_used, 1)
                    end(mm, (name, m))

            blocks_of("q_up", 16, QC, 0)
            pe.wait_ge(sem("latent_low"), QC + VC)
            blocks_of("k_up", 8, VC, QC)
            token_major("v_up", VC, QC, lambda kc: None)

            pe.wait_ge(sem("rotated"), 1)
            was_freed(pe, ("k_up", 7))
            for n in range(4 * HEADS + AHEAD + 1):
                if n < 4 * HEADS:
                    h, qt = n // 4, n % 4
                    w, q, part = (qt + 1) * P, slice(qt * P, qt * P + P), slice(h % 2 * 64, h % 2 * 64 + 64)
                    begin(("s", n))
                    s = PSb(("s", n))[:, 0:w]
                    pe.matmul(s, qn[:, h, q], kn[:, h, 0:w], start=True, stop=False)
                    end(pe.matmul(s, qr[part, h // 2, q], kr[part, 0:w], start=False, stop=True), ("s", n))
                if AHEAD <= n < 4 * HEADS + AHEAD:
                    k = n - AHEAD
                    h, qt = k // 4, k % 4
                    pe.wait_ge(sem("prob"), k + 1)
                    begin(("pT", k))
                    for j in range(qt + 1):
                        mm = pe.transpose(PSb(("pT", k))[:, j * P:(j + 1) * P],
                                          prob[:, k % AHEAD, j * P:(j + 1) * P], ident)
                    end(mm, ("pT", k))
                if n > AHEAD and (n - AHEAD) % 4 == 0:
                    h = (n - AHEAD) // 4 - 1
                    begin(("o", h))
                    if h == 0:
                        was_freed(pe, ("v_up", 7))
                    was_freed(pe, ("pT", 4 * h + 3))
                    for j in range(TT):
                        mm = pe.matmul(PSb(("o", h))[:, j * P:SEQ], vtok[:, j, h * P:(h + 1) * P],
                                       pT[:, h % 2, j, j * P:SEQ], start=j == 0, stop=j == TT - 1)
                    end(mm, ("o", h))
            token_major("mla_out", 8, 0, lambda kc: was_freed(pe, ("o", kc)))

            def experts(layer):
                bu, bv, bq = BASE[f"u{layer}"], BASE[f"v{layer}"], BASE[f"pq{layer}"]
                if layer == 0:
                    pe.sem_inc(gates_made, 2)
                norm(2 * layer + 1)
                pe.wait_ge(sem("keys_in"), 16 * (layer + 1))
                for n in range(17):
                    if n < 16:
                        key = (f"pq{layer}", n)
                        pe.wait_ge(lo_ready, bq + n + 1)
                        begin(key)
                        end(across(PSb(key), (bq + n) % RING, 2 * layer + 1 if n == 0 else None), key)
                    if n >= 1:
                        key = (f"sc{layer}", n - 1)
                        begin(key)
                        was_freed(pe, (f"pq{layer}", n - 1))
                        for t in range(TT):
                            mm = pe.matmul(PSb(key)[:, t * P:(t + 1) * P], qT[:, (n - 1) % 2, t * P:(t + 1) * P],
                                           keysT[:, n - 1, :], start=True, stop=True)
                        end(mm, key)
                was_freed(pe, (f"sc{layer}", 15))

                def u_tile(i, j):
                    c = i * UNROLL + j
                    pe.wait_ge(lo_ready, c + (bu + 1))
                    pe.wait_ge(gelu_done, c + (NKEYS * layer + 1))
                    across(PS[:, j % 4, :], (bu + j) % RING).then_inc(tile_used, 1)

                with pe.Fori(0, ROUTED_TURN - 1) as i:
                    for j in range(UNROLL):
                        u_tile(i, j)
                for j in range(UNROLL // 2):
                    u_tile(ROUTED_TURN - 1, j)
                for n in range(3):
                    pe.wait_ge(*((sem("routed"), layer + 1) if n < 2 else (sem("gates"), layer + 1)))
                    for t in range(TT):
                        src = ids[:, n, t, :] if n < 2 else top[:, t].rearrange("p h k -> p (h k)")
                        mm = pe.transpose(PS[:, 4 + n, t * P:(t + 1) * P], src, ident)
                    mm.then_inc(sem("routeT_ps"), 1)
                for j in range(UNROLL // 2, UNROLL):
                    u_tile(ROUTED_TURN - 1, j)
                pe.wait_ge(sem("routeT"), layer + 1)

                def spread(turn, q):
                    pe.wait_ge(onehots, turn * (TOK // 4) + (q + 1 + SEQ // 4 * layer))
                    pe.wait_ge(gate_moved, turn * (TOK // 4) + (q + 1 + SEQ // 4 * layer))
                    for k in range(4):
                        s = (4 * q + k) % 8
                        for w in range(2):
                            mm = pe.matmul(PS[:, 4 + q % 2, k * P:(k + 1) * P], onehot1[:, s, :],
                                           onehot2[:, s, w, :], start=w == 0, stop=w == 1)
                    mm.then_inc(gates_made, 1)

                with pe.Fori(ROUTED_TURN, TURNS) as i:
                    for j in range(UNROLL):
                        for q in quads_before(j):
                            spread(i - ROUTED_TURN, q)
                        u_tile(i, j)
                pe.wait_ge(gelu_done, NKEYS * (layer + 1) + 4)
                pe.wait_ge(gate_moved, SEQ // 4 * (layer + 1) + 2)

                def v_tile(i, j, start=False, signal=None):
                    c = i * UNROLL + j
                    pe.wait_ge(lo_ready, c + (bv + 1))
                    pe.wait_ge(sem("product_low"), c + (NKEYS * layer + 1))
                    rows(lambda n: PSb((f"v{layer}", n)), (bv + j) % RING, j % RING, start,
                         signal is not None, signal)

                for j in range(UNROLL):
                    v_tile(0, j, start=j == 0)
                with pe.Fori(1, TURNS - 1) as i:
                    for j in range(UNROLL):
                        v_tile(i, j)
                for j in range(UNROLL):
                    v_tile(TURNS - 1, j, signal=(lambda mm, n: end(mm, (f"v{layer}", n)))
                           if j == UNROLL - 1 else None)

            experts(0)

            norm(2)
            for name in ("hg_q", "hg_f", "hg_g"):
                for m in range(8):
                    projection(name, m, 2 if name == "hg_q" else None)
            token_major("hg_i", 8, 0, lambda kc: None)
            was_freed(pe, ("hg_i", 7))

            for what, h, p in recurrence():
                if what == "kd":
                    begin(("kd", h))
                    pe.wait_ge(sem("k_decayed"), h + 1)
                    for c in range(TT):
                        mm = pe.transpose(PSb(("kd", h))[:, c * P:(c + 1) * P], kdec[:, c * P:(c + 1) * P],
                                          ident)
                    end(mm, ("kd", h))
                elif what == "a":
                    begin(("a", h, p))
                    x = h * LEVELS + p - 1
                    if p:
                        pe.wait_ge(sem("level_x"), x + 1)
                    for c in range(TT):
                        t = slice(c * P, (c + 1) * P)
                        lhs, rhs = (xx[:, x % 2, t],) * 2 if p else (gk[:, h, t], gq[:, h, t])
                        mm = pe.matmul(PSb(("a", h, p))[:, t], lhs, rhs, start=True, stop=True)
                    end(mm, ("a", h, p))
                elif what == "st":
                    begin(("st", h))
                    was_freed(pe, ("kd", h))
                    for c in range(TT - 1):
                        mm = pe.matmul(PSb(("st", h))[:, c * P:(c + 1) * P], kdT[:, c, :],
                                       vrec[:, c, h * P:(h + 1) * P], start=True, stop=True)
                    end(mm, ("st", h))
                elif what == "hss":
                    begin(("hss", h))
                    pe.wait_ge(sem("head_sq"), h + 1)
                    end(pe.matmul(PSb(("hss", h)), ones, gk[:, h, :], start=True, stop=True), ("hss", h))
                elif what == "values":
                    if p == 0:
                        begin(("ho", h))
                    was_freed(pe, ("a", h, p))
                    for c in range(TT):
                        t = slice(c * P, (c + 1) * P)
                        mm = pe.matmul(PSb(("ho", h))[:, t], vrec[:, c, h * P:(h + 1) * P],
                                       a_sb[:, (8 * h + p) % 2, t], start=p == 0 and c == 0, stop=False,
                                       skip_group_check=True)
                    mm.then_inc(sem("a_used"), 1)
                else:
                    was_freed(pe, ("st", h))
                    pe.wait_ge(sem("q_decayed"), h + 1)
                    for c in range(1, TT):
                        t = slice(c * P, (c + 1) * P)
                        mm = pe.matmul(PSb(("ho", h))[:, t], state[:, c - 1, :], gq[:, h, t], start=False,
                                       stop=c == TT - 1, skip_group_check=True)
                    end(mm, ("ho", h))
            token_major("hg_out", 8, 0, lambda kc: pe.wait_ge(sem("gated_low"), kc + 1))

            experts(1)


def _constants():
    c = np.zeros((P, C_COLS), np.float32)
    c[:, C_ID:C_ID + P] = np.eye(P)
    c[:, C_ONE:C_ONE + P] = 1.0
    c[:, C_IOTA:C_IOTA + P] = np.arange(P)
    c[:, C_CAUSAL:C_CAUSAL + P] = np.where(np.arange(P)[None, :] <= np.arange(P)[:, None], 0.0, -1e30)
    row = np.arange(P) % ROPE
    inv = np.float32(THETA) ** (-np.arange(0, ROPE, 2, dtype=np.float32) / np.float32(ROPE))
    c[:, C_INV] = inv[row % (ROPE // 2)]
    c[:, C_SGN] = np.where(row < ROPE // 2, -1.0, 1.0)
    m = np.zeros((P, M_COLS), np.float32)
    m[:, 0:SEQ] = (np.arange(SEQ) % P != 0)
    s, t = np.arange(P)[:, None], np.arange(P)[None, :]
    for lv in range(LEVELS):
        half = P >> (lv + 1)
        m[:, SEQ + P * lv:SEQ + P * (lv + 1)] = ((s // (2 * half) == t // (2 * half))
                                                 & (s // half % 2 == 0) & (t // half % 2 == 1))
    m[:, SEQ + P * LEVELS:M_IOTA] = (s == t)
    m[:, M_IOTA:] = np.arange(P)
    return c, (m.view(np.uint32) >> 16).astype(np.uint16)


def _across_tiles(w):
    n = w.shape[1]
    return w.reshape(KC, P, n // P, P).transpose(2, 1, 0, 3).reshape(n // P, P, KC * P)


def _block_tiles(w):
    k, n = w.shape
    b = w.reshape(k // P, P, n // P, P).transpose(2, 0, 1, 3).reshape(-1, 8, P, P)
    return b.transpose(0, 2, 1, 3).reshape(-1, P, 8 * P)


def _columns(g):
    return g.reshape(-1, P).T


def kernel(**inputs):
    import concourse.bacc as _bacc
    from concourse import mybir as _mybir
    from concourse.bass_utils import run_bass_kernel_spmd as _run

    a = {k: np.asarray(v) for k, v in inputs.items()}
    cat = np.concatenate
    w_in = a["mla_w_in"][0]
    r = w_in[:, Q_LORA + KV_LORA:]
    swap = cat([r[:, ROPE // 2:], r[:, :ROPE // 2]], 1)
    z = cat([w_in[:, :Q_LORA + KV_LORA], r, r, swap, swap], 1)
    q_up = a["mla_w_q_up"][0].reshape(Q_LORA, HEADS, NOPE + ROPE)
    qr = q_up[:, :, NOPE:]
    qs = cat([qr[:, :, ROPE // 2:], qr[:, :, :ROPE // 2]], 2)
    q_all = cat([q_up[:, :, :NOPE].reshape(Q_LORA, -1), qr.reshape(Q_LORA, -1), qs.reshape(Q_LORA, -1)], 1)
    kv_up = a["mla_w_kv_up"][0].reshape(KV_LORA, HEADS, 2 * P)
    mla_t = cat([_across_tiles(z), _block_tiles(q_all), _block_tiles(kv_up[:, :, :P].reshape(KV_LORA, -1)),
                 kv_up[:, :, P:].reshape(VC, P, DM), a["mla_w_out"][0].reshape(8, P, DM)], 0)
    hg = a["hg_w_in"][0]
    hg_t = cat([_across_tiles(hg[:, :2 * DM]), _across_tiles(hg[:, 3 * DM:]),
                hg[:, 2 * DM:3 * DM].reshape(8, P, DM), a["hg_w_out"][0].reshape(8, P, DM)], 0)
    pq_t = np.stack([_across_tiles(w) for w in a["peer_w_q"]])
    keys = a["peer_sub_keys"].reshape(2, 16, NKEYS, P).transpose(0, 3, 1, 2)
    u_t = a["peer_u"].reshape(2, NKEYS, NKEYS, KC, P).transpose(0, 2, 4, 3, 1).reshape(2, NKEYS, P, DM)
    v_t = a["peer_v"].reshape(2, NKEYS, NKEYS, DM).transpose(0, 2, 1, 3)
    gains = cat([_columns(g) for g in (a["ln_mix"][0], a["ln_ffn"][0], a["ln_mix"][1], a["ln_ffn"][1],
                                       a["mla_q_norm"][0], a["mla_kv_norm"][0], a["hg_out_norm"][0],
                                       a["hg_lb"][0], a["hg_lb"][1])], 1)
    consts, masks = _constants()
    arrays = {
        "x": a["x"][0], "pos": a["positions"], "consts": consts, "masks": masks, "gains": gains,
        "fgain": a["ln_final"][None], "mla_t": mla_t, "hg_t": hg_t, "pq_t": pq_t, "keys_t": keys,
        "u_t": u_t, "v_t": v_t,
    }
    arrays = {f"in_{k}": np.ascontiguousarray(v) for k, v in arrays.items()}
    nc = _bacc.Bacc("TRN2", target_bir_lowering=False, num_devices=1)
    args = [nc.dram_tensor(k, v.shape, _mybir.dt.from_np(v.dtype), kind="ExternalInput").ap()
            for k, v in arrays.items()]
    args.append(nc.dram_tensor("out_0", (SEQ, DM), _mybir.dt.float32, kind="ExternalOutput").ap())
    model(nc, *args)
    got = _run(nc, [arrays], core_ids=[0]).results[0]["out_0"]
    return got.reshape(1, SEQ, DM)
```
